# Optimizing a Trainium2 kernel written in Bass

```python
import math
import jax, jax.numpy as jnp
from jax import lax
import numpy as np

D_MODEL = 1024
BATCH = 1
SEQ = 256
DEPTH = 2

N_MIXERS = 4
HEAD_DIM = 64
N_HEADS = D_MODEL // HEAD_DIM
ROT_DIM = HEAD_DIM // 4
ROPE_THETA = 500000.0
Q_BLOCK = 128
DIL_CONFIGS = ((128, 1), (512, 4), (2048, 16))
N_HEADS_DIL = 8
DIL_GROUP_WIDTH = N_HEADS_DIL * HEAD_DIM
DIL_IN_WIDTH = len(DIL_CONFIGS) * 3 * DIL_GROUP_WIDTH
IDX_HEADS = 8
IDX_DIM = 64
TOPK_TOKENS = 256
DSA_IN_WIDTH = 3 * D_MODEL + IDX_HEADS * IDX_DIM + IDX_DIM + IDX_HEADS
MOBA_BLOCK = 256
MOBA_TOPK = 3
MOBA_Q_CHUNK = 32
D_FF = 4 * D_MODEL
PLE_DIM = 256
EPS = 1e-6


def _n_layers_of(mixer):
    return len(range(mixer, DEPTH, N_MIXERS))

def rms_norm(x, g):
    x32 = x.astype(jnp.float32)
    y = x32 * lax.rsqrt(jnp.mean(x32 * x32, axis=-1, keepdims=True) + EPS)
    return (y * g.astype(jnp.float32)).astype(x.dtype)

def rope_tables(positions):
    inv_freq = ROPE_THETA ** (-jnp.arange(0, ROT_DIM, 2, dtype=jnp.float32) / ROT_DIM)
    ang = positions.astype(jnp.float32)[..., None] * inv_freq
    return jnp.cos(ang)[:, :, None, :], jnp.sin(ang)[:, :, None, :]

def apply_partial_rope(t, cos, sin):
    half = ROT_DIM // 2
    t1 = t[..., :half].astype(jnp.float32)
    t2 = t[..., half:ROT_DIM].astype(jnp.float32)
    rot = jnp.concatenate([t1 * cos - t2 * sin, t2 * cos + t1 * sin], axis=-1).astype(t.dtype)
    return jnp.concatenate([rot, t[..., ROT_DIM:]], axis=-1)

def stick_breaking_attention(x, w_in, w_out):
    B, S, _ = x.shape
    q, k, v = jnp.split(x @ w_in, 3, axis=-1)
    q = q.reshape(B, S, N_HEADS, HEAD_DIM)
    k = k.reshape(B, S, N_HEADS, HEAD_DIM)
    v = v.reshape(B, S, N_HEADS, HEAD_DIM)
    scale = HEAD_DIM ** -0.5
    outs = []
    for blk in range(S // Q_BLOCK):
        t0 = blk * Q_BLOCK
        L = t0 + Q_BLOCK
        z = jnp.einsum('bqhd,bkhd->bhqk', q[:, t0:L], k[:, :L]).astype(jnp.float32) * scale
        t_idx = t0 + jnp.arange(Q_BLOCK)[:, None]
        s_idx = jnp.arange(L)[None, :]
        past = s_idx < t_idx
        log_fail = jnp.where(past, jax.nn.log_sigmoid(-z), 0.0)
        later = lax.cumsum(log_fail, axis=3, reverse=True) - log_fail
        a = jnp.where(past, jnp.exp(jax.nn.log_sigmoid(z) + later), 0.0)
        outs.append(jnp.einsum('bhqk,bkhd->bqhd', a.astype(v.dtype), v[:, :L]))
    o = jnp.concatenate(outs, axis=1).reshape(B, S, N_HEADS * HEAD_DIM)
    return o @ w_out

def banded_attention(q, k, v, n_back):
    N, L, H, Dh = q.shape
    nb = L // Q_BLOCK
    qb = q.reshape(N, nb, Q_BLOCK, H, Dh)
    kb = k.reshape(N, nb, Q_BLOCK, H, Dh)
    vb = v.reshape(N, nb, Q_BLOCK, H, Dh)
    zero = jnp.zeros_like(kb[:, :1])
    k2 = jnp.concatenate([jnp.concatenate([zero, kb[:, :-1]], axis=1), kb], axis=2)
    v2 = jnp.concatenate([jnp.concatenate([zero, vb[:, :-1]], axis=1), vb], axis=2)
    s = jnp.einsum('nbqhd,nbkhd->nbhqk', qb, k2).astype(jnp.float32) * (Dh ** -0.5)
    dist = Q_BLOCK + jnp.arange(Q_BLOCK)[:, None] - jnp.arange(2 * Q_BLOCK)[None, :]
    band = (dist >= 0) & (dist <= n_back)
    first_pad = (jnp.arange(nb) == 0)[:, None, None] & (jnp.arange(2 * Q_BLOCK) < Q_BLOCK)[None, None, :]
    mask = band[None] & ~first_pad
    s = jnp.where(mask[None, :, None], s, -jnp.inf)
    lse = jax.nn.logsumexp(s, axis=-1)
    prob = jnp.exp(s - lse[..., None])
    o = jnp.einsum('nbhqk,nbkhd->nbqhd', prob.astype(v.dtype), v2)
    return o.reshape(N, L, H, Dh), lse.transpose(0, 1, 3, 2).reshape(N, L, H)

def dilated_attention(x, w_in, w_out, cos, sin):
    B, S, _ = x.shape
    H = N_HEADS_DIL
    G = len(DIL_CONFIGS)
    proj = (x @ w_in).reshape(B, S, G, 3, H, HEAD_DIM)
    outs, lses = [], []
    for g, (window, dil) in enumerate(DIL_CONFIGS):
        q = apply_partial_rope(proj[:, :, g, 0], cos, sin)
        k = apply_partial_rope(proj[:, :, g, 1], cos, sin)
        v = proj[:, :, g, 2]
        L = S // dil
        Lp = -(-L // Q_BLOCK) * Q_BLOCK

        def strided(t):
            t = t.reshape(B, L, dil, H, HEAD_DIM).transpose(0, 2, 1, 3, 4).reshape(B * dil, L, H, HEAD_DIM)
            return jnp.pad(t, ((0, 0), (0, Lp - L), (0, 0), (0, 0)))

        o, lse = banded_attention(strided(q), strided(k), strided(v), window // dil)
        o = o[:, :L].reshape(B, dil, L, H, HEAD_DIM).transpose(0, 2, 1, 3, 4).reshape(B, S, H, HEAD_DIM)
        lse = lse[:, :L].reshape(B, dil, L, H).transpose(0, 2, 1, 3).reshape(B, S, H)
        outs.append(o)
        lses.append(lse)
    alpha = jax.nn.softmax(jnp.stack(lses, axis=0), axis=0)
    o = jnp.einsum('gbsh,gbshd->bshd', alpha, jnp.stack(outs, axis=0).astype(jnp.float32)).astype(x.dtype)
    return o.reshape(B, S, H * HEAD_DIM) @ w_out

def dsa_attention(x, w_in, w_out, cos, sin):
    B, S, _ = x.shape
    D = N_HEADS * HEAD_DIM
    cuts = [D, 2 * D, 3 * D, 3 * D + IDX_HEADS * IDX_DIM, 3 * D + IDX_HEADS * IDX_DIM + IDX_DIM]
    q, k, v, qi, ki, wi = jnp.split(x @ w_in, cuts, axis=-1)
    q = apply_partial_rope(q.reshape(B, S, N_HEADS, HEAD_DIM), cos, sin)
    k = apply_partial_rope(k.reshape(B, S, N_HEADS, HEAD_DIM), cos, sin)
    v = v.reshape(B, S, N_HEADS, HEAD_DIM)
    qi = apply_partial_rope(qi.reshape(B, S, IDX_HEADS, IDX_DIM), cos, sin)
    ki = apply_partial_rope(ki.reshape(B, S, 1, IDX_DIM), cos, sin)[:, :, 0]
    wi = wi.astype(jnp.float32) * (IDX_HEADS ** -0.5)
    topk = min(TOPK_TOKENS, S // 4)
    scale = HEAD_DIM ** -0.5
    key_pos = jnp.arange(S)

    def block(bi):
        t0 = bi * Q_BLOCK
        t_pos = t0 + jnp.arange(Q_BLOCK)
        qb = lax.dynamic_slice_in_dim(q, t0, Q_BLOCK, axis=1)
        qib = lax.dynamic_slice_in_dim(qi, t0, Q_BLOCK, axis=1)
        wib = lax.dynamic_slice_in_dim(wi, t0, Q_BLOCK, axis=1)
        rel = jax.nn.relu(jnp.einsum('bqhd,bkd->bqhk', qib, ki).astype(jnp.float32))
        score = jnp.einsum('bqh,bqhk->bqk', wib, rel)
        causal = key_pos[None, :] <= t_pos[:, None]
        score = jnp.where(causal[None], score, -jnp.inf)
        _, idx = lax.top_k(score, topk)
        valid = idx <= t_pos[None, :, None]
        k_sel = jax.vmap(lambda kk, ii: kk[ii])(k, idx)
        v_sel = jax.vmap(lambda vv, ii: vv[ii])(v, idx)
        s = jnp.einsum('bqhd,bqkhd->bqhk', qb, k_sel).astype(jnp.float32) * scale
        s = jnp.where(valid[:, :, None, :], s, -jnp.inf)
        prob = jax.nn.softmax(s, axis=-1)
        return jnp.einsum('bqhk,bqkhd->bqhd', prob.astype(v.dtype), v_sel)

    o = lax.map(block, jnp.arange(S // Q_BLOCK))
    o = o.transpose(1, 0, 2, 3, 4).reshape(B, S, D)
    return o @ w_out

def moba_attention(x, w_in, w_out, cos, sin):
    B, S, _ = x.shape
    H = N_HEADS
    q, k, v = jnp.split(x @ w_in, 3, axis=-1)
    q = apply_partial_rope(q.reshape(B, S, H, HEAD_DIM), cos, sin)
    k = apply_partial_rope(k.reshape(B, S, H, HEAD_DIM), cos, sin)
    v = v.reshape(B, S, H, HEAD_DIM)
    nb = -(-S // MOBA_BLOCK)
    Sp = nb * MOBA_BLOCK
    pad = ((0, 0), (0, Sp - S), (0, 0), (0, 0))
    kb = jnp.pad(k, pad).reshape(B, nb, MOBA_BLOCK, H, HEAD_DIM).transpose(0, 3, 1, 2, 4)
    vb = jnp.pad(v, pad).reshape(B, nb, MOBA_BLOCK, H, HEAD_DIM).transpose(0, 3, 1, 2, 4)
    k_mean = jnp.mean(kb.astype(jnp.float32), axis=3)
    topk = min(MOBA_TOPK, nb - 1)
    scale = HEAD_DIM ** -0.5
    b_ix = jnp.arange(B)[:, None, None, None]
    h_ix = jnp.arange(H)[None, None, :, None]

    def chunk(ci):
        t0 = ci * MOBA_Q_CHUNK
        t_pos = t0 + jnp.arange(MOBA_Q_CHUNK)
        cur = t0 // MOBA_BLOCK
        qc = lax.dynamic_slice_in_dim(q, t0, MOBA_Q_CHUNK, axis=1)
        k_own = lax.dynamic_index_in_dim(kb, cur, axis=2, keepdims=False)
        v_own = lax.dynamic_index_in_dim(vb, cur, axis=2, keepdims=False)
        own_pos = cur * MOBA_BLOCK + jnp.arange(MOBA_BLOCK)
        s_own = jnp.einsum('bqhd,bhkd->bqhk', qc, k_own).astype(jnp.float32) * scale
        s_own = jnp.where((own_pos[None, :] <= t_pos[:, None])[None, :, None, :], s_own, -jnp.inf)
        if topk == 0:
            prob = jax.nn.softmax(s_own, axis=-1)
            return jnp.einsum('bqhk,bhkd->bqhd', prob.astype(v.dtype), v_own)
        gate = jnp.einsum('bqhd,bhnd->bqhn', qc.astype(jnp.float32), k_mean)
        gate = jnp.where(jnp.arange(nb) < cur, gate, -jnp.inf)
        _, sel = lax.top_k(gate, topk)
        valid = sel < cur
        k_sel = kb[b_ix, h_ix, sel]
        v_sel = vb[b_ix, h_ix, sel]
        s_sel = jnp.einsum('bqhd,bqhjkd->bqhjk', qc, k_sel).astype(jnp.float32) * scale
        s_sel = jnp.where(valid[..., None], s_sel, -jnp.inf).reshape(B, MOBA_Q_CHUNK, H, topk * MOBA_BLOCK)
        prob = jax.nn.softmax(jnp.concatenate([s_sel, s_own], axis=-1), axis=-1).astype(v.dtype)
        p_sel = prob[..., :topk * MOBA_BLOCK].reshape(B, MOBA_Q_CHUNK, H, topk, MOBA_BLOCK)
        p_own = prob[..., topk * MOBA_BLOCK:]
        return (jnp.einsum('bqhjk,bqhjkd->bqhd', p_sel, v_sel)
                + jnp.einsum('bqhk,bhkd->bqhd', p_own, v_own))

    o = lax.map(chunk, jnp.arange(S // MOBA_Q_CHUNK))
    o = o.transpose(1, 0, 2, 3, 4).reshape(B, S, H * HEAD_DIM)
    return o @ w_out

def first_inputs(seed: int = 0) -> dict:
    key = jax.random.key(seed)
    ks = iter(jax.random.split(key, 32))

    def dense(shape, fan_in):
        return jax.random.normal(next(ks), shape, jnp.float32) * (fan_in ** -0.5)

    def gain(shape):
        return 1.0 + 0.05 * jax.random.normal(next(ks), shape, jnp.float32)

    nA, nB, nC, nD = (_n_layers_of(m) for m in range(N_MIXERS))
    x = jax.random.normal(next(ks), (BATCH, SEQ, D_MODEL), jnp.float32)
    p = jax.random.normal(next(ks), (DEPTH, BATCH, SEQ, PLE_DIM), jnp.float32)
    offsets = jax.random.randint(next(ks), (BATCH, 1), 0, 4096, dtype=jnp.int32)
    positions = offsets + jnp.arange(SEQ, dtype=jnp.int32)[None, :]
    return {
        'x': x,
        'p': p,
        'positions': positions,
        'w_in_sb': dense((nA, D_MODEL, 3 * D_MODEL), D_MODEL),
        'w_out_sb': dense((nA, D_MODEL, D_MODEL), D_MODEL),
        'w_in_dil': dense((nB, D_MODEL, DIL_IN_WIDTH), D_MODEL),
        'w_out_dil': dense((nB, DIL_GROUP_WIDTH, D_MODEL), DIL_GROUP_WIDTH),
        'w_in_dsa': dense((nC, D_MODEL, DSA_IN_WIDTH), D_MODEL),
        'w_out_dsa': dense((nC, D_MODEL, D_MODEL), D_MODEL),
        'w_in_moba': dense((nD, D_MODEL, 3 * D_MODEL), D_MODEL),
        'w_out_moba': dense((nD, D_MODEL, D_MODEL), D_MODEL),
        'g_mix_pre': gain((DEPTH, D_MODEL)),
        'g_mix_post': gain((DEPTH, D_MODEL)),
        'g_ffn_pre': gain((DEPTH, D_MODEL)),
        'g_ffn_post': gain((DEPTH, D_MODEL)),
        'w_ff_in': dense((DEPTH, D_MODEL, D_FF), D_MODEL),
        'w_ff_out': dense((DEPTH, D_FF, D_MODEL), D_FF),
        'g_ple': gain((DEPTH, D_MODEL)),
        'w_ple_gate': dense((DEPTH, D_MODEL, D_MODEL), D_MODEL),
        'w_ple': dense((DEPTH, PLE_DIM, D_MODEL), PLE_DIM),
    }

def first_block(x, p, positions, w_in_sb, w_out_sb, w_in_dil, w_out_dil, w_in_dsa, w_out_dsa,
              w_in_moba, w_out_moba, g_mix_pre, g_mix_post, g_ffn_pre, g_ffn_post,
              w_ff_in, w_ff_out, g_ple, w_ple_gate, w_ple):
    cos, sin = rope_tables(positions)
    h = x
    for i in range(DEPTH):
        mixer, j = i % N_MIXERS, i // N_MIXERS
        u = rms_norm(h, g_mix_pre[i])
        if mixer == 0:
            y = stick_breaking_attention(u, w_in_sb[j], w_out_sb[j])
        elif mixer == 1:
            y = dilated_attention(u, w_in_dil[j], w_out_dil[j], cos, sin)
        elif mixer == 2:
            y = dsa_attention(u, w_in_dsa[j], w_out_dsa[j], cos, sin)
        else:
            y = moba_attention(u, w_in_moba[j], w_out_moba[j], cos, sin)
        h = h + rms_norm(y, g_mix_post[i])
        u = rms_norm(h, g_ffn_pre[i])
        f = jnp.square(jax.nn.relu(u @ w_ff_in[i])) @ w_ff_out[i]
        h = h + rms_norm(f, g_ffn_post[i])
        gate = jax.nn.sigmoid(rms_norm(h, g_ple[i]) @ w_ple_gate[i])
        h = h + (p[i] @ w_ple[i]) * gate
    return h


GRID_W = 64
CTX_LEN = 256
ROPE_THETA_2 = 10000.0
N_MOD = 6
MLA_HEADS = 8
MLA_NOPE = 64
MLA_ROPE = 32
MLA_V = 64
MLA_Q_RANK = 384
MLA_KV_RANK = 256
POOL_WINDOWS = (2, 4, 8, 16)
POOL_WIDTH = 512
POOL_GROUP = POOL_WIDTH // len(POOL_WINDOWS)
MIX0_IN = MLA_Q_RANK + MLA_KV_RANK + MLA_ROPE + POOL_WIDTH
MIX0_OUT = MLA_HEADS * MLA_V + POOL_WIDTH
GQA_HEADS = 8
GQA_KV_HEADS = 2
GQA_HEAD_DIM = 128
GQA_GROUP = GQA_HEADS // GQA_KV_HEADS
GQA_Q_W = GQA_HEADS * GQA_HEAD_DIM
GQA_KV_W = GQA_KV_HEADS * GQA_HEAD_DIM
D_FF_2 = 2816
CONV_W = 3
N_EVEN = (DEPTH + 1) // 2
N_ODD = DEPTH // 2


def rms_norm_2(x, gain=None):
    xf = x.astype(jnp.float32)
    y = (xf * lax.rsqrt(jnp.mean(xf * xf, axis=-1, keepdims=True) + EPS)).astype(x.dtype)
    return y if gain is None else y * gain

def modulate(x, shift, scale):
    return rms_norm_2(x) * (1.0 + scale) + shift

def axial_rope_tables(n_tokens, rope_dim):
    rows = n_tokens // GRID_W
    row = jnp.repeat(jnp.arange(rows, dtype=jnp.float32), GRID_W)
    col = jnp.tile(jnp.arange(GRID_W, dtype=jnp.float32), rows)
    n_freq = rope_dim // 4
    freq = ROPE_THETA_2 ** (-jnp.arange(n_freq, dtype=jnp.float32) / n_freq)
    ang = jnp.concatenate([row[:, None] * freq, col[:, None] * freq], axis=-1)
    return jnp.cos(ang), jnp.sin(ang)

def apply_rope(x, cos, sin):
    xr = x.reshape(x.shape[:-1] + (x.shape[-1] // 2, 2))
    x0, x1 = xr[..., 0], xr[..., 1]
    c = cos[None, :, None, :].astype(x.dtype)
    s = sin[None, :, None, :].astype(x.dtype)
    return jnp.stack([x0 * c - x1 * s, x0 * s + x1 * c], axis=-1).reshape(x.shape)

def attention(q, k, v):
    B, Nq, KV, G, Dh = q.shape
    blk = min(Q_BLOCK, Nq)
    qb = jnp.moveaxis(q.reshape(B, Nq // blk, blk, KV, G, Dh), 1, 0)
    scale = Dh ** -0.5

    def one_block(qi):
        s = jnp.einsum('bqhgd,bkhd->bhgqk', qi, k).astype(jnp.float32) * scale
        p = jax.nn.softmax(s, axis=-1).astype(v.dtype)
        return jnp.einsum('bhgqk,bkhd->bqhgd', p, v)

    o = lax.map(one_block, qb)
    return jnp.moveaxis(o, 0, 1).reshape(B, Nq, KV * G * v.shape[-1])

def multiscale_pool(p, w_pool, s_pool):
    B, T, C = p.shape
    cs = jnp.cumsum(p.astype(jnp.float32), axis=1)
    cs = jnp.concatenate([jnp.zeros((B, 1, C), jnp.float32), cs], axis=1)
    t = jnp.arange(T)
    outs = []
    for g, w in enumerate(POOL_WINDOWS):
        lo = jnp.clip(t - w // 2, 0, T)
        hi = jnp.clip(t - w // 2 + w, 0, T)
        csg = cs[:, :, g * POOL_GROUP:(g + 1) * POOL_GROUP]
        mean = (csg[:, hi] - csg[:, lo]) / (hi - lo).astype(jnp.float32)[None, :, None]
        d = mean.astype(p.dtype) - p[:, :, g * POOL_GROUP:(g + 1) * POOL_GROUP]
        outs.append(d @ w_pool[g])
    return jnp.concatenate(outs, axis=-1) * s_pool

def mla_q(cq, g_q, w_uq, cos, sin, rope):
    B, T, _ = cq.shape
    q = (rms_norm_2(cq, g_q) @ w_uq).reshape(B, T, MLA_HEADS, MLA_NOPE + MLA_ROPE)
    if rope:
        q = jnp.concatenate([q[..., :MLA_NOPE], apply_rope(q[..., MLA_NOPE:], cos, sin)], axis=-1)
    return q[:, :, :, None, :]

def mla_kv(ckv, kr, g_kv, w_uk, w_uv, cos, sin, rope):
    B, T, _ = ckv.shape
    ckv = rms_norm_2(ckv, g_kv)
    k_nope = (ckv @ w_uk).reshape(B, T, MLA_HEADS, MLA_NOPE)
    v = (ckv @ w_uv).reshape(B, T, MLA_HEADS, MLA_V)
    kr = kr[:, :, None, :]
    if rope:
        kr = apply_rope(kr, cos, sin)
    k = jnp.concatenate([k_nope, jnp.broadcast_to(kr, (B, T, MLA_HEADS, MLA_ROPE))], axis=-1)
    return k, v

def mla_pool_mixer(hc, hl, w_in, g_q, w_uq, g_kv, w_uk, w_uv, w_pool, s_pool, w_out, cos, sin, need_ctx):
    i_kv = MLA_Q_RANK
    i_kr = i_kv + MLA_KV_RANK
    i_p = i_kr + MLA_ROPE
    pl = hl @ w_in
    ql = mla_q(pl[..., :i_kv], g_q, w_uq, cos, sin, True)
    kl, vl = mla_kv(pl[..., i_kv:i_kr], pl[..., i_kr:i_p], g_kv, w_uk, w_uv, cos, sin, True)
    if need_ctx:
        pc = hc @ w_in
        qc = mla_q(pc[..., :i_kv], g_q, w_uq, cos, sin, False)
        kc, vc = mla_kv(pc[..., i_kv:i_kr], pc[..., i_kr:i_p], g_kv, w_uk, w_uv, cos, sin, False)
    else:
        pkv = hc @ w_in[:, i_kv:i_p]
        kc, vc = mla_kv(pkv[..., :MLA_KV_RANK], pkv[..., MLA_KV_RANK:], g_kv, w_uk, w_uv, cos, sin, False)
    al = attention(ql, jnp.concatenate([kc, kl], axis=1), jnp.concatenate([vc, vl], axis=1))
    ol = jnp.concatenate([al, multiscale_pool(pl[..., i_p:], w_pool, s_pool)], axis=-1) @ w_out
    oc = None
    if need_ctx:
        ac = attention(qc, kc, vc)
        oc = jnp.concatenate([ac, multiscale_pool(pc[..., i_p:], w_pool, s_pool)], axis=-1) @ w_out
    return oc, ol

def gqa_q(a, g_q, cos, sin, rope):
    B, T, _ = a.shape
    q = rms_norm_2(a.reshape(B, T, GQA_HEADS, GQA_HEAD_DIM), g_q)
    if rope:
        q = apply_rope(q, cos, sin)
    return q.reshape(B, T, GQA_KV_HEADS, GQA_GROUP, GQA_HEAD_DIM)

def gqa_kv(a, g_k, cos, sin, rope):
    B, T, _ = a.shape
    k = rms_norm_2(a[..., :GQA_KV_W].reshape(B, T, GQA_KV_HEADS, GQA_HEAD_DIM), g_k)
    v = a[..., GQA_KV_W:].reshape(B, T, GQA_KV_HEADS, GQA_HEAD_DIM)
    if rope:
        k = apply_rope(k, cos, sin)
    return k, v

def gqa_mixer(hc, hl, w_in, g_q, g_k, w_out, cos, sin, need_ctx):
    pl = hl @ w_in
    ql = gqa_q(pl[..., :GQA_Q_W], g_q, cos, sin, True)
    kl, vl = gqa_kv(pl[..., GQA_Q_W:], g_k, cos, sin, True)
    if need_ctx:
        pc = hc @ w_in
        qc = gqa_q(pc[..., :GQA_Q_W], g_q, cos, sin, False)
        kc, vc = gqa_kv(pc[..., GQA_Q_W:], g_k, cos, sin, False)
    else:
        kc, vc = gqa_kv(hc @ w_in[:, GQA_Q_W:], g_k, cos, sin, False)
    ol = attention(ql, jnp.concatenate([kc, kl], axis=1), jnp.concatenate([vc, vl], axis=1)) @ w_out
    oc = attention(qc, kc, vc) @ w_out if need_ctx else None
    return oc, ol

def conv_ffn(h, w_up, conv_w, conv_b, w_down):
    a = h @ w_up
    g, u = a[..., :D_FF_2], a[..., D_FF_2:]
    T = g.shape[1]
    half = CONV_W // 2
    gp = jnp.pad(g, ((0, 0), (half, half), (0, 0)))
    acc = conv_b + gp[:, 0:T] * conv_w[0]
    for j in range(1, CONV_W):
        acc = acc + gp[:, j:j + T] * conv_w[j]
    return (jax.nn.silu(acc) * u) @ w_down

def second_inputs(seed: int = 0) -> dict:
    key = jax.random.key(seed)
    ks = iter(jax.random.split(key, 32))
    D = D_MODEL

    def normal(shape, scale=1.0):
        return jax.random.normal(next(ks), shape, jnp.float32) * scale

    def gain(shape):
        return 1.0 + 0.05 * normal(shape)

    return {
        'x': normal((BATCH, SEQ, D)),
        'c': normal((BATCH, D)),
        'ctx': normal((BATCH, CTX_LEN, D)),
        'c_ctx': normal((D,)),
        'w_mod': normal((DEPTH, D, N_MOD * D), D ** -0.5),
        'b_mod': normal((DEPTH, N_MOD * D), 0.02),
        'mix0_w_in': normal((N_EVEN, D, MIX0_IN), D ** -0.5),
        'mla_g_q': gain((N_EVEN, MLA_Q_RANK)),
        'mla_w_uq': normal((N_EVEN, MLA_Q_RANK, MLA_HEADS * (MLA_NOPE + MLA_ROPE)), MLA_Q_RANK ** -0.5),
        'mla_g_kv': gain((N_EVEN, MLA_KV_RANK)),
        'mla_w_uk': normal((N_EVEN, MLA_KV_RANK, MLA_HEADS * MLA_NOPE), MLA_KV_RANK ** -0.5),
        'mla_w_uv': normal((N_EVEN, MLA_KV_RANK, MLA_HEADS * MLA_V), MLA_KV_RANK ** -0.5),
        'pool_w': normal((N_EVEN, len(POOL_WINDOWS), POOL_GROUP, POOL_GROUP), POOL_GROUP ** -0.5),
        'pool_scale': gain((N_EVEN, POOL_WIDTH)),
        'mix0_w_out': normal((N_EVEN, MIX0_OUT, D), MIX0_OUT ** -0.5),
        'gqa_w_in': normal((N_ODD, D, GQA_Q_W + 2 * GQA_KV_W), D ** -0.5),
        'gqa_g_q': gain((N_ODD, GQA_HEAD_DIM)),
        'gqa_g_k': gain((N_ODD, GQA_HEAD_DIM)),
        'gqa_w_out': normal((N_ODD, GQA_Q_W, D), GQA_Q_W ** -0.5),
        'ffn_w_up': normal((DEPTH, D, 2 * D_FF_2), D ** -0.5),
        'ffn_conv_w': normal((DEPTH, CONV_W, D_FF_2), CONV_W ** -0.5),
        'ffn_conv_b': normal((DEPTH, D_FF_2), 0.02),
        'ffn_w_down': normal((DEPTH, D_FF_2, D), D_FF_2 ** -0.5),
        'g_final': gain((D,)),
    }

def second_block(x, c, ctx, c_ctx, w_mod, b_mod, mix0_w_in, mla_g_q, mla_w_uq, mla_g_kv, mla_w_uk, mla_w_uv,
              pool_w, pool_scale, mix0_w_out, gqa_w_in, gqa_g_q, gqa_g_k, gqa_w_out,
              ffn_w_up, ffn_conv_w, ffn_conv_b, ffn_w_down, g_final):
    B, N, D = x.shape
    cos_a, sin_a = axial_rope_tables(N, MLA_ROPE)
    cos_c, sin_c = axial_rope_tables(N, GQA_HEAD_DIM)
    xl, xc = x, ctx
    for i in range(DEPTH):
        last = i == DEPTH - 1
        j = i // 2
        ml = (jax.nn.silu(c) @ w_mod[i] + b_mod[i]).reshape(B, N_MOD, 1, D)
        mc = (jax.nn.silu(c_ctx) @ w_mod[i] + b_mod[i]).reshape(N_MOD, D)
        hl = modulate(xl, ml[:, 0], ml[:, 1])
        hc = modulate(xc, mc[0], mc[1])
        if i % 2 == 0:
            oc, ol = mla_pool_mixer(hc, hl, mix0_w_in[j], mla_g_q[j], mla_w_uq[j], mla_g_kv[j], mla_w_uk[j],
                                    mla_w_uv[j], pool_w[j], pool_scale[j], mix0_w_out[j], cos_a, sin_a, not last)
        else:
            oc, ol = gqa_mixer(hc, hl, gqa_w_in[j], gqa_g_q[j], gqa_g_k[j], gqa_w_out[j], cos_c, sin_c, not last)
        xl = xl + ml[:, 2] * ol
        xl = xl + ml[:, 5] * conv_ffn(modulate(xl, ml[:, 3], ml[:, 4]),
                                      ffn_w_up[i], ffn_conv_w[i], ffn_conv_b[i], ffn_w_down[i])
        if not last:
            xc = xc + mc[2] * oc
            xc = xc + mc[5] * conv_ffn(modulate(xc, mc[3], mc[4]),
                                       ffn_w_up[i], ffn_conv_w[i], ffn_conv_b[i], ffn_w_down[i])
    return rms_norm_2(xl, g_final)


def setup_inputs(seed=0):
    out = dict(first_inputs(seed))
    for name, value in second_inputs(seed + 1).items():
        if name != "x":
            out[name + "_2"] = value
    return out


def reference(
    x, p, positions, w_in_sb, w_out_sb, w_in_dil, w_out_dil, w_in_dsa, w_out_dsa, w_in_moba,
    w_out_moba, g_mix_pre, g_mix_post, g_ffn_pre, g_ffn_post, w_ff_in, w_ff_out, g_ple,
    w_ple_gate, w_ple, c_2, ctx_2, c_ctx_2, w_mod_2, b_mod_2, mix0_w_in_2, mla_g_q_2,
    mla_w_uq_2, mla_g_kv_2, mla_w_uk_2, mla_w_uv_2, pool_w_2, pool_scale_2, mix0_w_out_2,
    gqa_w_in_2, gqa_g_q_2, gqa_g_k_2, gqa_w_out_2, ffn_w_up_2, ffn_conv_w_2, ffn_conv_b_2,
    ffn_w_down_2, g_final_2,
):
    x = first_block(
        x, p, positions, w_in_sb, w_out_sb, w_in_dil, w_out_dil, w_in_dsa, w_out_dsa, w_in_moba,
        w_out_moba, g_mix_pre, g_mix_post, g_ffn_pre, g_ffn_post, w_ff_in, w_ff_out, g_ple,
        w_ple_gate, w_ple,
    )
    return second_block(
        x, c_2, ctx_2, c_ctx_2, w_mod_2, b_mod_2, mix0_w_in_2, mla_g_q_2, mla_w_uq_2,
        mla_g_kv_2, mla_w_uk_2, mla_w_uv_2, pool_w_2, pool_scale_2, mix0_w_out_2, gqa_w_in_2,
        gqa_g_q_2, gqa_g_k_2, gqa_w_out_2, ffn_w_up_2, ffn_conv_w_2, ffn_conv_b_2, ffn_w_down_2,
        g_final_2,
    )


_drawn_inputs = setup_inputs


def setup_inputs(seed=0):
    import zlib

    import numpy as np

    out = dict(_drawn_inputs(seed))
    spreads = {}
    factors = {'g_ple': 7.303,
     'ctx_2': 2.94,
     'b_mod_2': 2.848,
     'mla_g_q_2': 8.0,
     'mla_g_kv_2': 8.0,
     'pool_scale_2': 6.97,
     'gqa_g_q_2': 8.0,
     'gqa_g_k_2': 8.0,
     'ffn_conv_b_2': 8.0}
    for name, (base, spread) in spreads.items():
        noise = np.random.default_rng([zlib.crc32(name.encode()), seed]).standard_normal(out[name].shape)
        drawn = base * np.exp(spread * noise) if base else spread * noise
        out[name] = __import__('jax').numpy.asarray(drawn.astype(out[name].dtype))
    for name, factor in factors.items():
        out[name] = (out[name] * factor).astype(out[name].dtype)
    return out
```

```python
from contextlib import ExitStack

import concourse.bass as bass
import numpy as np
from concourse import mybir

F32 = mybir.dt.float32
F32R = mybir.dt.float32r
I32 = mybir.dt.int32
ALU = mybir.AluOpType
ACT = mybir.ActivationFunctionType
AX = mybir.AxisListType

P = 128
D = 1024
S = 256
T2 = 2 * S
KD = D // P
EPS = 1e-6
DFF = 4096
DFF2 = 2816
KF2 = DFF2 // P
HEADS, HD = 16, 64
DIL = (1, 4, 16)
DIL_BACK = 128
MLA_HEADS, MLA_NOPE, MLA_ROPE = 8, 64, 32
MLA_HD = MLA_NOPE + MLA_ROPE
GQA_HEADS, GQA_KV = 8, 2
POOL_W = (2, 4, 8, 16)
PAD = 16
SLOT = 2048
RAW = 4
NEG = -1.0e30
STOP = None


def constants():
    i = np.arange(P)
    ident = np.eye(P)
    ones = np.ones((P, P))
    negtri = -(i[:, None] >= i[None, :]).astype(float)
    perm1 = np.zeros((P, P))
    for base in (0, 64):
        for j in range(8):
            perm1[base + j + 8, base + j] = -1.0
            perm1[base + j, base + j + 8] = 1.0
    perm_g = np.zeros((P, P))
    for j in range(0, P, 2):
        perm_g[j + 1, j] = -1.0
        perm_g[j, j + 1] = 1.0
    perm_m = np.zeros((P, P))
    perm_m[MLA_NOPE:MLA_HD, MLA_NOPE:MLA_HD] = perm_g[:MLA_ROPE, :MLA_ROPE]
    past = (i[:, None] < i[None, :]).astype(float)
    squares = np.concatenate([ident, ones, negtri, -ones, perm1, perm_m, perm_g, past], axis=1)

    freq = np.zeros((P, 1))
    for base in (0, 64):
        freq[base:base + 16, 0] = 500000.0 ** (-np.tile(np.arange(8), 2) / 8.0)

    def axial(dim):
        t = np.arange(S)
        f = 10000.0 ** (-np.arange(dim // 4) / (dim // 4))
        ang = np.concatenate([(t // 64)[:, None] * f, (t % 64)[:, None] * f], axis=-1)
        return np.repeat(np.cos(ang).T, 2, axis=0), np.repeat(np.sin(ang).T, 2, axis=0)

    cm, sm = np.ones((P, S)), np.zeros((P, S))
    cm[MLA_NOPE:MLA_HD], sm[MLA_NOPE:MLA_HD] = axial(MLA_ROPE)
    cg, sg = axial(P)
    t = np.arange(S)
    count = [np.clip(t - w // 2 + w, 0, S) - np.clip(t - w // 2, 0, S) for w in POOL_W]
    rcount = np.broadcast_to((1.0 / np.stack(count)).reshape(1, -1), (P, 4 * S))
    def band(q0, nk):
        q = q0 + i[:, None]
        k = np.arange(nk)[None, :]
        return [np.where((k <= q) & ((q - k) % d == 0) & (q - k <= DIL_BACK * d), 0.0, NEG) for d in DIL]
    masks = np.concatenate(band(0, P) + band(P, 2 * P), axis=1)
    rope2 = np.concatenate([cm, sm, cg, sg], axis=1)
    return {k: np.ascontiguousarray(v, dtype=np.float32) for k, v in dict(
        const_squares=squares, const_freq=freq, const_rope2=rope2, const_rcount=rcount, const_masks=masks).items()}


class Counting:

    def __init__(self, noted):
        self.noted, self.seen, self.count, self.engine, self.sems = noted, {}, {}, {}, {}
        self.last = {}

    def raised(self, engine, family, key=None, by=1):
        assert self.engine.setdefault(family, engine) == engine, family
        self.count[family] = self.count.get(family, 0) + by
        self.seen[family, key] = self.count[family]
        self.last[engine] = (family, self.count[family])
        return by

    def note(self, family, key):
        self.seen[family, key] = self.count[family]

    def end(self, engine, i):
        self.seen["end", (engine, i)] = self.last.get(engine)

    def after(self, family, key=None):
        return self.noted[family, key] if self.noted else 1

    def after_phase(self, engine, i):
        last = self.noted["end", (engine, i)] if self.noted else None
        return (self.sems[last[0]], last[1]) if last else None


FAMILIES = """weights_high weights_low weights_used small_loaded const_loaded scalar_step vector_step tensor_step
 group_read_s group_read_v operand_high operand_low stat_squares stat_summed rstd_ready
 normed moved rotated swapped scores weights_exp weights_normed turned turned_copied attended
 max_ready fail_ready fail_summed stick_weights masked""".split()


def build(nc, A, out, noted, dry_stop=None):
    C = Counting(noted)
    with ExitStack() as ctx:
        for f in FAMILIES:
            C.sems[f] = ctx.enter_context(nc.semaphore(f))
        landed = [ctx.enter_context(nc.semaphore(f"landed{i}")) for i in range(RAW)]
        loaded = {n: ctx.enter_context(nc.semaphore(f"loaded_{n}")) for n in ("squares", "rows", "freq", "pos", "x", "arena", "p")}
        stored = ctx.enter_context(nc.semaphore("stored"))

        def sb(name, shape, dt=F32):
            return ctx.enter_context(nc.sbuf_tensor(name, shape, dt))

        HH0 = -(-nc.sbuf_base // 32) * 32
        hh = sb("hh", [P, 8192], F32R)
        hl = sb("hl", [P, 8192], F32R)
        raw = sb("raw", [P, RAW, SLOT])
        whi = sb("whi", [P, 2, SLOT], F32R)
        wlo = sb("wlo", [P, 2, SLOT], F32R)
        h = sb("h", [P, KD, T2])
        uh = sb("uh", [P, KD, T2], F32R)
        ul = sb("ul", [P, KD, T2], F32R)
        y = sb("y", [P, KD, T2])
        squares = sb("squares", [P, 8, P])
        sq = sb("sq", [P, 2, T2])
        lnv = sb("lnv", [P, T2])
        rstd = sb("rstd", [P, T2])
        cos1 = sb("cos1", [P, S])
        sin1 = sb("sin1", [P, S])
        freq = sb("freq", [P, 1])
        vec = sb("vec", [P, P])
        convv = sb("convv", [P, 2, 96])
        bmod = sb("bmod", [P, 96])
        modc = sb("modc", [P, 2, 48, 2])
        modrow = sb("modrow", [2, 512])
        silu = sb("silu", [P, 2, KD])
        cc = sb("cc", [P, KD, 2])
        small = sb("small", [P, 64])
        ident, ones, negtri, negones, perm1, perm_m, perm_g, past = (squares[:, j, :] for j in range(8))
        ps = ctx.enter_context(nc.psum_tensor("ps", [P, 8, 512], F32))


        def arena(name, shape, off, dt=F32):
            n = int(np.prod(shape[1:])) * 4
            assert off + n <= 65536, (name, off + n)
            return nc.alloc_sbuf_tensor_at(name, shape, dt, offset=HH0 + off)

        K = 1024
        rows = arena("rows", [P, 4, P], 0)
        xin = arena("xin", [P, 4, D], 4 * K)
        posi = arena("posi", [P, S], 20 * K, I32)
        ang = arena("ang", [P, S], 21 * K)
        turns = arena("turns", [P, 2, S], 22 * K)
        q1 = arena("q1", [P, 8, S], 0)
        k1 = arena("k1", [P, 8, S], 8 * K)
        v1 = arena("v1", [P, 2, D], 16 * K)
        sbt = arena("sbt", [P, 2, 384], 24 * K)
        sbe = arena("sbe", [P, 2, 384], 27 * K)
        sbl = arena("sbl", [P, 2, 384], 30 * K)
        sbf = arena("sbf", [P, 2, 384], 33 * K)
        sba = arena("sba", [P, 2, 384], 36 * K)
        qk2 = arena("qk2", [P, 24, S], 0)
        v2 = arena("v2", [P, 2, 3 * 512], 24 * K)
        masks = arena("masks", [P, 1152], 36 * K)
        sm = arena("sm", [P, 2, 768], 41 * K)
        pr = arena("pr", [P, 2, 768], 47 * K)
        pt = arena("pt", [P, 2, 768], 53 * K)
        rtmp = arena("rtmp", [P, 2, S], 59 * K)
        pbuf = arena("pbuf", [P, 4, 2, S + 2 * PAD], 0)
        abuf = arena("abuf", [P, 4, 2, S + 2 * PAD], 10 * K)
        rcount = arena("rcount", [P, 4, S], 20 * K)
        pdif = arena("pdif", [P, 4, T2], 24 * K)
        qm = arena("qm", [P, 8, T2], 0)
        km = arena("km", [P, 8, T2], 16 * K)
        vm = arena("vm", [P, 4, 512], 32 * K)
        kr = arena("kr", [P, T2], 62 * K)
        ropem = arena("ropem", [P, 2, S], 40 * K)
        ch = arena("ch", [P, 5, T2], 42 * K, F32R)
        cl = arena("cl", [P, 5, T2], 52 * K, F32R)
        qg = arena("qg", [P, 8, S], 0)
        kg = arena("kg", [P, 2, T2], 8 * K)
        vg = arena("vg", [P, 4, S], 12 * K)
        ropeg = arena("ropeg", [P, 2, S], 16 * K)
        pin = arena("pin", [P, 2, S], 0)
        ph_ = arena("ph", [P, 2, S], 2 * K, F32R)
        pl_ = arena("pl", [P, 2, S], 4 * K, F32R)
        pt32 = arena("pt32", [P, 2, S], 6 * K)
        ge = arena("ge", [P, 2, 2, S], 8 * K)
        work = sb("work", [P, 2, 2, S])
        cacc = arena("cacc", [P, 2, 512], 24 * K)
        csil = arena("csil", [P, 2, 512], 28 * K)

        def hid(buf, t, T):
            return buf[:, t * T:(t + 1) * T]

        chunks = []
        phases = []

        def linear(name, W, nk, cols, T, kind, mode="T", m=P, xin=("u", 0), kmax=8, tok0=0, k0=0, split=True, last=None):
            job = dict(kind="linear", name=name, evac=kind, T=T, mode=mode, m=m, x=xin, tok0=tok0, groups=[])
            for g, (c0, nc_) in enumerate(cols):
                grp = []
                nparts = -(-nk // kmax)
                sizes = [nk // nparts + (1 if i < nk % nparts else 0) for i in range(nparts)]
                a = 0
                for kn in sizes:
                    ck = dict(job=job, g=g, k=a, kn=kn, C=nc_, src=W[(k0 + a) * P:(k0 + a + kn) * P, c0:c0 + nc_],
                              r=len(chunks), first=a == 0, last=a + kn == nk)
                    assert kn * nc_ <= SLOT
                    chunks.append(ck)
                    grp.append(ck)
                    a += kn
                job["groups"].append(grp)
            phases.append(job)
            return job

        def phase(kind, **kw):
            phases.append(dict(kind=kind, **kw))

        def pairs(c0, n, w=256):
            return [(c0 + j, w) for j in range(0, n, w)]

        ROWS_G = {}
        row_list = []

        def rows_of(name, ap, n):
            ROWS_G[name] = len(row_list)
            for j in range(n):
                row_list.append((ap, j))

        phase("init")
        lay = 0
        for l in range(2):
            phase("stats", src="h", n=8, T=S, D=D)
            phase("apply", src="h", n=8, T=S, gain=("g_mix_pre", l))
            if l == 0:
                Wi = A["w_in_sb"][0]
                linear("stick_qk", Wi, 8, pairs(0, 2 * D), S, "qk1")
                linear("stick_v", Wi, 8, pairs(2 * D, D), S, "v", mode="V")
                phase("stick")
                linear("stick_out", A["w_out_sb"][0], 8, pairs(0, D), S, "y")
            else:
                Wi = A["w_in_dil"][0]
                for g in range(3):
                    linear(f"dil_qk{g}", Wi, 8, pairs(g * 1536, 1024), S, "qk2")
                    linear(f"dil_v{g}", Wi, 8, pairs(g * 1536 + 1024, 512), S, "v", mode="V")
                phase("rope", what="dil")
                phase("softmax", what="dil")
                linear("dil_out", A["w_out_dil"][0], 4, pairs(0, D), S, "y")
            phase("stats", src="y", n=8, T=S, D=D)
            phase("residual", gain=("g_mix_post", l))
            phase("stats", src="h", n=8, T=S, D=D)
            phase("apply", src="h", n=8, T=S, gain=("g_ffn_pre", l))
            linear(f"ff_in{l}", A["w_ff_in"][l], 8, pairs(0, DFF), S, "relu2")
            linear(f"ff_out{l}", A["w_ff_out"][l], 32, pairs(0, D), S, "y", xin=("h", 0))
            phase("stats", src="y", n=8, T=S, D=D)
            phase("residual", gain=("g_ffn_post", l))
            phase("stats", src="h", n=8, T=S, D=D)
            phase("apply", src="h", n=8, T=S, gain=("g_ple", l))
            linear(f"gate{l}", A["w_ple_gate"][l], 8, pairs(0, D), S, "gate")
            phase("ple", l=l)
            linear(f"ple{l}", A["w_ple"][l], 2, pairs(0, D), S, "addgated", xin=("p", 0))
        phase("mod")
        for l in range(2):
            Tt = T2 if l == 0 else S
            phase("stats", src="h", n=8, T=T2, D=D)
            phase("apply", src="h", n=8, T=T2, mod=(l, 0))
            if l == 0:
                Wi = A["mix0_w_in_2"][0]
                linear("mix_c", Wi, 8, [(0, 256), (256, 256), (512, 160)], T2, "mixc")
                linear("mix_p", Wi, 8, pairs(672, 512), T2, "mixp")
                phase("pool")
                linear("pool_w", A["pool_w_2"][0].rearrange("g i o -> (g i) o"), 4, [(0, P)], T2, "poolw", xin=("u", 0))
                for src0, n, dd, g in ((0, 3, 384, "mla_g_q"), (3, 2, 256, "mla_g_kv")):
                    phase("stats", src="y", s0=src0, n=n, T=T2, D=dd)
                    phase("apply", src="y", s0=src0, n=n, T=T2, gain=(g, 0), dst="c")
                linear("uq", A["mla_w_uq_2"][0], 3, pairs(0, 768, 192), T2, "uq", m=96, xin=("c", 0))
                linear("uk", A["mla_w_uk_2"][0], 2, pairs(0, 512), T2, "uk", xin=("c", 3))
                linear("uv", A["mla_w_uv_2"][0], 2, pairs(0, 512), T2, "v", mode="V", xin=("c", 3))
                phase("rope", what="mla")
                phase("softmax", what="mla")
                linear("mix_out", A["mix0_w_out_2"][0], 8, pairs(0, D), T2, "gated", last=(0, 2))
                phases[-1]["mod"] = (0, 2)
            else:
                Wi = A["gqa_w_in_2"][0]
                linear("gqa_q", Wi, 8, pairs(0, D), S, "qg")
                linear("gqa_k", Wi, 8, pairs(D, 256), T2, "kg")
                linear("gqa_v", Wi, 8, pairs(D + 256, 256), T2, "v", mode="V")
                phase("qknorm")
                phase("rope", what="gqa")
                phase("softmax", what="gqa")
                linear("gqa_out", A["gqa_w_out_2"][0], 8, pairs(0, D), S, "gated")
                phases[-1]["mod"] = (1, 2)
            phase("stats", src="h", n=8, T=Tt, D=D)
            phase("apply", src="h", n=8, T=Tt, mod=(l, 3))
            Wu, Wd = A["ffn_w_up_2"][l], A["ffn_w_down_2"][l]
            halves = [(0, 12), (12, 10)] if l == 0 else [(0, 22)]
            for n, (f0, nf) in enumerate(halves):
                cols = [c for j in range(nf // 2) for c in ((f0 * P + j * 256, 256), (DFF2 + f0 * P + j * 256, 256))]
                linear(f"up{l}{n}", Wu, 8, cols, Tt, "conv")
                phases[-1].update(l=l, f0=f0)
                only = "gated" if len(halves) == 1 else ("y" if n == 0 else "gated2")
                linear(f"down{l}{n}", Wd, nf, pairs(0, D), Tt, only, xin=("h", 0), k0=f0)
                phases[-1]["mod"] = (l, 5)
        phase("stats", src="h", n=8, T=S, D=D)
        phase("final")
        if dry_stop is not None:
            phases[:] = phases[:dry_stop]
            live = {id(p) for p in phases}
            chunks[:] = [c for c in chunks if id(c["job"]) in live]
            phase("dump")
        for i, p in enumerate(phases):
            p["i"] = i
        order = []
        for p in phases:
            if p["kind"] == "linear":
                order += [c for g in p["groups"] for c in g]
            if p["kind"] == "mod":
                for l in range(2):
                    for c in range(12):
                        for half in range(2):
                            order.append(dict(job=p, mod=(l, c, half), kn=4, C=512,
                                              src=A["w_mod_2"][l][half * 512:(half + 1) * 512, c * 512:(c + 1) * 512]))
        chunks = order
        n_split = 0
        for r, c in enumerate(chunks):
            c["r"] = r
            if "mod" not in c:
                c["s"] = n_split
                n_split += 1
        splits = [c for c in chunks if "s" in c]

        def splits_in_turn(s, p):
            return s < len(splits) and (splits[s]["job"]["i"] < mod_i or p["i"] >= mod_i)

        mod_i = max([q["i"] for q in phases if q["kind"] == "mod"] + [-1])
        mod_s = [c["s"] for c in splits if c["job"]["i"] > mod_i][:2] if mod_i >= 0 else []
        gi = 0
        for p in phases:
            if p["kind"] == "linear":
                for g in p["groups"]:
                    for c in g:
                        c["gi"] = gi
                    gi += 1
        VREADS = {"y", "gated", "gated2", "addgated", "conv", "poolw"}
        group_sem = {}
        for p in phases:
            if p["kind"] == "linear":
                for g in p["groups"]:
                    group_sem[g[0]["gi"]] = "group_read_v" if p["evac"] in VREADS else "group_read_s"

        def tokens(p):
            return slice(p.get("tok0", 0), p.get("tok0", 0) + p["T"])

        def gain(p, k):
            name, l = p["gain"]
            c = ROW[name] + (l * 8 if name.startswith("g_") else 0) + k
            return vec[:, c:c + 1]

        ROW = {}
        at_row = 0
        for name, n in (("g_mix_pre", 16), ("g_mix_post", 16), ("g_ffn_pre", 16), ("g_ffn_post", 16), ("g_ple", 16),
                        ("g_final_2", 8), ("mla_g_q", 3), ("mla_g_kv", 2), ("pool_scale_2", 4), ("gqa_g_q", 1),
                        ("gqa_g_k", 1), ("c_2", 8), ("c_ctx_2", 8)):
            ROW[name] = at_row
            at_row += n

        def mod_at(l, which, k, seg):
            return modc[:, l, which * 8 + k, seg:seg + 1]

        def operand(p, k, T, hi):
            name, off = p["x"]
            t = tokens(p)
            if name == "u":
                return (uh if hi else ul)[:, off + k, t]
            if name == "h":
                return hid(hh if hi else hl, off + k, T)
            if name == "c":
                return (ch if hi else cl)[:, off + k, t]
            return (ph_ if hi else pl_)[:, k, :]

        def acc(g, T, cols=None):
            b = (g["gi"] % 2) * 2
            return ps[:, b:b + 2, 0:T]

        def segs(T):
            return [(s, slice(s * S, (s + 1) * S)) for s in range(T // S)]

        def softmax_units(what):
            units = []
            if what == "dil":
                for pair in range(4):
                    for q in range(2):
                        for hd in (2 * pair, 2 * pair + 1):
                            nk = q + 1
                            o = (hd % 2) * 64
                            prod = []
                            for g in range(3):
                                prod.append((qk2[o:o + 64, g * 8 + hd // 2, q * P:(q + 1) * P],
                                             qk2[o:o + 64, g * 8 + 4 + hd // 2, 0:nk * P], g * nk * P))
                            vals = [v2[:, kt, g * 512 + hd * 64:g * 512 + hd * 64 + 64] for g in range(3) for kt in range(nk)]
                            units.append(dict(prod=prod, W=3 * nk * P, mask=(0 if q == 0 else 384), vals=vals,
                                              scale=HD ** -0.5, rows=(o, o + 64), pair=pair, q=q, opair=pair, col=q * P))
            if what == "mla":
                n = 0
                for seg in (1, 0):
                    for pair in range(4):
                        for q in range(2):
                            for hd in (2 * pair, 2 * pair + 1):
                                o = (hd % 2) * 64
                                keys = [(S, T2)] if seg == 1 else [(0, T2)]
                                a, b = keys[0]
                                t0 = seg * S + q * P
                                prod = [(qm[0:96, hd, t0:t0 + P], km[0:96, hd, a:b], 0)]
                                vals = [vm[:, kt, hd * 64:(hd + 1) * 64] for kt in range(a // P, b // P)]
                                units.append(dict(prod=prod, W=b - a, mask=None, vals=vals, scale=MLA_HD ** -0.5,
                                                  rows=(o, o + 64), pair=n, opair=pair, q=q, col=t0))
                        n += 1
            if what == "gqa":
                for hd in range(8):
                    for q in range(2):
                        kv = hd // 4
                        prod = [(qg[:, hd, q * P:(q + 1) * P], kg[:, kv, :], 0)]
                        vals = [vg[:, kt, kv * P:(kv + 1) * P] for kt in range(4)]
                        units.append(dict(prod=prod, W=T2, mask=None, vals=vals, scale=P ** -0.5, rows=(0, P),
                                          pair=hd, opair=hd, q=q, col=q * P))
            for n, u in enumerate(units):
                u["n"] = n
                u["ends"] = n + 1 == len(units) or units[n + 1]["pair"] != u["pair"]
            return units

        def rope_tiles(what):
            if what == "dil":
                return [(qk2[:, t, :], perm1, cos1[:, :], sin1[:, :], P) for t in range(24)]
            if what == "mla":
                r = MLA_HD
                return ([(kr[0:r, 0:S], perm_m[0:r, 0:r], ropem[0:r, 0, :], ropem[0:r, 1, :], r)]
                        + [(qm[0:r, hd, 0:S], perm_m[0:r, 0:r], ropem[0:r, 0, :], ropem[0:r, 1, :], r) for hd in range(8)])
            return ([(qg[:, hd, :], perm_g, ropeg[:, 0, :], ropeg[:, 1, :], P) for hd in range(8)]
                    + [(kg[:, kv, 0:S], perm_g, ropeg[:, 0, :], ropeg[:, 1, :], P) for kv in range(2)])

        def at(family, key=None):
            return C.sems[family], C.after(family, key)

        def ended(i):
            return [v for v in (C.after_phase(e, i - 1) for e in ENGINES) if v] if i else []

        ENGINES = ("tensor", "scalar", "vector")

        block = ctx.enter_context(nc.Block())

        @block.sync
        def _(sp):
            with nc.allow_non_contiguous_dma(reason="small"):
                sp.dma_start(squares[:, :, :], A["const_squares"].rearrange("p (j c) -> p j c", j=8)).then_inc(loaded["squares"], 16)
                sp.dma_start(xin[:, 0:2, :], A["x"][0].rearrange("(t p) d -> p t d", p=P)).then_inc(loaded["x"], 16)
                sp.dma_start(xin[:, 2:4, :], A["ctx_2"][0].rearrange("(t p) d -> p t d", p=P)).then_inc(loaded["x"], 16)
                row = lambda ap: ap.rearrange("a (k p) -> (a k) p", p=P)
                r0 = 0
                for name in ("g_mix_pre", "g_mix_post", "g_ffn_pre", "g_ffn_post", "g_ple", "g_final_2", "mla_g_q_2",
                             "mla_g_kv_2", "pool_scale_2", "gqa_g_q_2", "gqa_g_k_2", "c_2", "c_ctx_2"):
                    ap = A[name]
                    ap = row(ap) if len(ap.shape) == 2 else ap.rearrange("(k p) -> k p", p=P)
                    sp.dma_start(rows[r0:r0 + ap.shape[0], 0, :], ap).then_inc(loaded["rows"], 16)
                    r0 += ap.shape[0]
                for l in range(2):
                    sp.dma_start(rows[0:66, 1 + l, :], A["ffn_conv_w_2"][l].rearrange("j (k p) -> (j k) p", p=P)).then_inc(loaded["rows"], 16)
                    sp.dma_start(rows[66:88, 1 + l, :], A["ffn_conv_b_2"][l:l + 1].rearrange("a (k p) -> (a k) p", p=P)).then_inc(loaded["rows"], 16)
                sp.dma_start(rows[0:96, 3, :], row(A["b_mod_2"])).then_inc(loaded["rows"], 16)
                sp.dma_start(freq[:, :], A["const_freq"]).then_inc(loaded["freq"], 16)
                sp.dma_start(posi[:, :], A["positions"].to_broadcast([P, S])).then_inc(loaded["pos"], 16)
                done_arena = [0]
                nxt = 0

                def stream(upto):
                    nonlocal nxt
                    while nxt < min(upto, len(chunks)):
                        c = chunks[nxt]
                        if nxt >= RAW:
                            o = chunks[nxt - RAW]
                            if "s" in o:
                                sp.wait_ge(*at("weights_low", o["s"]))
                            else:
                                sp.wait_ge(*at("weights_used", ("mod", o["r"])))
                        dst = raw[:, nxt % RAW, 0:c["kn"] * c["C"]].rearrange("p (k c) -> p k c", k=c["kn"])
                        sp.dma_start(dst, c["src"].rearrange("(k p) c -> p k c", p=P)).then_inc(landed[nxt % RAW], 16)
                        nxt += 1

                stream(RAW)
                for p in phases:
                    if p["kind"] == "linear":
                        last = p["groups"][-1][-1]
                        stream(last["r"] + 1 + RAW)
                    elif p["kind"] == "mod":
                        stream(max(c["r"] for c in chunks if c.get("job") is p) + 1 + RAW)
                    elif p["kind"] in ("final", "dump"):
                        sp.wait_ge(*at("turned_copied", (p["i"], 7)))
                        for t in range(2):
                            sp.dma_start(out[0].rearrange("(t p) d -> p t d", p=P)[:, t, :], xin[:, t, :]).then_inc(stored, 16)
                        sp.wait_ge(stored, 32)

        arena_loads = {}
        n_arena = [0]
        for p in phases:
            if p["kind"] == "rope" and p["what"] == "dil":
                p["loads"] = [(masks[:, :], A["const_masks"])]
            if p["kind"] == "rope" and p["what"] == "gqa":
                p["loads"] = [(ropeg[:, :, :], A["const_rope2"][:, 2 * S:].rearrange("p (j c) -> p j c", j=2))]
            if p["kind"] == "linear" and p["evac"] == "uq":
                p["loads"] = []
            if p["kind"] == "rope" and p["what"] == "mla":
                p["loads"] = [(ropem[:, :, :], A["const_rope2"][:, 0:2 * S].rearrange("p (j c) -> p j c", j=2))]
            if p["kind"] == "pool":
                p["loads"] = [(rcount[:, :, :], A["const_rcount"].rearrange("p (g c) -> p g c", g=4))]
            if p["kind"] == "ple":
                p["loads"] = [(pin[:, :, :], A["p"][p["l"], 0].rearrange("(t p) d -> p t d", p=P))]
            for _ in p.get("loads", ()):
                n_arena[0] += 1
            p["arena_value"] = 16 * n_arena[0]

        @block.gpsimd
        def _(pool):
            for p in phases:
                for dst, src in p.get("loads", ()):
                    for sem, value in ended(p["i"]):
                        pool.wait_ge(sem, value)
                    pool.dma_start(dst, src).then_inc(loaded["arena"], 16)

        @block.tensor
        def _(pe):
            def up(family, key=None):
                return C.sems[family], C.raised("tensor", family, key)


            def mm(out_, lhsT, rhs, start, stop):
                return pe.matmul(out_, lhsT, rhs, start=start, stop=stop, skip_group_check=True)

            def linear_pe(p):
                T = p["T"]
                for grp in p["groups"]:
                    for c in grp:
                        if c["first"] and c["gi"] >= 2:
                            pe.wait_ge(*at(group_sem[c["gi"] - 2], ("group", c["gi"] - 2)))
                        pe.wait_ge(*at("weights_low", c["s"]))
                        s = c["s"] % 2
                        A_ = acc(c, T)
                        if p["mode"] == "T":
                            tiles = [(j, j * p["m"], p["m"]) for j in range(c["C"] // p["m"])]
                            if c["C"] == 160:
                                tiles = [(0, 0, P), (1, 64, 96)]
                            if p["evac"] == "poolw":
                                tiles = [(0, 0, P)]
                            for j, c0, m in tiles:
                                for k in range(c["kn"]):
                                    kk = c["k"] + k
                                    w = [b[:, s, k * c["C"] + c0:k * c["C"] + c0 + m] for b in (whi, wlo)]
                                    x = [operand(p, kk, T, hi) for hi in (True, False)]
                                    st, en = c["first"] and k == 0, c["last"] and k == c["kn"] - 1
                                    o = A_[0:m, j, :]
                                    mm(o, w[0], x[0], st, False)
                                    mm(o, w[0], x[1], False, False)
                                    last = mm(o, w[1], x[0], False, en)
                        else:
                            nt = T // P
                            for t in range(nt):
                                b, col = (t, 0) if nt == 2 else (t // 2, (t % 2) * 256)
                                o = ps[:, (c["gi"] % 2) * 2 + b, col:col + 256]
                                for k in range(c["kn"]):
                                    kk = c["k"] + k
                                    w = [b_[:, s, k * 256:(k + 1) * 256] for b_ in (whi, wlo)]
                                    x = [operand(p, kk, T, hi)[:, t * P:(t + 1) * P] for hi in (True, False)]
                                    mm(o, x[0], w[0], k == 0, False)
                                    mm(o, x[0], w[1], False, False)
                                    last = mm(o, x[1], w[0], False, k == c["kn"] - 1)
                        last.then_inc(*up("weights_used", c["s"]))

            def pool_pe(p):
                c = p["groups"][0][0]
                pe.wait_ge(*at("weights_low", c["s"]))
                if c["gi"] >= 2:
                    pe.wait_ge(*at(group_sem[c["gi"] - 2], ("group", c["gi"] - 2)))
                pe.wait_ge(*at(group_sem[c["gi"] - 1], ("group", c["gi"] - 1)))
                s = c["s"] % 2
                for g in range(4):
                    w = [b[:, s, g * P:(g + 1) * P] for b in (whi, wlo)]
                    o = ps[:, g, :]
                    mm(o, w[0], uh[:, g, :], True, False)
                    mm(o, w[0], ul[:, g, :], False, False)
                    last = mm(o, w[1], uh[:, g, :], False, True)
                last.then_inc(*up("weights_used", c["s"]))

            for p in phases:
                kind, i = p["kind"], p["i"]
                for sem, value in ended(i):
                    pe.wait_ge(sem, value)
                if kind == "init":
                    pe.wait_ge(loaded["squares"], 16)
                    pe.wait_ge(loaded["rows"], 16 * 18)
                    for j in range(4):
                        n = (at_row, 88, 88, 96)[j]
                        last = pe.transpose(ps[:, 0, j * P:j * P + n], rows[0:n, j, :], ident[0:n, 0:n])
                    last.then_inc(*up("turned", "rows"))
                    pe.wait_ge(loaded["x"], 32)
                    for k in range(8):
                        if k >= 3:
                            pe.wait_ge(*at("turned_copied", ("x", k - 3)))
                        for t in range(4):
                            last = pe.transpose(ps[:, 1 + k % 3, t * P:(t + 1) * P], xin[:, t, k * P:(k + 1) * P], ident)
                        last.then_inc(*up("turned", ("x", k)))
                elif kind == "stats":
                    for k in range(p["n"]):
                        pe.wait_ge(*at("stat_squares", (i, k)))
                        mm(ps[:, 4, 0:p["T"]], ones, sq[:, k % 2, 0:p["T"]], k == 0, k == p["n"] - 1).then_inc(
                            *up("stat_summed", (i, k)))
                elif kind == "linear":
                    if p["evac"] == "poolw":
                        pool_pe(p)
                    else:
                        linear_pe(p)
                elif kind == "stick":
                    def z(hd):
                        o = (hd % 2) * 64
                        if hd >= 2:
                            pe.wait_ge(*at("stick_weights", (i, hd - 2)))
                        b = hd % 2
                        qh = q1[o:o + 64, hd // 2, :]
                        mm(ps[:, b, 0:256], k1[o:o + 64, hd // 2, 0:P], qh, True, False)
                        mm(ps[:, b, 256:384], k1[o:o + 64, hd // 2, P:S], qh[:, P:S], False, True).then_inc(
                            *up("scores", (i, hd)))

                    z(0)
                    for hd in range(HEADS):
                        if hd + 1 < HEADS:
                            z(hd + 1)
                        b = hd % 2
                        pe.wait_ge(*at("fail_ready", (i, hd)))
                        mm(ps[:, b, 0:256], negtri, sbf[:, b, 0:256], False, False)
                        mm(ps[:, b, 128:256], negones, sbf[:, b, 256:384], False, False)
                        mm(ps[:, b, 256:384], negtri, sbf[:, b, 256:384], False, True).then_inc(
                            *up("fail_summed", (i, hd)))
                        pe.wait_ge(*at("masked", (i, hd)))
                        pair, o = hd // 2, (hd % 2) * 64
                        if pair >= 2 and hd % 2 == 0:
                            pe.wait_ge(*at("operand_low", (i, pair - 2)))
                        dst = ps[o:o + 64, 6 + pair % 2, :]
                        vv = [v1[:, t, hd * 64:(hd + 1) * 64] for t in range(2)]
                        mm(dst[:, 0:256], vv[0], sba[:, b, 0:256], True, False)
                        mm(dst[:, 128:256], vv[1], sba[:, b, 256:384], False, True).then_inc(
                            *up("attended", (i, hd)))
                elif kind == "rope":
                    for t, (tile, perm, c_, s_, r) in enumerate(rope_tiles(p["what"])):
                        if t >= 2:
                            pe.wait_ge(*at("rotated", (i, t - 2)))
                        mm(ps[0:r, t % 2, 0:S], perm, tile, True, True).then_inc(*up("swapped", (i, t)))
                elif kind == "softmax":
                    units = softmax_units(p["what"])

                    def scores(u):
                        n = u["n"]
                        if n >= 2:
                            pe.wait_ge(*at("max_ready" if u["mask"] is not None else "weights_exp", (i, n - 2)))
                        for lhsT, rhs, col in u["prod"]:
                            width = rhs.shape[-1]
                            c0 = 0
                            while c0 < width:
                                w = min(width - c0, 512 - (col + c0) % 512)
                                bank = (n % 2) * 2 + (col + c0) // 512
                                last = mm(ps[:, bank, (col + c0) % 512:(col + c0) % 512 + w], lhsT, rhs[:, c0:c0 + w], True, True)
                                c0 += w
                        last.then_inc(*up("scores", (i, n)))

                    def turn_and_attend(u):
                        n = u["n"]
                        pe.wait_ge(*at("weights_normed", (i, n)))
                        if n >= 1:
                            pe.wait_ge(*at("turned_copied", (i, n - 1)))
                        kt = u["W"] // P
                        for k in range(kt):
                            last = pe.transpose(ps[:, 4 + k // 4, (k % 4) * P:(k % 4 + 1) * P], pr[:, n % 2, k * P:(k + 1) * P], ident)
                        last.then_inc(*up("turned", (i, n)))

                    def attend(u):
                        n = u["n"]
                        kt = u["W"] // P
                        pe.wait_ge(*at("turned_copied", (i, n)))
                        a, b = u["rows"]
                        if u["pair"] >= 2:
                            pe.wait_ge(*at("operand_low", (i, u["pair"] - 2)))
                        o = ps[a:b, 6 + u["pair"] % 2, u["q"] * P:(u["q"] + 1) * P]
                        for k in range(kt):
                            last = mm(o, u["vals"][k], pt[:, n % 2, k * P:(k + 1) * P], k == 0, k == kt - 1)
                        last.then_inc(*up("attended", (i, n)))

                    N = len(units)
                    for n in range(N + 2):
                        if n < N:
                            scores(units[n])
                        if 1 <= n <= N:
                            turn_and_attend(units[n - 1])
                        if n >= 2:
                            attend(units[n - 2])
                elif kind == "ple":
                    pe.wait_ge(loaded["arena"], p["arena_value"])
                    for k in range(2):
                        for t in range(2):
                            last = pe.transpose(ps[:, 4, k * S + t * P:k * S + (t + 1) * P], pin[:, t, k * P:(k + 1) * P], ident)
                    last.then_inc(*up("turned", (i, 0)))
                elif kind == "qknorm":
                    for k in range(10):
                        T = S if k < 8 else T2
                        pe.wait_ge(*at("stat_squares", (i, k)))
                        if k >= 1:
                            pe.wait_ge(*at("rstd_ready", (i, k - 1)))
                        mm(ps[:, 4, 0:T], ones, sq[:, k % 2, 0:T], True, True).then_inc(*up("stat_summed", (i, k)))
                elif kind == "mod":
                    for c in [c for c in chunks if c.get("job") is p]:
                        l, g, half = c["mod"]
                        n = l * 12 + g
                        pe.wait_ge(landed[c["r"] % RAW], 16 * (c["r"] // RAW + 1))
                        if half == 0 and n >= 1:
                            pe.wait_ge(*at("moved", (i, n - 1)))
                        for k in range(4):
                            last = mm(ps[0:2, 4, :], cc[:, half * 4 + k, :], raw[:, c["r"] % RAW, k * 512:(k + 1) * 512],
                                      half == 0 and k == 0, half == 1 and k == 3)
                        last.then_inc(*up("weights_used", ("mod", c["r"])))
                        if half == 1:
                            pe.wait_ge(*at("moved", (i, n)))
                            for j in range(4):
                                last = pe.transpose(ps[:, 5, (n * 4 + j) * 2:(n * 4 + j) * 2 + 2], modrow[:, j * P:(j + 1) * P], ident[0:2, 0:2])
                            last.then_inc(*up("turned", (i, n)))
                elif kind in ("final", "dump"):
                    for k in range(8):
                        if kind == "final":
                            pe.wait_ge(*at("normed", (i, k)))
                        src = y if kind == "final" else h
                        if k >= 3:
                            pe.wait_ge(*at("turned_copied", (i, k - 3)))
                        for t in range(2):
                            last = pe.transpose(ps[:, 1 + k % 3, t * P:(t + 1) * P], src[:, k, t * P:(t + 1) * P], ident)
                        last.then_inc(*up("turned", (i, k)))
                C.end("tensor", i)

        @block.scalar
        def _(act):
            def up(family, key=None):
                return C.sems[family], C.raised("scalar", family, key)

            def own():
                return C.sems[C.last["scalar"][0]], C.last["scalar"][1]


            def split_high(s):
                if not splits_in_turn(s, p):
                    return
                c = splits[s]
                n = c["kn"] * c["C"]
                act.wait_ge(landed[c["r"] % RAW], 16 * (c["r"] // RAW + 1))
                if s >= 2:
                    act.wait_ge(*at("weights_used", s - 2))
                act.wait_ge(*own())
                nc.scalar.activation(whi[:, s % 2, 0:n], raw[:, c["r"] % RAW, 0:n], ACT.Copy).then_inc(
                    *up("weights_high", s))

            def evac(p, grp):
                c = grp[0]
                T, kind, i, g = p["T"], p["evac"], p["i"], c["g"]
                key = ("group", c["gi"])
                A_ = acc(c, T)
                act.wait_ge(*at("weights_used", grp[-1]["s"]))
                if kind == "qk1":
                    dst = (q1 if g < 4 else k1)[:, (g % 4) * 2:(g % 4) * 2 + 2, :]
                    act.wait_ge(*own())
                    nc.scalar.activation(dst, A_, ACT.Copy, scale=HD ** -0.5 if g < 4 else 1.0).then_inc(
                        *up("group_read_s", key))
                elif kind == "qk2":
                    grp_no = int(p["name"][-1])
                    act.wait_ge(*own())
                    nc.scalar.activation(qk2[:, grp_no * 8 + g * 2:grp_no * 8 + g * 2 + 2, :], A_, ACT.Copy).then_inc(
                        *up("group_read_s", key))
                elif kind == "v":
                    nt = T // P
                    src = ps[:, (c["gi"] % 2) * 2:(c["gi"] % 2) * 2 + 2, 0:256 if nt == 2 else 512]
                    if nt == 4:
                        src = src.rearrange("p b (t c) -> p b t c", t=2)
                    name = p["name"]
                    if name == "stick_v":
                        dst = v1[:, :, g * 256:(g + 1) * 256]
                    elif name.startswith("dil_v"):
                        c0 = int(name[-1]) * 512 + g * 256
                        dst = v2[:, :, c0:c0 + 256]
                    elif name == "uv":
                        dst = vm[:, :, g * 256:(g + 1) * 256].rearrange("p (b t) c -> p b t c", b=2)
                    else:
                        dst = vg[:, :, :].rearrange("p (b t) c -> p b t c", b=2)
                    act.wait_ge(*own())
                    nc.scalar.activation(dst, src, ACT.Copy).then_inc(*up("group_read_s", key))
                elif kind == "relu2":
                    act.wait_ge(*own())
                    nc.scalar.activation(work[:, c["gi"] % 2, :, 0:S], A_, ACT.Relu).then_inc(*up("group_read_s", key))
                    act.wait_ge(*at("normed", ("sq", c["gi"])))
                    act.wait_ge(*own())
                    nc.scalar.activation(hh[:, 2 * g * S:2 * (g + 1) * S].rearrange("p (t c) -> p t c", t=2), y[:, 2 * (c["gi"] % 2):2 * (c["gi"] % 2) + 2, 0:S], ACT.Copy).then_inc(
                        *up("operand_high", (i, g)))
                elif kind == "gate":
                    if g >= 2:
                        act.wait_ge(*at("normed", ("gate", i, g - 2)))
                    act.wait_ge(*own())
                    nc.scalar.activation(ge[:, g % 2, :, :], A_, ACT.Exp, scale=-1.0).then_inc(*up("group_read_s", key))
                elif kind == "mixc":
                    if g < 2:
                        act.wait_ge(*own())
                        nc.scalar.activation(y[:, 2 * g:2 * g + 2, :], A_, ACT.Copy).then_inc(*up("group_read_s", key))
                    else:
                        act.wait_ge(*own())
                        nc.scalar.activation(y[:, 4, :], A_[:, 0, :], ACT.Copy).then_inc(*up("scalar_step"))
                        act.wait_ge(*own())
                        nc.scalar.activation(kr[0:96, :], A_[0:96, 1, :], ACT.Copy).then_inc(*up("group_read_s", key))
                elif kind == "mixp":
                    for j in range(2):
                        act.wait_ge(*own())
                        nc.scalar.activation(pbuf[:, 2 * g + j, :, PAD:PAD + S], A_[:, j, :].rearrange("p (s c) -> p s c", s=2), ACT.Copy).then_inc(
                            *up("group_read_s", key if j else None))
                elif kind == "uq":
                    act.wait_ge(*own())
                    nc.scalar.activation(qm[0:96, 2 * g:2 * g + 2, :], A_[0:96], ACT.Copy).then_inc(*up("group_read_s", key))
                elif kind == "uk":
                    for par in range(2):
                        act.wait_ge(*own())
                        nc.scalar.activation(km[0:64, 4 * g + par:4 * g + 4:2, :], A_[64 * par:64 * par + 64], ACT.Copy).then_inc(
                            *up("group_read_s", key if par else None))
                elif kind == "qg":
                    act.wait_ge(*own())
                    nc.scalar.activation(qg[:, 2 * g:2 * g + 2, :], A_, ACT.Copy).then_inc(*up("group_read_s", key))
                elif kind == "kg":
                    act.wait_ge(*own())
                    nc.scalar.activation(kg[:, :, :], A_, ACT.Copy).then_inc(*up("group_read_s", key))
                elif kind == "poolw":
                    for t in range(4):
                        act.wait_ge(*own())
                        nc.scalar.activation(uh[:, 4 + t, :], ps[:, t, :], ACT.Copy, scale=vec[:, ROW["pool_scale_2"] + t:ROW["pool_scale_2"] + t + 1]).then_inc(
                            *up("operand_high", (i, t)))
                elif kind == "conv" and g % 2 == 0:
                    l, f0 = p["l"], p["f0"]
                    for j in range(2):
                        f = f0 + g + j
                        if g >= 2:
                            act.wait_ge(*at("operand_low", (i, g - 1, j)))
                        act.wait_ge(*own())
                        nc.scalar.activation(cacc[:, j, 0:T], A_[:, j, :], ACT.Identity, bias=convv[:, l, 66 + f:67 + f], scale=convv[:, l, 22 + f:23 + f]).then_inc(
                            *up("moved", (i, g, j)))
                    for j in range(2):
                        act.wait_ge(*at("group_read_v", (i, g, j)))
                        act.wait_ge(*own())
                        nc.scalar.activation(csil[:, j, 0:T], cacc[:, j, 0:T], ACT.Silu).then_inc(
                            *up("stick_weights", (i, g, j)))
                elif kind == "conv":
                    for j in range(2):
                        act.wait_ge(*at("group_read_v", (i, g, j)))
                        act.wait_ge(*own())
                        nc.scalar.activation(hid(hh, g - 1 + j, T), csil[:, j, 0:T], ACT.Copy).then_inc(
                            *up("operand_high", (i, g, j)))

            nc.scalar.preload_act_table_set("natural_log_exp_and_others")
            for p in phases:
                kind, i = p["kind"], p["i"]
                for sem, value in ended(i):
                    act.wait_ge(sem, value)
                if kind == "init":
                    act.wait_ge(*at("turned", "rows"))
                    for n, dst in enumerate((vec[:, 0:at_row], convv[:, 0, 0:88], convv[:, 1, 0:88], bmod[:, 0:96])):
                        nc.scalar.activation(dst, ps[:, 0, n * P:n * P + (at_row, 88, 88, 96)[n]], ACT.Copy).then_inc(
                            *up("scalar_step"))
                    for k in range(8):
                        act.wait_ge(*at("turned", ("x", k)))
                        act.wait_ge(*own())
                        nc.scalar.activation(h[:, k, :], ps[:, 1 + k % 3, :], ACT.Copy).then_inc(
                            *up("turned_copied", ("x", k)))
                    act.wait_ge(*at("normed", "angles"))
                    act.wait_ge(*own())
                    nc.scalar.activation(sin1[:, :], turns[:, 0, :], ACT.Sin).then_inc(*up("scalar_step"))
                    act.wait_ge(*own())
                    nc.scalar.activation(cos1[:, :], turns[:, 1, :], ACT.Sin).then_inc(*up("scalar_step"))
                    nc.scalar.preload_act_table_set("natural_log_exp_and_others")
                    act.wait_ge(*own())
                    nc.scalar.activation(silu[:, 0, :], vec[:, ROW["c_2"]:ROW["c_2"] + 8], ACT.Exp, scale=-1.0).then_inc(
                        *up("scalar_step"))
                    act.wait_ge(*own())
                    nc.scalar.activation(silu[:, 1, :], vec[:, ROW["c_ctx_2"]:ROW["c_ctx_2"] + 8], ACT.Exp, scale=-1.0).then_inc(
                        *up("weights_exp", "cond"))
                    split_high(0)
                    split_high(1)
                elif kind == "stats":
                    src = h if p["src"] == "h" else y
                    s0 = p.get("s0", 0)
                    for k in range(p["n"]):
                        if k >= 2:
                            act.wait_ge(*at("stat_summed", (i, k - 2)))
                        act.wait_ge(*own())
                        nc.scalar.activation(sq[:, k % 2, 0:p["T"]], src[:, s0 + k, 0:p["T"]], ACT.Square).then_inc(
                            *up("stat_squares", (i, k)))
                    act.wait_ge(*at("stat_summed", (i, p["n"] - 1)))
                    act.wait_ge(*own())
                    nc.scalar.activation(lnv[:, 0:p["T"]], ps[:, 4, 0:p["T"]], ACT.Ln, scale=1.0 / p["D"], bias=small[:, 40:41]).then_inc(
                        *up("scalar_step"))
                    act.wait_ge(*own())
                    nc.scalar.activation(rstd[:, 0:p["T"]], lnv[:, 0:p["T"]], ACT.Exp, scale=-0.5).then_inc(
                        *up("rstd_ready", i))
                elif kind == "apply":
                    for k in range(p["n"]):
                        act.wait_ge(*at("normed", (i, k)))
                        dst = ch if p.get("dst") == "c" else uh
                        k_ = p.get("s0", 0) + k if p.get("dst") == "c" else k
                        act.wait_ge(*own())
                        nc.scalar.activation(dst[:, k_, 0:p["T"]], y[:, p.get("s0", 0) + k, 0:p["T"]], ACT.Copy).then_inc(
                            *up("operand_high", (i, k)))
                elif kind == "linear":
                    for grp in p["groups"]:
                        for c in grp:
                            split_high(c["s"] + 2)
                        evac(p, grp)
                elif kind == "stick":
                    def ex(hd):
                        b = hd % 2
                        act.wait_ge(*at("scores", (i, hd)))
                        act.wait_ge(*own())
                        nc.scalar.activation(sbt[:, b, :], ps[:, b, 0:384], ACT.Abs).then_inc(*up("scalar_step"))
                        act.wait_ge(*own())
                        nc.scalar.activation(sbe[:, b, :], sbt[:, b, :], ACT.Exp, scale=-1.0).then_inc(*up("scalar_step"))
                        if hd >= 2:
                            act.wait_ge(*at("fail_ready", (i, hd - 2)))
                        act.wait_ge(*own())
                        nc.scalar.activation(sbl[:, b, :], sbe[:, b, :], ACT.Ln, bias=1.0).then_inc(
                            *up("weights_exp", (i, hd)))

                    ex(0)
                    for hd in range(HEADS):
                        if hd + 1 < HEADS:
                            ex(hd + 1)
                        b = hd % 2
                        act.wait_ge(*at("fail_summed", (i, hd)))
                        if hd >= 2:
                            act.wait_ge(*at("attended", (i, hd - 2)))
                        act.wait_ge(*own())
                        nc.scalar.activation(sba[:, b, :], ps[:, b, 0:384], ACT.Exp).then_inc(*up("stick_weights", (i, hd)))
                        if hd % 2 == 1:
                            act.wait_ge(*at("attended", (i, hd)))
                            act.wait_ge(*own())
                            nc.scalar.activation(uh[:, hd // 2, 0:S], ps[:, 6 + (hd // 2) % 2, 0:S], ACT.Copy).then_inc(
                                *up("operand_high", (i, hd // 2)))
                elif kind == "softmax":
                    units = softmax_units(p["what"])
                    N = len(units)

                    def exp_(u):
                        n = u["n"]
                        act.wait_ge(*at("max_ready", (i, n)))
                        b = n % 2
                        W = u["W"]
                        if u["mask"] is not None:
                            src = sm[:, b, 0:W]
                        else:
                            src = ps[:, b * 2, 0:W]
                        if n >= 2:
                            act.wait_ge(*at("turned", (i, n - 2)))
                        act.wait_ge(*own())
                        nc.scalar.activation(pr[:, b, 0:W], src, ACT.Exp, scale=u["scale"], bias=small[:, b:b + 1], accum_out=small[:, 2 + b:3 + b]).then_inc(
                            *up("weights_exp", (i, n)))

                    def copy_(u):
                        n = u["n"]
                        W = u["W"]
                        act.wait_ge(*at("turned", (i, n)))
                        if n >= 2:
                            act.wait_ge(*at("attended", (i, n - 2)))
                        for c0 in range(0, W, 512):
                            w = min(512, W - c0)
                            act.wait_ge(*own())
                            nc.scalar.activation(pt[:, n % 2, c0:c0 + w], ps[:, 4 + c0 // 512, 0:w], ACT.Copy).then_inc(
                                *up("turned_copied", (i, n)))

                    def high_(u):
                        n = u["n"]
                        act.wait_ge(*at("attended", (i, n)))
                        t0 = u["col"] - u["q"] * P
                        act.wait_ge(*own())
                        nc.scalar.activation(uh[:, u["opair"], t0:t0 + S], ps[:, 6 + u["pair"] % 2, 0:S], ACT.Copy).then_inc(
                            *up("operand_high", (i, u["pair"])))

                    for n in range(N + 2):
                        if n < N:
                            exp_(units[n])
                        if 1 <= n <= N:
                            copy_(units[n - 1])
                        if n >= 2 and units[n - 2]["ends"]:
                            high_(units[n - 2])
                elif kind == "ple":
                    act.wait_ge(*at("turned", (i, 0)))
                    act.wait_ge(*own())
                    nc.scalar.activation(ph_[:, :, :], ps[:, 4, :].rearrange("p (k c) -> p k c", k=2), ACT.Copy).then_inc(
                        *up("operand_high", (i, 0)))
                    act.wait_ge(*at("operand_low", (i, 0)))
                elif kind == "pool":
                    act.wait_ge(*at("normed", (i, 0)))
                    act.wait_ge(*own())
                    nc.scalar.activation(uh[:, 0:4, :], pdif[:, :, :], ACT.Copy).then_inc(*up("operand_high", (i, 0)))
                elif kind == "qknorm":
                    for k in range(10):
                        T = S if k < 8 else T2
                        src = qg[:, k, :] if k < 8 else kg[:, k - 8, :]
                        if k >= 2:
                            act.wait_ge(*at("stat_summed", (i, k - 2)))
                        act.wait_ge(*own())
                        nc.scalar.activation(sq[:, k % 2, 0:T], src, ACT.Square).then_inc(*up("stat_squares", (i, k)))
                        act.wait_ge(*at("stat_summed", (i, k)))
                        act.wait_ge(*own())
                        nc.scalar.activation(lnv[:, 0:T], ps[:, 4, 0:T], ACT.Ln, scale=1.0 / P, bias=small[:, 40:41]).then_inc(
                            *up("scalar_step"))
                        if k >= 1:
                            act.wait_ge(*at("normed", (i, k - 1)))
                        act.wait_ge(*own())
                        nc.scalar.activation(rstd[:, 0:T], lnv[:, 0:T], ACT.Exp, scale=-0.5).then_inc(
                            *up("rstd_ready", (i, k)))
                elif kind == "mod":
                    for n in range(24):
                        act.wait_ge(*at("weights_used", ("mod", [c for c in chunks if c.get("mod") == (n // 12, n % 12, 1)][0]["r"])))
                        if n >= 1:
                            act.wait_ge(*at("turned", (i, n - 1)))
                        act.wait_ge(*own())
                        nc.scalar.activation(modrow[:, :], ps[0:2, 4, :], ACT.Copy).then_inc(*up("moved", (i, n)))
                    for s in mod_s:
                        split_high(s)
                elif kind in ("final", "dump"):
                    for k in range(8):
                        act.wait_ge(*at("turned", (i, k)))
                        act.wait_ge(*own())
                        nc.scalar.activation(xin[:, 0:2, k * P:(k + 1) * P], ps[:, 1 + k % 3, 0:S].rearrange("p (t c) -> p t c", t=2), ACT.Copy).then_inc(
                            *up("turned_copied", (i, k)))
                C.end("scalar", i)

        @block.vector
        def _(dve):
            def up(family, key=None):
                return C.sems[family], C.raised("vector", family, key)

            def own():
                return C.sems[C.last["vector"][0]], C.last["vector"][1]

            def split_low(s):
                if not splits_in_turn(s, p):
                    return
                c = splits[s]
                n = c["kn"] * c["C"]
                dve.wait_ge(*at("weights_high", s))
                dve.wait_ge(*own())
                nc.vector.tensor_tensor(wlo[:, s % 2, 0:n], raw[:, c["r"] % RAW, 0:n], whi[:, s % 2, 0:n].bitcast(F32), ALU.subtract).then_inc(
                    *up("weights_low", s))

            def evac(p, grp):
                c = grp[0]
                T, kind, i, g = p["T"], p["evac"], p["i"], c["g"]
                key = ("group", c["gi"])
                A_ = acc(c, T)
                if kind == "y":
                    dve.wait_ge(*at("weights_used", grp[-1]["s"]))
                    dve.wait_ge(*own())
                    nc.vector.tensor_copy(y[:, 2 * g:2 * g + 2, 0:T], A_).then_inc(*up("group_read_v", key))
                elif kind == "relu2":
                    dve.wait_ge(*at("group_read_s", key))
                    w = work[:, c["gi"] % 2, :, 0:S]
                    yy = y[:, 2 * (c["gi"] % 2):2 * (c["gi"] % 2) + 2, 0:S]
                    dve.wait_ge(*own())
                    nc.vector.tensor_tensor(yy, w, w, ALU.mult).then_inc(*up("normed", ("sq", c["gi"])))
                    dve.wait_ge(*at("operand_high", (i, g)))
                    v = lambda b: b[:, 2 * g * S:2 * (g + 1) * S].rearrange("p (t c) -> p t c", t=2)
                    dve.wait_ge(*own())
                    nc.vector.tensor_tensor(v(hl), yy, v(hh).bitcast(F32), ALU.subtract).then_inc(*up("operand_low", (i, g)))
                elif kind == "gate":
                    dve.wait_ge(*at("group_read_s", key))
                    gg = ge[:, g % 2, :, :]
                    dve.wait_ge(*own())
                    nc.vector.tensor_scalar(gg, gg, 1.0, None, ALU.add).then_inc(*up("vector_step"))
                    dve.wait_ge(*own())
                    nc.vector.reciprocal(y[:, 2 * g:2 * g + 2, 0:S], gg).then_inc(*up("normed", ("gate", i, g)))
                elif kind == "addgated":
                    dve.wait_ge(*at("weights_used", grp[-1]["s"]))
                    yy = y[:, 2 * g:2 * g + 2, 0:S]
                    dve.wait_ge(*own())
                    nc.vector.tensor_tensor(yy, A_, yy, ALU.mult).then_inc(*up("group_read_v", key))
                    hh_ = h[:, 2 * g:2 * g + 2, 0:S]
                    dve.wait_ge(*own())
                    nc.vector.tensor_tensor(hh_, hh_, yy, ALU.add).then_inc(*up("vector_step"))
                elif kind in ("gated", "gated2"):
                    dve.wait_ge(*at("weights_used", grp[-1]["s"]))
                    src = A_
                    if kind == "gated2":
                        src = y[:, 2 * g:2 * g + 2, 0:T]
                        dve.wait_ge(*own())
                        nc.vector.tensor_tensor(src, A_, src, ALU.add).then_inc(*up("vector_step"))
                    l, which = p["mod"]
                    for j in range(2):
                        for s_, sl in segs(T):
                            k = 2 * g + j
                            dve.wait_ge(*own())
                            nc.vector.scalar_tensor_tensor(h[:, k, sl], src[:, j, sl], mod_at(l, which, k, s_), h[:, k, sl], ALU.mult, ALU.add).then_inc(
                                *up("group_read_v", key))
                elif kind == "poolw":
                    for t in range(4):
                        dve.wait_ge(*at("operand_high", (i, t)))
                        sc = vec[:, ROW["pool_scale_2"] + t:ROW["pool_scale_2"] + t + 1]
                        dve.wait_ge(*own())
                        nc.vector.scalar_tensor_tensor(ul[:, 4 + t, :], ps[:, t, :], sc, uh[:, 4 + t, :].bitcast(F32), ALU.mult, ALU.subtract).then_inc(
                            *up("group_read_v", key))
                elif kind == "conv" and g % 2 == 0:
                    l, f0 = p["l"], p["f0"]
                    ns = T // S
                    for j in range(2):
                        f = f0 + g + j
                        dve.wait_ge(*at("moved", (i, g, j)))
                        a = cacc[:, j, 0:T].rearrange("p (s c) -> p s c", s=ns)
                        x = A_[:, j, :].rearrange("p (s c) -> p s c", s=ns)
                        dve.wait_ge(*own())
                        nc.vector.scalar_tensor_tensor(a[:, :, 1:S], x[:, :, 0:S - 1], convv[:, l, f:f + 1], a[:, :, 1:S], ALU.mult, ALU.add).then_inc(
                            *up("vector_step"))
                        dve.wait_ge(*own())
                        nc.vector.scalar_tensor_tensor(a[:, :, 0:S - 1], x[:, :, 1:S], convv[:, l, 44 + f:45 + f], a[:, :, 0:S - 1], ALU.mult, ALU.add).then_inc(
                            *up("group_read_v", (i, g, j)))
                    C.note("group_read_v", key)
                elif kind == "conv":
                    dve.wait_ge(*at("weights_used", grp[-1]["s"]))
                    for j in range(2):
                        dve.wait_ge(*at("stick_weights", (i, g - 1, j)))
                        dve.wait_ge(*own())
                        nc.vector.tensor_tensor(csil[:, j, 0:T], A_[:, j, :], csil[:, j, 0:T], ALU.mult).then_inc(
                            *up("group_read_v", (i, g, j)))
                    C.note("group_read_v", key)
                    for j in range(2):
                        dve.wait_ge(*at("operand_high", (i, g, j)))
                        dve.wait_ge(*own())
                        nc.vector.tensor_tensor(hid(hl, g - 1 + j, T), csil[:, j, 0:T], hid(hh, g - 1 + j, T).bitcast(F32), ALU.subtract).then_inc(
                            *up("operand_low", (i, g, j)))

            for p in phases:
                kind, i = p["kind"], p["i"]
                for sem, value in ended(i):
                    dve.wait_ge(sem, value)
                if kind == "init":
                    nc.vector.memset(small[:, :], EPS).then_inc(*up("vector_step"))
                    dve.wait_ge(loaded["pos"], 16)
                    dve.wait_ge(loaded["freq"], 16)
                    dve.wait_ge(*own())
                    nc.vector.tensor_copy(ang[:, :], posi[:, :]).then_inc(*up("vector_step"))
                    dve.wait_ge(*own())
                    nc.vector.tensor_scalar(ang[:, :], ang[:, :], freq[:, 0:1], None, ALU.mult).then_inc(*up("vector_step"))
                    magic = 12582912.0
                    c1 = 6.28125
                    c2 = float(np.float32(2 * np.pi - c1))
                    c3 = 2 * np.pi - c1 - c2
                    for n, off in enumerate((0.0, 0.25)):
                        t = turns[:, n, :]
                        dve.wait_ge(*own())
                        nc.vector.tensor_scalar(lnv[:, 0:S], ang[:, :], 1 / (2 * np.pi), off, ALU.mult, ALU.add).then_inc(
                            *up("vector_step"))
                        dve.wait_ge(*own())
                        nc.vector.tensor_scalar(lnv[:, 0:S], lnv[:, 0:S], magic, magic, ALU.add, ALU.subtract).then_inc(
                            *up("vector_step"))
                        dve.wait_ge(*own())
                        nc.vector.scalar_tensor_tensor(t, lnv[:, 0:S], -c1, ang[:, :], ALU.mult, ALU.add).then_inc(
                            *up("vector_step"))
                        dve.wait_ge(*own())
                        nc.vector.scalar_tensor_tensor(t, lnv[:, 0:S], -c2, t, ALU.mult, ALU.add).then_inc(
                            *up("vector_step"))
                        dve.wait_ge(*own())
                        nc.vector.scalar_tensor_tensor(t, lnv[:, 0:S], -c3, t, ALU.mult, ALU.add).then_inc(
                            *up("vector_step"))
                        dve.wait_ge(*own())
                        nc.vector.tensor_scalar(t, t, off * 2 * np.pi, 3.1415925, ALU.add, ALU.min).then_inc(
                            *up("vector_step"))
                        dve.wait_ge(*own())
                        nc.vector.tensor_scalar(t, t, -3.1415925, None, ALU.max).then_inc(*up("normed", "angles"))
                    dve.wait_ge(*at("weights_exp", "cond"))
                    dve.wait_ge(*own())
                    nc.vector.tensor_scalar(silu[:, :, :], silu[:, :, :], 1.0, None, ALU.add).then_inc(*up("vector_step"))
                    dve.wait_ge(*own())
                    nc.vector.reciprocal(silu[:, :, :], silu[:, :, :]).then_inc(*up("vector_step"))
                    for n, name in enumerate(("c_2", "c_ctx_2")):
                        dve.wait_ge(*own())
                        nc.vector.tensor_tensor(cc[:, :, n], vec[:, ROW[name]:ROW[name] + 8], silu[:, n, :], ALU.mult).then_inc(
                            *up("vector_step"))
                    dve.wait_ge(*at("turned_copied", ("x", 7)))
                    split_low(0)
                    split_low(1)
                elif kind == "apply":
                    T = p["T"]
                    src = h if p["src"] == "h" else y
                    s0 = p.get("s0", 0)
                    for k in range(p["n"]):
                        d = y[:, s0 + k, 0:T]
                        if "gain" in p:
                            dve.wait_ge(*own())
                            nc.vector.scalar_tensor_tensor(d, src[:, s0 + k, 0:T], gain(p, k), rstd[:, 0:T], ALU.mult, ALU.mult).then_inc(
                                *up("normed", (i, k)))
                        else:
                            l, which = p["mod"]
                            for s_, sl in segs(T):
                                dve.wait_ge(*own())
                                nc.vector.scalar_tensor_tensor(y[:, k, sl], h[:, k, sl], mod_at(l, which + 1, k, s_), rstd[:, sl], ALU.mult, ALU.mult).then_inc(
                                    *up("vector_step"))
                            for s_, sl in segs(T):
                                dve.wait_ge(*own())
                                nc.vector.tensor_scalar(y[:, k, sl], y[:, k, sl], mod_at(l, which, k, s_), None, ALU.add).then_inc(
                                    *up("normed", (i, k)))
                    for k in range(p["n"]):
                        c = p.get("dst") == "c"
                        k_ = s0 + k if c else k
                        dve.wait_ge(*at("operand_high", (i, k)))
                        dve.wait_ge(*own())
                        nc.vector.tensor_tensor((cl if c else ul)[:, k_, 0:T], y[:, s0 + k, 0:T], (ch if c else uh)[:, k_, 0:T].bitcast(F32), ALU.subtract).then_inc(
                            *up("operand_low", (i, k)))
                elif kind == "residual":
                    for k in range(8):
                        dve.wait_ge(*own())
                        nc.vector.scalar_tensor_tensor(y[:, k, 0:S], y[:, k, 0:S], gain(p, k), rstd[:, 0:S], ALU.mult, ALU.mult).then_inc(
                            *up("vector_step"))
                    for k in range(8):
                        dve.wait_ge(*own())
                        nc.vector.tensor_tensor(h[:, k, 0:S], h[:, k, 0:S], y[:, k, 0:S], ALU.add).then_inc(
                            *up("vector_step"))
                elif kind == "linear":
                    for grp in p["groups"]:
                        for c in grp:
                            split_low(c["s"] + 2)
                        evac(p, grp)
                elif kind == "stick":
                    for hd in range(HEADS):
                        b = hd % 2
                        dve.wait_ge(*at("weights_exp", (i, hd)))
                        if hd >= 2:
                            dve.wait_ge(*at("fail_summed", (i, hd - 2)))
                        dve.wait_ge(*own())
                        nc.vector.scalar_tensor_tensor(sbf[:, b, :], ps[:, b, 0:384], 0.0, sbl[:, b, :], ALU.max, ALU.add).then_inc(
                            *up("vector_step"))
                        for c0 in (0, 256):
                            dve.wait_ge(*own())
                            nc.vector.tensor_tensor(sbf[:, b, c0:c0 + P], sbf[:, b, c0:c0 + P], past, ALU.mult).then_inc(
                                *up("fail_ready", (i, hd)))
                        dve.wait_ge(*at("stick_weights", (i, hd)))
                        for c0 in (0, 256):
                            dve.wait_ge(*own())
                            nc.vector.scalar_tensor_tensor(sba[:, b, c0:c0 + P], sba[:, b, c0:c0 + P], 1.0, past, ALU.min, ALU.mult).then_inc(
                                *up("masked", (i, hd)))
                        if hd % 2 == 1:
                            pair = hd // 2
                            dve.wait_ge(*at("operand_high", (i, pair)))
                            dve.wait_ge(*own())
                            nc.vector.tensor_tensor(ul[:, pair, 0:S], ps[:, 6 + pair % 2, 0:S], uh[:, pair, 0:S].bitcast(F32), ALU.subtract).then_inc(
                                *up("operand_low", (i, pair)))
                elif kind == "rope":
                    dve.wait_ge(loaded["arena"], p["arena_value"])
                    for t, (tile, perm, c_, s_, r) in enumerate(rope_tiles(p["what"])):
                        dve.wait_ge(*at("swapped", (i, t)))
                        tmp = work[0:r, 0, 0, 0:S]
                        dve.wait_ge(*own())
                        nc.vector.tensor_tensor(tmp, ps[0:r, t % 2, 0:S], s_, ALU.mult).then_inc(*up("vector_step"))
                        dve.wait_ge(*own())
                        nc.vector.tensor_tensor(tile, tile, c_, ALU.mult).then_inc(*up("vector_step"))
                        dve.wait_ge(*own())
                        nc.vector.tensor_tensor(tile, tile, tmp, ALU.add).then_inc(*up("rotated", (i, t)))
                    if p["what"] == "mla":
                        src = kr[64:96, :]
                        for hd in range(8):
                            dve.wait_ge(*own())
                            nc.vector.tensor_copy(km[64:96, hd, :], src).then_inc(*up("vector_step"))
                elif kind == "softmax":
                    units = softmax_units(p["what"])
                    N = len(units)

                    def max_(u):
                        n, W, b = u["n"], u["W"], u["n"] % 2
                        dve.wait_ge(*at("scores", (i, n)))
                        if n >= 2:
                            dve.wait_ge(*at("weights_exp", (i, n - 2)))
                        if u["mask"] is not None:
                            for c0 in range(0, W, 512):
                                w = min(512, W - c0)
                                dve.wait_ge(*own())
                                nc.vector.tensor_tensor(sm[:, b, c0:c0 + w], ps[:, b * 2 + c0 // 512, 0:w], masks[:, u["mask"] + c0:u["mask"] + c0 + w], ALU.add).then_inc(
                                    *up("vector_step"))
                            src = sm[:, b, 0:W]
                        else:
                            src = ps[:, b * 2, 0:W]
                        dve.wait_ge(*own())
                        nc.vector.tensor_reduce(small[:, 4 + b:5 + b], src, AX.X, ALU.max).then_inc(*up("vector_step"))
                        dve.wait_ge(*own())
                        nc.vector.tensor_scalar(small[:, b:b + 1], small[:, 4 + b:5 + b], -u["scale"], None, ALU.mult).then_inc(
                            *up("max_ready", (i, n)))

                    def norm_(u):
                        n, W, b = u["n"], u["W"], u["n"] % 2
                        dve.wait_ge(*at("weights_exp", (i, n)))
                        dve.wait_ge(*own())
                        nc.vector.reciprocal(small[:, 6 + b:7 + b], small[:, 2 + b:3 + b]).then_inc(*up("vector_step"))
                        dve.wait_ge(*own())
                        nc.vector.tensor_scalar(pr[:, b, 0:W], pr[:, b, 0:W], small[:, 6 + b:7 + b], None, ALU.mult).then_inc(
                            *up("weights_normed", (i, n)))

                    def low_(u):
                        t0 = u["col"] - u["q"] * P
                        dve.wait_ge(*at("operand_high", (i, u["pair"])))
                        dve.wait_ge(*own())
                        nc.vector.tensor_tensor(ul[:, u["opair"], t0:t0 + S], ps[:, 6 + u["pair"] % 2, 0:S], uh[:, u["opair"], t0:t0 + S].bitcast(F32), ALU.subtract).then_inc(
                            *up("operand_low", (i, u["pair"])))

                    for n in range(N + 2):
                        if n < N:
                            max_(units[n])
                        if 1 <= n <= N:
                            norm_(units[n - 1])
                        if n >= 2 and units[n - 2]["ends"]:
                            low_(units[n - 2])
                elif kind == "ple":
                    dve.wait_ge(*at("operand_high", (i, 0)))
                    dve.wait_ge(*own())
                    nc.vector.tensor_tensor(pl_[:, :, :], ps[:, 4, :].rearrange("p (k c) -> p k c", k=2), ph_[:, :, :].bitcast(F32), ALU.subtract).then_inc(
                        *up("operand_low", (i, 0)))
                elif kind == "pool":
                    dve.wait_ge(loaded["arena"], p["arena_value"])
                    L = S + 2 * PAD
                    dve.wait_ge(*own())
                    nc.vector.memset(pbuf[:, :, :, 0:PAD], 0.0).then_inc(*up("vector_step"))
                    dve.wait_ge(*own())
                    nc.vector.memset(pbuf[:, :, :, PAD + S:L], 0.0).then_inc(*up("vector_step"))
                    dve.wait_ge(*own())
                    nc.vector.tensor_tensor(abuf[:, :, :, 0:L - 1], pbuf[:, :, :, 0:L - 1], pbuf[:, :, :, 1:L], ALU.add).then_inc(
                        *up("vector_step"))
                    for n, w in enumerate((2, 4, 8)):
                        end = L - 2 * w + 1
                        dve.wait_ge(*own())
                        nc.vector.tensor_tensor(abuf[:, n + 1:4, :, 0:end], abuf[:, n + 1:4, :, 0:end], abuf[:, n + 1:4, :, w:w + end], ALU.add).then_inc(
                            *up("vector_step"))
                    for g, w in enumerate(POOL_W):
                        for s_, sl in segs(T2):
                            a = abuf[:, g, s_, PAD - w // 2:PAD - w // 2 + S]
                            dve.wait_ge(*own())
                            nc.vector.tensor_tensor(a, a, rcount[:, g, :], ALU.mult).then_inc(*up("vector_step"))
                            dve.wait_ge(*own())
                            nc.vector.tensor_tensor(pdif[:, g, sl], a, pbuf[:, g, s_, PAD:PAD + S], ALU.subtract).then_inc(
                                *up("normed", (i, 0)))
                    dve.wait_ge(*at("operand_high", (i, 0)))
                    dve.wait_ge(*own())
                    nc.vector.tensor_tensor(ul[:, 0:4, :], pdif[:, :, :], uh[:, 0:4, :].bitcast(F32), ALU.subtract).then_inc(
                        *up("operand_low", (i, 0)))
                elif kind == "qknorm":
                    for k in range(10):
                        T = S if k < 8 else T2
                        t = qg[:, k, :] if k < 8 else kg[:, k - 8, :]
                        g = ROW["gqa_g_q" if k < 8 else "gqa_g_k"]
                        dve.wait_ge(*at("rstd_ready", (i, k)))
                        dve.wait_ge(*own())
                        nc.vector.scalar_tensor_tensor(t, t, vec[:, g:g + 1], rstd[:, 0:T], ALU.mult, ALU.mult).then_inc(
                            *up("normed", (i, k)))
                elif kind == "mod":
                    dve.wait_ge(*at("turned", (i, 23)))
                    for s_ in range(2):
                        for l in range(2):
                            dve.wait_ge(*own())
                            nc.vector.tensor_tensor(modc[:, l, :, s_], ps[:, 5, l * 96:(l + 1) * 96].rearrange("p (c s) -> p s c", s=2)[:, s_, :], bmod[:, l * 48:(l + 1) * 48], ALU.add).then_inc(
                                *up("vector_step"))
                    for l in range(2):
                        for which in (1, 4):
                            m = modc[:, l, which * 8:which * 8 + 8, :]
                            dve.wait_ge(*own())
                            nc.vector.tensor_scalar(m, m, 1.0, None, ALU.add).then_inc(*up("vector_step"))
                    for s in mod_s:
                        split_low(s)
                elif kind == "final":
                    for k in range(8):
                        c = ROW["g_final_2"] + k
                        dve.wait_ge(*own())
                        nc.vector.scalar_tensor_tensor(y[:, k, 0:S], h[:, k, 0:S], vec[:, c:c + 1], rstd[:, 0:S], ALU.mult, ALU.mult).then_inc(
                            *up("normed", (i, k)))
                C.end("vector", i)
    return C


def kernel(**inputs):
    import concourse.bacc as bacc
    from concourse.bass_utils import run_bass_kernel_spmd as run

    skip = {"w_in_dsa", "w_out_dsa", "w_in_moba", "w_out_moba"}
    arrays = {n: np.ascontiguousarray(a) for n, a in inputs.items() if n not in skip}
    arrays.update(constants())

    def program(noted):
        nc = bacc.Bacc("TRN2", target_bir_lowering=False, num_devices=1, dynamic_dma_scratch_size=8192)
        A = {n: nc.dram_tensor("in_" + n, a.shape, mybir.dt.from_np(a.dtype), kind="ExternalInput").ap()
             for n, a in arrays.items()}
        out = nc.dram_tensor("out", (1, S, D), F32, kind="ExternalOutput").ap()
        return nc, build(nc, A, out, noted, STOP)

    noted = program(None)[1].seen
    nc, _ = program(noted)
    r = run(nc, [{"in_" + n: a for n, a in arrays.items()}], core_ids=[0])
    return r.results[0]["out"]
```

```python
from contextlib import ExitStack

import concourse.bass as bass
import numpy as np
from concourse import mybir

F32 = mybir.dt.float32
F32R = mybir.dt.float32r
I32 = mybir.dt.int32
ALU = mybir.AluOpType
ACT = mybir.ActivationFunctionType
AX = mybir.AxisListType

P = 128
D = 1024
S = 256
T2 = 2 * S
KD = D // P
EPS = 1e-6
DFF = 4096
DFF2 = 2816
KF2 = DFF2 // P
HEADS, HD = 16, 64
DIL = (1, 4, 16)
DIL_BACK = 128
MLA_HEADS, MLA_NOPE, MLA_ROPE = 8, 64, 32
MLA_HD = MLA_NOPE + MLA_ROPE
GQA_HEADS, GQA_KV = 8, 2
POOL_W = (2, 4, 8, 16)
PAD = 16
SLOT = 2048
RAW = 3
SPLIT = 3
NEG = -1.0e30
STOP = None


def constants():
    i = np.arange(P)
    ident = np.eye(P)
    ones = np.ones((P, P))
    negtri = -(i[:, None] >= i[None, :]).astype(float)
    perm1 = np.zeros((P, P))
    for base in (0, 64):
        for j in range(8):
            perm1[base + j + 8, base + j] = -1.0
            perm1[base + j, base + j + 8] = 1.0
    perm_g = np.zeros((P, P))
    for j in range(0, P, 2):
        perm_g[j + 1, j] = -1.0
        perm_g[j, j + 1] = 1.0
    perm_m = np.zeros((P, P))
    perm_m[MLA_NOPE:MLA_HD, MLA_NOPE:MLA_HD] = perm_g[:MLA_ROPE, :MLA_ROPE]
    past = (i[:, None] < i[None, :]).astype(float)
    select = np.zeros((P, P))
    for q in range(4):
        select[32 * q, 0] = select[32 * q + 1, 1] = 1.0
    squares = np.concatenate([ident, ones, negtri, -ones, perm1, perm_m, perm_g, past, select], axis=1)

    freq = np.zeros((P, 1))
    for base in (0, 64):
        freq[base:base + 16, 0] = 500000.0 ** (-np.tile(np.arange(8), 2) / 8.0)

    def axial(dim):
        t = np.arange(S)
        f = 10000.0 ** (-np.arange(dim // 4) / (dim // 4))
        ang = np.concatenate([(t // 64)[:, None] * f, (t % 64)[:, None] * f], axis=-1)
        return np.repeat(np.cos(ang).T, 2, axis=0), np.repeat(np.sin(ang).T, 2, axis=0)

    cm, sm = np.ones((P, S)), np.zeros((P, S))
    cm[MLA_NOPE:MLA_HD], sm[MLA_NOPE:MLA_HD] = axial(MLA_ROPE)
    cg, sg = axial(P)
    t = np.arange(S)
    count = [np.clip(t - w // 2 + w, 0, S) - np.clip(t - w // 2, 0, S) for w in POOL_W]
    rcount = np.broadcast_to((1.0 / np.stack(count)).reshape(1, -1), (P, 4 * S))
    def band(q0, nk):
        q = q0 + i[:, None]
        k = np.arange(nk)[None, :]
        return [np.where((k <= q) & ((q - k) % d == 0) & (q - k <= DIL_BACK * d), 0.0, NEG) for d in DIL]
    masks = np.concatenate(band(0, P) + band(P, 2 * P), axis=1)
    rope2 = np.concatenate([cm, sm, cg, sg], axis=1)
    return {k: np.ascontiguousarray(v, dtype=np.float32) for k, v in dict(
        const_squares=squares, const_freq=freq, const_rope2=rope2, const_rcount=rcount, const_masks=masks).items()}


class Counting:

    def __init__(self, noted):
        self.noted, self.seen, self.count, self.engine, self.sems = noted, {}, {}, {}, {}
        self.last = {}

    def raised(self, engine, family, key=None, by=1):
        assert self.engine.setdefault(family, engine) == engine, family
        self.count[family] = self.count.get(family, 0) + by
        self.seen[family, key] = self.count[family]
        self.last[engine] = (family, self.count[family])
        return by

    def note(self, family, key):
        self.seen[family, key] = self.count[family]

    def end(self, engine, i):
        self.seen["end", (engine, i)] = self.last.get(engine)

    def after(self, family, key=None):
        return self.noted[family, key] if self.noted else 1

    def after_phase(self, engine, i):
        last = self.noted["end", (engine, i)] if self.noted else None
        return (self.sems[last[0]], last[1]) if last else None


FAMILIES = """weights_high weights_low weights_used small_loaded const_loaded scalar_step vector_step tensor_step
 group_read_s group_read_v operand_high operand_low stat_squares stat_summed rstd_ready
 normed moved rotated swapped scores weights_exp weights_normed turned turned_copied attended
 max_ready fail_ready fail_summed stick_weights masked mod_rows mod_turned mod_kept gated_silu tiles_ready""".split()


def build(nc, A, out, noted, dry_stop=None):
    C = Counting(noted)
    with ExitStack() as ctx:
        for f in FAMILIES:
            C.sems[f] = ctx.enter_context(nc.semaphore(f))
        landed = [ctx.enter_context(nc.semaphore(f"landed{i}")) for i in range(RAW)]
        loaded = {n: ctx.enter_context(nc.semaphore(f"loaded_{n}")) for n in ("squares", "rows", "freq", "pos", "x", "arena", "p")}
        stored = ctx.enter_context(nc.semaphore("stored"))

        def sb(name, shape, dt=F32):
            return ctx.enter_context(nc.sbuf_tensor(name, shape, dt))

        HH0 = -(-nc.sbuf_base // 32) * 32
        hh = sb("hh", [P, 8192], F32R)
        hl = sb("hl", [P, 8192], F32R)
        raw = sb("raw", [P, RAW, SLOT])
        whi = sb("whi", [P, SPLIT, SLOT], F32R)
        wlo = sb("wlo", [P, SPLIT, SLOT], F32R)
        h = sb("h", [P, KD, T2])
        uh = sb("uh", [P, KD, T2], F32R)
        ul = sb("ul", [P, KD, T2], F32R)
        y = sb("y", [P, KD, T2])
        squares = sb("squares", [P, 9, P])
        sq = sb("sq", [P, 2, T2])
        lnv = sb("lnv", [P, T2])
        rstd = sb("rstd", [P, T2])
        cos1 = sb("cos1", [P, S])
        sin1 = sb("sin1", [P, S])
        freq = sb("freq", [P, 1])
        vec = sb("vec", [P, P])
        convv = sb("convv", [P, 2, 96])
        bmod = sb("bmod", [P, 96])
        modc = sb("modc", [P, 2, 48, 2])
        silu = sb("silu", [P, 2, KD])
        cc = sb("cc", [P, KD, 2])
        small = sb("small", [P, 64])
        ident, ones, negtri, negones, perm1, perm_m, perm_g, past, select = (squares[:, j, :] for j in range(9))
        select = select[:, 0:2]
        ps = ctx.enter_context(nc.psum_tensor("ps", [P, 8, 512], F32))


        def arena(name, shape, off, dt=F32):
            n = int(np.prod(shape[1:])) * 4
            assert off + n <= 65536, (name, off + n)
            return nc.alloc_sbuf_tensor_at(name, shape, dt, offset=HH0 + off)

        K = 1024
        rows = arena("rows", [P, 4, P], 0)
        xin = arena("xin", [P, 4, D], 4 * K)
        posi = arena("posi", [P, S], 20 * K, I32)
        ang = arena("ang", [P, S], 21 * K)
        turns = arena("turns", [P, 2, S], 22 * K)
        q1 = arena("q1", [P, 8, S], 0)
        k1 = arena("k1", [P, 8, S], 8 * K)
        v1 = arena("v1", [P, 2, D], 16 * K)
        sbt = arena("sbt", [P, 2, 384], 24 * K)
        sbe = arena("sbe", [P, 2, 384], 27 * K)
        sbl = arena("sbl", [P, 2, 384], 30 * K)
        sbf = arena("sbf", [P, 2, 384], 33 * K)
        sba = arena("sba", [P, 2, 384], 36 * K)
        qk2 = arena("qk2", [P, 24, S], 0)
        v2 = arena("v2", [P, 2, 3 * 512], 24 * K)
        masks = arena("masks", [P, 1152], 36 * K)
        sm = arena("sm", [P, 2, 768], 41 * K)
        pr = arena("pr", [P, 2, 768], 47 * K)
        pt = arena("pt", [P, 2, 768], 53 * K)
        rtmp = arena("rtmp", [P, 2, S], 59 * K)
        pbuf = arena("pbuf", [P, 4, 2, S + 2 * PAD], 0)
        abuf = arena("abuf", [P, 4, 2, S + 2 * PAD], 10 * K)
        rcount = arena("rcount", [P, 4, S], 20 * K)
        pdif = arena("pdif", [P, 4, T2], 24 * K)
        qm = arena("qm", [P, 8, T2], 0)
        km = arena("km", [P, 8, T2], 16 * K)
        vm = arena("vm", [P, 4, 512], 32 * K)
        kr = arena("kr", [P, T2], 62 * K)
        ropem = arena("ropem", [P, 2, S], 40 * K)
        ch = arena("ch", [P, 5, T2], 42 * K, F32R)
        cl = arena("cl", [P, 5, T2], 52 * K, F32R)
        qg = arena("qg", [P, 8, S], 0)
        kg = arena("kg", [P, 2, T2], 8 * K)
        vg = arena("vg", [P, 4, S], 12 * K)
        ropeg = arena("ropeg", [P, 2, S], 16 * K)
        pin = arena("pin", [P, 2, S], 0)
        ph_ = arena("ph", [P, 2, S], 2 * K, F32R)
        pl_ = arena("pl", [P, 2, S], 4 * K, F32R)
        pt32 = arena("pt32", [P, 2, S], 6 * K)
        ge = arena("ge", [P, 2, 2, S], 8 * K)
        work = sb("work", [P, 2, 2, S])
        modrow = lnv[:, :]
        cacc = arena("cacc", [P, 2, 512], 24 * K)
        csil = arena("csil", [P, 2, 512], 28 * K)

        def hid(buf, t, T):
            return buf[:, t * T:(t + 1) * T]

        chunks = []
        phases = []

        def linear(name, W, nk, cols, T, kind, mode="T", m=P, xin=("u", 0), kmax=8, tok0=0, k0=0, split=True, last=None):
            job = dict(kind="linear", name=name, evac=kind, T=T, mode=mode, m=m, x=xin, tok0=tok0, groups=[])
            for g, (c0, nc_) in enumerate(cols):
                grp = []
                nparts = -(-nk // kmax)
                sizes = [nk // nparts + (1 if i < nk % nparts else 0) for i in range(nparts)]
                a = 0
                for kn in sizes:
                    ck = dict(job=job, g=g, k=a, kn=kn, C=nc_, src=W[(k0 + a) * P:(k0 + a + kn) * P, c0:c0 + nc_],
                              r=len(chunks), first=a == 0, last=a + kn == nk)
                    assert kn * nc_ <= SLOT
                    chunks.append(ck)
                    grp.append(ck)
                    a += kn
                job["groups"].append(grp)
            phases.append(job)
            return job

        def phase(kind, **kw):
            phases.append(dict(kind=kind, **kw))

        def pairs(c0, n, w=256):
            return [(c0 + j, w) for j in range(0, n, w)]

        ROWS_G = {}
        row_list = []

        def rows_of(name, ap, n):
            ROWS_G[name] = len(row_list)
            for j in range(n):
                row_list.append((ap, j))

        phase("init")
        lay = 0
        for l in range(2):
            if l == 0:
                phase("stats", src="h", n=8, T=S, D=D)
            phase("apply", src="h", n=8, T=S, gain=("g_mix_pre", l))
            if l == 0:
                Wi = A["w_in_sb"][0]
                linear("stick_qk", Wi, 8, pairs(0, 2 * D), S, "qk1")
                linear("stick_v", Wi, 8, pairs(2 * D, D), S, "v", mode="V")
                phase("stick", n_mods=7)
                linear("stick_out", A["w_out_sb"][0], 8, pairs(0, D), S, "y")
            else:
                Wi = A["w_in_dil"][0]
                for g in range(3):
                    linear(f"dil_qk{g}", Wi, 8, pairs(g * 1536, 1024), S, "qk2")
                    linear(f"dil_v{g}", Wi, 8, pairs(g * 1536 + 1024, 512), S, "v", mode="V")
                phase("softmax", what="dil")
                linear("dil_out", A["w_out_dil"][0], 4, pairs(0, D), S, "y")
            phases[-1].update(stat="y")
            phase("join", T=S, stat="h", gain=("g_mix_post", l))
            phase("apply", src="h", n=8, T=S, gain=("g_ffn_pre", l))
            linear(f"ff_in{l}", A["w_ff_in"][l], 8, pairs(0, DFF), S, "relu2")
            linear(f"ff_out{l}", A["w_ff_out"][l], 32, pairs(0, D), S, "y", xin=("h", 0))
            phases[-1].update(stat="y")
            phase("join", T=S, stat="h", gain=("g_ffn_post", l))
            phase("apply", src="h", n=8, T=S, gain=("g_ple", l))
            linear(f"gate{l}", A["w_ple_gate"][l], 8, pairs(0, D), S, "gate")
            phase("ple", l=l)
            linear(f"ple{l}", A["w_ple"][l], 2, pairs(0, D), S, "addgated", xin=("p", 0))
            phases[-1].update(stat="h")
        for l in range(2):
            Tt = T2 if l == 0 else S
            if l == 0:
                phase("stats", src="h", n=8, T=T2, D=D)
            phase("apply", src="h", n=8, T=T2, mod=(l, 0))
            if l == 0:
                Wi = A["mix0_w_in_2"][0]
                linear("mix_c", Wi, 8, [(0, 256), (256, 256), (512, 160)], T2, "mixc")
                linear("mix_p", Wi, 8, pairs(672, 512), T2, "mixp")
                phase("pool")
                linear("pool_w", A["pool_w_2"][0].rearrange("g i o -> (g i) o"), 4, [(0, P)], T2, "poolw", xin=("u", 0))
                for src0, n, dd, g in ((0, 3, 384, "mla_g_q"), (3, 2, 256, "mla_g_kv")):
                    phase("stats", src="y", s0=src0, n=n, T=T2, D=dd)
                    phase("apply", src="y", s0=src0, n=n, T=T2, gain=(g, 0), dst="c")
                linear("uq", A["mla_w_uq_2"][0], 3, pairs(0, 768, 192), T2, "uq", m=96, xin=("c", 0))
                linear("uk", A["mla_w_uk_2"][0], 2, pairs(0, 512), T2, "uk", xin=("c", 3))
                linear("uv", A["mla_w_uv_2"][0], 2, pairs(0, 512), T2, "v", mode="V", xin=("c", 3))
                phase("rope", what="mla")
                phase("softmax", what="mla")
                linear("mix_out", A["mix0_w_out_2"][0], 8, pairs(0, D), T2, "gated", last=(0, 2))
                phases[-1].update(mod=(0, 2), stat="h")
            else:
                Wi = A["gqa_w_in_2"][0]
                linear("gqa_q", Wi, 8, pairs(0, D), S, "qg")
                linear("gqa_k", Wi, 8, pairs(D, 256), T2, "kg")
                linear("gqa_v", Wi, 8, pairs(D + 256, 256), T2, "v", mode="V")
                phase("qknorm")
                phase("rope", what="gqa")
                phase("softmax", what="gqa")
                linear("gqa_out", A["gqa_w_out_2"][0], 8, pairs(0, D), S, "gated")
                phases[-1].update(mod=(1, 2), stat="h")
            phase("apply", src="h", n=8, T=Tt, mod=(l, 3))
            Wu, Wd = A["ffn_w_up_2"][l], A["ffn_w_down_2"][l]
            halves = [(0, 12), (12, 10)] if l == 0 else [(0, 22)]
            for n, (f0, nf) in enumerate(halves):
                cols = [c for j in range(nf // 2) for c in ((f0 * P + j * 256, 256), (DFF2 + f0 * P + j * 256, 256))]
                linear(f"up{l}{n}", Wu, 8, cols, Tt, "conv")
                phases[-1].update(l=l, f0=f0)
                only = "gated" if len(halves) == 1 else ("y" if n == 0 else "gated2")
                linear(f"down{l}{n}", Wd, nf, pairs(0, D), Tt, only, xin=("h", 0), k0=f0)
                phases[-1]["mod"] = (l, 5)
            phases[-1]["stat"] = "h"
        phase("final")
        if dry_stop is not None:
            phases[:] = phases[:dry_stop]
            live = {id(p) for p in phases}
            chunks[:] = [c for c in chunks if id(c["job"]) in live]
            phase("dump")
        for i, p in enumerate(phases):
            p["i"] = i
        mod_after = dict(stick_qk=(4,), ff_in0=(2, 7, 12), ff_out0=(0, 1, 2), gate0=(1,), dil_qk0=(1,), dil_qk1=(1,),
                         dil_qk2=(1,), ff_in1=(2, 7, 12), ff_out1=(0, 1, 2))
        own_chunks, behind, mod_n = [], {}, 0
        for p in phases:
            p["mods"] = {}
            places = range(p["n_mods"]) if "n_mods" in p else mod_after.get(p.get("name"), ())
            for g, grp in enumerate(p.get("groups", [()])):
                own_chunks += grp
                for place in places:
                    if "groups" in p and place != g:
                        continue
                    l, c = divmod(mod_n, 12)
                    pair = [dict(job=p, mod=(l, c, half), kn=4, C=512,
                                 src=A["w_mod_2"][l][half * 512:(half + 1) * 512, c * 512:(c + 1) * 512]) for half in range(2)]
                    behind.setdefault(len(own_chunks) + SPLIT - (2 if "groups" in p else 1), []).extend(pair)
                    p["mods"][place] = (mod_n, pair)
                    mod_n += 1
        assert mod_n == 24 or dry_stop is not None
        order = []
        for n, c in enumerate(own_chunks):
            order += [c] + behind.get(n, [])
        chunks = order
        n_split = 0
        for r, c in enumerate(chunks):
            c["r"] = r
            if "mod" not in c:
                c["s"] = n_split
                n_split += 1
        splits = [c for c in chunks if "s" in c]

        source = None
        for p in phases:
            before = phases[p["i"] - 1] if p["i"] else None
            p["barrier"] = True
            if p["kind"] != "linear":
                source = None
                continue
            p["fed"] = None
            if before["kind"] == "apply" and before.get("dst") != "c":
                source = "u"
                p["fed"] = lambda k, b=before["i"]: (b, k)
                p["barrier"] = False
            elif before["kind"] == "linear" and before["evac"] == "relu2":
                p["fed"] = lambda k, b=before["i"]: (b, k // 2)
                p["barrier"] = False
                source = None
            elif before["kind"] == "linear" and before["evac"] == "conv":
                p["fed"] = lambda k, b=before["i"]: (b, k // 2 * 2 + 1, k % 2)
                p["barrier"] = False
            elif before["kind"] == "linear" and p["x"][0] == "u" and not before.get("stat"):
                p["barrier"] = False
        gi = 0
        for p in phases:
            if p["kind"] == "linear":
                for g in p["groups"]:
                    for c in g:
                        c["gi"] = gi
                    gi += 1
        VREADS = {"y", "gated", "gated2", "addgated", "conv", "poolw"}
        group_sem = {}
        for p in phases:
            if p["kind"] == "linear":
                for g in p["groups"]:
                    group_sem[g[0]["gi"]] = "group_read_v" if p["evac"] in VREADS else "group_read_s"

        def tokens(p):
            return slice(p.get("tok0", 0), p.get("tok0", 0) + p["T"])

        def gain(p, k):
            name, l = p["gain"]
            c = ROW[name] + (l * 8 if name.startswith("g_") else 0) + k
            return vec[:, c:c + 1]

        ROW = {}
        at_row = 0
        for name, n in (("g_mix_pre", 16), ("g_mix_post", 16), ("g_ffn_pre", 16), ("g_ffn_post", 16), ("g_ple", 16),
                        ("g_final_2", 8), ("mla_g_q", 3), ("mla_g_kv", 2), ("pool_scale_2", 4), ("gqa_g_q", 1),
                        ("gqa_g_k", 1), ("c_2", 8), ("c_ctx_2", 8)):
            ROW[name] = at_row
            at_row += n

        def mod_at(l, which, k, seg):
            return modc[:, l, which * 8 + k, seg:seg + 1]

        def operand(p, k, T, hi):
            name, off = p["x"]
            t = tokens(p)
            if name == "u":
                return (uh if hi else ul)[:, off + k, t]
            if name == "h":
                return hid(hh if hi else hl, off + k, T)
            if name == "c":
                return (ch if hi else cl)[:, off + k, t]
            return (ph_ if hi else pl_)[:, k, :]

        def acc(g, T, cols=None):
            b = (g["gi"] % 2) * 2
            return ps[:, b:b + 2, 0:T]

        def segs(T):
            return [(s, slice(s * S, (s + 1) * S)) for s in range(T // S)]

        def softmax_units(what):
            units = []
            if what == "dil":
                for pair in range(4):
                    for q in range(2):
                        for hd in (2 * pair, 2 * pair + 1):
                            nk = q + 1
                            o = (hd % 2) * 64
                            prod = []
                            for g in range(3):
                                prod.append((qk2[o:o + 64, g * 8 + hd // 2, q * P:(q + 1) * P],
                                             qk2[o:o + 64, g * 8 + 4 + hd // 2, 0:nk * P], g * nk * P))
                            vals = [v2[:, kt, g * 512 + hd * 64:g * 512 + hd * 64 + 64] for g in range(3) for kt in range(nk)]
                            units.append(dict(prod=prod, W=3 * nk * P, mask=(0 if q == 0 else 384), vals=vals,
                                              scale=HD ** -0.5, rows=(o, o + 64), pair=pair, q=q, opair=pair, col=q * P))
            if what == "mla":
                n = 0
                for seg in (1, 0):
                    for pair in range(4):
                        for q in range(2):
                            for hd in (2 * pair, 2 * pair + 1):
                                o = (hd % 2) * 64
                                keys = [(S, T2)] if seg == 1 else [(0, T2)]
                                a, b = keys[0]
                                t0 = seg * S + q * P
                                prod = [(qm[0:96, hd, t0:t0 + P], km[0:96, hd, a:b], 0)]
                                vals = [vm[:, kt, hd * 64:(hd + 1) * 64] for kt in range(a // P, b // P)]
                                units.append(dict(prod=prod, W=b - a, mask=None, vals=vals, scale=MLA_HD ** -0.5,
                                                  rows=(o, o + 64), pair=n, opair=pair, q=q, col=t0))
                        n += 1
            if what == "gqa":
                for hd in range(8):
                    for q in range(2):
                        kv = hd // 4
                        prod = [(qg[:, hd, q * P:(q + 1) * P], kg[:, kv, :], 0)]
                        vals = [vg[:, kt, kv * P:(kv + 1) * P] for kt in range(4)]
                        units.append(dict(prod=prod, W=T2, mask=None, vals=vals, scale=P ** -0.5, rows=(0, P),
                                          pair=hd, opair=hd, q=q, col=q * P))
            for n, u in enumerate(units):
                u["n"] = n
                u["ends"] = n + 1 == len(units) or units[n + 1]["pair"] != u["pair"]
            return units

        def rotation(p, g):
            if p["evac"] == "qk2":
                t = int(p["name"][-1]) * 8 + 2 * g
                return qk2[:, t:t + 2, :], perm1, cos1, sin1, P
            return None

        def rope_tiles(what):
            if what == "mla":
                r = MLA_HD
                return ([(kr[0:r, 0:S], perm_m[0:r, 0:r], ropem[0:r, 0, :], ropem[0:r, 1, :], r)]
                        + [(qm[0:r, hd, 0:S], perm_m[0:r, 0:r], ropem[0:r, 0, :], ropem[0:r, 1, :], r) for hd in range(8)])
            return ([(qg[:, hd, :], perm_g, ropeg[:, 0, :], ropeg[:, 1, :], P) for hd in range(8)]
                    + [(kg[:, kv, 0:S], perm_g, ropeg[:, 0, :], ropeg[:, 1, :], P) for kv in range(2)])

        def at(family, key=None):
            return C.sems[family], C.after(family, key)

        def ended(i):
            return [v for v in (C.after_phase(e, i - 1) for e in ENGINES) if v] if i and phases[i]["barrier"] else []

        ENGINES = ("tensor", "scalar", "vector")

        block = ctx.enter_context(nc.Block())

        @block.sync
        def _(sp):
            with nc.allow_non_contiguous_dma(reason="small"):
                sp.dma_start(squares[:, :, :], A["const_squares"].rearrange("p (j c) -> p j c", j=9)).then_inc(loaded["squares"], 16)
                sp.dma_start(xin[:, 0:2, :], A["x"][0].rearrange("(t p) d -> p t d", p=P)).then_inc(loaded["x"], 16)
                sp.dma_start(xin[:, 2:4, :], A["ctx_2"][0].rearrange("(t p) d -> p t d", p=P)).then_inc(loaded["x"], 16)
                row = lambda ap: ap.rearrange("a (k p) -> (a k) p", p=P)
                r0 = 0
                for name in ("g_mix_pre", "g_mix_post", "g_ffn_pre", "g_ffn_post", "g_ple", "g_final_2", "mla_g_q_2",
                             "mla_g_kv_2", "pool_scale_2", "gqa_g_q_2", "gqa_g_k_2", "c_2", "c_ctx_2"):
                    ap = A[name]
                    ap = row(ap) if len(ap.shape) == 2 else ap.rearrange("(k p) -> k p", p=P)
                    sp.dma_start(rows[r0:r0 + ap.shape[0], 0, :], ap).then_inc(loaded["rows"], 16)
                    r0 += ap.shape[0]
                for l in range(2):
                    sp.dma_start(rows[0:66, 1 + l, :], A["ffn_conv_w_2"][l].rearrange("j (k p) -> (j k) p", p=P)).then_inc(loaded["rows"], 16)
                    sp.dma_start(rows[66:88, 1 + l, :], A["ffn_conv_b_2"][l:l + 1].rearrange("a (k p) -> (a k) p", p=P)).then_inc(loaded["rows"], 16)
                sp.dma_start(rows[0:96, 3, :], row(A["b_mod_2"])).then_inc(loaded["rows"], 16)
                sp.dma_start(freq[:, :], A["const_freq"]).then_inc(loaded["freq"], 16)
                sp.dma_start(posi[:, :], A["positions"].to_broadcast([P, S])).then_inc(loaded["pos"], 16)
                for c in chunks:
                    r = c["r"]
                    if r >= RAW:
                        o = chunks[r - RAW]
                        if "s" in o:
                            sp.wait_ge(*at("weights_low", o["s"]))
                        else:
                            sp.wait_ge(*at("weights_used", ("mod", o["r"])))
                    dst = raw[:, r % RAW, 0:c["kn"] * c["C"]].rearrange("p (k c) -> p k c", k=c["kn"])
                    sp.dma_start(dst, c["src"].rearrange("(k p) c -> p k c", p=P)).then_inc(landed[r % RAW], 16)
                sp.wait_ge(*at("turned_copied", (phases[-1]["i"], 7)))
                for t in range(2):
                    sp.dma_start(out[0].rearrange("(t p) d -> p t d", p=P)[:, t, :], xin[:, t, :]).then_inc(stored, 16)
                sp.wait_ge(stored, 32)

        n_arena = [0]
        for p in phases:
            if p.get("name") == "dil_qk0":
                p["loads"] = [(masks[:, :], A["const_masks"])]
            if p.get("name") == "gqa_q":
                p["loads"] = [(ropeg[:, :, :], A["const_rope2"][:, 2 * S:].rearrange("p (j c) -> p j c", j=2))]
            if p.get("name") == "uq":
                p["loads"] = [(ropem[:, :, :], A["const_rope2"][:, 0:2 * S].rearrange("p (j c) -> p j c", j=2))]
            if p.get("name") == "mix_c":
                p["loads"] = [(rcount[:, :, :], A["const_rcount"].rearrange("p (g c) -> p g c", g=4))]
            if p["kind"] == "ple":
                p["loads"] = [(pin[:, :, :], A["p"][p["l"], 0].rearrange("(t p) d -> p t d", p=P))]
            for _ in p.get("loads", ()):
                n_arena[0] += 1
            p["arena_value"] = 16 * n_arena[0]

        @block.tensor
        def _(pe):
            def up(family, key=None):
                return C.sems[family], C.raised("tensor", family, key)


            def mm(out_, lhsT, rhs, start, stop):
                return pe.matmul(out_, lhsT, rhs, start=start, stop=stop, skip_group_check=True)

            def square_sums(p, g):
                T, last_g = p["T"], 3
                pe.wait_ge(*at("stat_squares", (p["i"], g)))
                for j in range(2):
                    sq_ = sq[:, g % 2, j * S:(j + 1) * S] if T == S else sq[:, j, :]
                    last = mm(ps[:, 4, 0:T], ones, sq_, g == 0 and j == 0, g == last_g and j == 1)
                last.then_inc(*up("stat_summed", (p["i"], g)))

            pending = []

            def swap_pending():
                while pending:
                    q, g = pending.pop()
                    tile, perm, _, _, r = rotation(q, g)
                    pe.wait_ge(*at("group_read_s", ("group", q["groups"][g][0]["gi"])))
                    if swaps[0]:
                        pe.wait_ge(*at("rotated", swaps[0] - 1))
                    mm(ps[0:r, 5, :].rearrange("p (t c) -> p t c", t=2)[:, 0:tile.shape[1], :], perm, tile, True, True).then_inc(
                        *up("swapped", swaps[0]))
                    swaps[0] += 1

            swaps = [0]

            def linear_pe(p):
                T = p["T"]
                for g, grp in enumerate(p["groups"]):
                    if p.get("stat") and g >= 2:
                        square_sums(p, g - 2)
                    for c in grp:
                        if c["first"] and c["gi"] >= 2:
                            pe.wait_ge(*at(group_sem[c["gi"] - 2], ("group", c["gi"] - 2)))
                        pe.wait_ge(*at("weights_low", c["s"]))
                        s = c["s"] % SPLIT
                        A_ = acc(c, T)
                        if p["mode"] == "T":
                            tiles = [(j, j * p["m"], p["m"]) for j in range(c["C"] // p["m"])]
                            if c["C"] == 160:
                                tiles = [(0, 0, P), (1, 64, 96)]
                            if p["evac"] == "poolw":
                                tiles = [(0, 0, P)]
                            for j, c0, m in tiles:
                                for k in range(c["kn"]):
                                    kk = c["k"] + k
                                    if g == 0 and j == 0 and p["fed"]:
                                        pe.wait_ge(*at("operand_low", p["fed"](kk)))
                                    w = [b[:, s, k * c["C"] + c0:k * c["C"] + c0 + m] for b in (whi, wlo)]
                                    x = [operand(p, kk, T, hi) for hi in (True, False)]
                                    st, en = c["first"] and k == 0, c["last"] and k == c["kn"] - 1
                                    o = A_[0:m, j, :]
                                    mm(o, w[0], x[0], st, False)
                                    mm(o, w[0], x[1], False, False)
                                    last = mm(o, w[1], x[0], False, en)
                        else:
                            nt = T // P
                            for t in range(nt):
                                b, col = (t, 0) if nt == 2 else (t // 2, (t % 2) * 256)
                                o = ps[:, (c["gi"] % 2) * 2 + b, col:col + 256]
                                for k in range(c["kn"]):
                                    kk = c["k"] + k
                                    if g == 0 and t == 0 and p["fed"]:
                                        pe.wait_ge(*at("operand_low", p["fed"](kk)))
                                    w = [b_[:, s, k * 256:(k + 1) * 256] for b_ in (whi, wlo)]
                                    x = [operand(p, kk, T, hi)[:, t * P:(t + 1) * P] for hi in (True, False)]
                                    mm(o, x[0], w[0], k == 0, False)
                                    mm(o, x[0], w[1], False, False)
                                    last = mm(o, x[1], w[0], False, k == c["kn"] - 1)
                        last.then_inc(*up("weights_used", c["s"]))
                    if g - 1 in p["mods"]:
                        mod_turn(p["mods"][g - 1][0])
                    if g in p["mods"]:
                        mod_products(*p["mods"][g])
                    swap_pending()
                    if rotation(p, g):
                        pending.append((p, g))
                if p.get("stat"):
                    square_sums(p, g - 1)
                    square_sums(p, g)

            def pool_pe(p):
                c = p["groups"][0][0]
                pe.wait_ge(*at("weights_low", c["s"]))
                if c["gi"] >= 2:
                    pe.wait_ge(*at(group_sem[c["gi"] - 2], ("group", c["gi"] - 2)))
                pe.wait_ge(*at(group_sem[c["gi"] - 1], ("group", c["gi"] - 1)))
                s = c["s"] % SPLIT
                for g in range(4):
                    w = [b[:, s, g * P:(g + 1) * P] for b in (whi, wlo)]
                    o = ps[:, g, :]
                    mm(o, w[0], uh[:, g, :], True, False)
                    mm(o, w[0], ul[:, g, :], False, False)
                    last = mm(o, w[1], uh[:, g, :], False, True)
                last.then_inc(*up("weights_used", c["s"]))

            def mod_products(n, pair):
                if n >= 2:
                    pe.wait_ge(*at("mod_kept", n - 2))
                for half, c in enumerate(pair):
                    pe.wait_ge(landed[c["r"] % RAW], 16 * (c["r"] // RAW + 1))
                    for k in range(4):
                        last = mm(ps[32 * k:32 * k + 2, 6 + n % 2, :], cc[:, half * 4 + k, :], raw[:, c["r"] % RAW, k * 512:(k + 1) * 512],
                                  half == 0, half == 1)
                    last.then_inc(*up("weights_used", ("mod", c["r"])))

            def mod_turn(n):
                pe.wait_ge(*at("mod_rows", n))
                for j in range(4):
                    last = mm(ps[:, 6 + n % 2, 2 * j:2 * j + 2], modrow[:, j * P:(j + 1) * P], select, True, True)
                last.then_inc(*up("mod_turned", n))

            for p in phases:
                kind, i = p["kind"], p["i"]
                if kind != "linear":
                    swap_pending()
                for sem, value in ended(i):
                    pe.wait_ge(sem, value)
                if kind == "init":
                    pe.wait_ge(loaded["squares"], 16)
                    pe.wait_ge(loaded["rows"], 16 * 18)
                    for b in (6, 7):
                        mm(ps[:, b, :], ones, squares[:, 0:4, :].rearrange("p j c -> p (j c)"), True, True)
                    for j in range(4):
                        n = (at_row, 88, 88, 96)[j]
                        last = pe.transpose(ps[:, 0, j * P:j * P + n], rows[0:n, j, :], ident[0:n, 0:n])
                    last.then_inc(*up("turned", "rows"))
                    pe.wait_ge(loaded["x"], 32)
                    for k in range(8):
                        if k >= 3:
                            pe.wait_ge(*at("turned_copied", ("x", k - 3)))
                        for t in range(4):
                            last = pe.transpose(ps[:, 1 + k % 3, t * P:(t + 1) * P], xin[:, t, k * P:(k + 1) * P], ident)
                        last.then_inc(*up("turned", ("x", k)))
                elif kind == "stats":
                    for k in range(p["n"]):
                        pe.wait_ge(*at("stat_squares", (i, k)))
                        mm(ps[:, 4, 0:p["T"]], ones, sq[:, k % 2, 0:p["T"]], k == 0, k == p["n"] - 1).then_inc(
                            *up("stat_summed", (i, k)))
                elif kind == "join":
                    for g in range(4):
                        square_sums(p, g)
                elif kind == "linear":
                    if p["evac"] == "poolw":
                        pool_pe(p)
                    else:
                        linear_pe(p)
                elif kind == "stick":
                    def z(hd):
                        o = (hd % 2) * 64
                        if hd >= 4:
                            pe.wait_ge(*at("stick_weights", (i, hd - 4)))
                        b = hd % 4
                        qh = q1[o:o + 64, hd // 2, :]
                        mm(ps[:, b, 0:256], k1[o:o + 64, hd // 2, 0:P], qh, True, False)
                        mm(ps[:, b, 256:384], k1[o:o + 64, hd // 2, P:S], qh[:, P:S], False, True).then_inc(
                            *up("scores", (i, hd)))

                    def attend(hd):
                        b = hd % 2
                        pe.wait_ge(*at("masked", (i, hd)))
                        pair, o = hd // 2, (hd % 2) * 64
                        if pair >= 2 and hd % 2 == 0:
                            pe.wait_ge(*at("operand_low", (i, pair - 2)))
                        dst = ps[o:o + 64, 4 + pair % 2, 0:S]
                        vv = [v1[:, t, hd * 64:(hd + 1) * 64] for t in range(2)]
                        mm(dst[:, 0:256], vv[0], sba[:, b, 0:256], True, False)
                        mm(dst[:, 128:256], vv[1], sba[:, b, 256:384], False, True).then_inc(
                            *up("attended", (i, hd)))

                    z(0)
                    z(1)
                    for hd in range(HEADS):
                        if hd + 2 < HEADS:
                            z(hd + 2)
                        b = hd % 2
                        pe.wait_ge(*at("fail_ready", (i, hd)))
                        zb = hd % 4
                        mm(ps[:, zb, 0:256], negtri, sbf[:, b, 0:256], False, False)
                        mm(ps[:, zb, 128:256], negones, sbf[:, b, 256:384], False, False)
                        mm(ps[:, zb, 256:384], negtri, sbf[:, b, 256:384], False, True).then_inc(
                            *up("fail_summed", (i, hd)))
                        if hd >= 1:
                            attend(hd - 1)
                        if hd % 2 == 1 and hd // 2 < len(p["mods"]):
                            mod_products(*p["mods"][hd // 2])
                            mod_turn(p["mods"][hd // 2][0])
                    attend(HEADS - 1)
                elif kind == "rope":
                    for t, (tile, perm, c_, s_, r) in enumerate(rope_tiles(p["what"])):
                        if t >= 2:
                            pe.wait_ge(*at("rotated", (i, t - 2)))
                        mm(ps[0:r, t % 2, 0:S], perm, tile, True, True).then_inc(*up("swapped", (i, t)))
                elif kind == "softmax":
                    units = softmax_units(p["what"])

                    def scores(u):
                        n = u["n"]
                        if u["mask"] is not None and n >= 2:
                            pe.wait_ge(*at("max_ready", (i, n - 2)))
                        if u["mask"] is None and n >= 4:
                            pe.wait_ge(*at("weights_exp", (i, n - 4)))
                        for lhsT, rhs, col in u["prod"]:
                            width = rhs.shape[-1]
                            c0 = 0
                            while c0 < width:
                                w = min(width - c0, 512 - (col + c0) % 512)
                                bank = (n % 2) * 2 + (col + c0) // 512 if u["mask"] is not None else n % 4
                                last = mm(ps[:, bank, (col + c0) % 512:(col + c0) % 512 + w], lhsT, rhs[:, c0:c0 + w], True, True)
                                c0 += w
                        last.then_inc(*up("scores", (i, n)))

                    def turn(u):
                        n = u["n"]
                        pe.wait_ge(*at("weights_normed", (i, n)))
                        wide = u["mask"] is not None
                        if n >= (1 if wide else 2):
                            pe.wait_ge(*at("turned_copied", (i, n - (1 if wide else 2))))
                        kt = u["W"] // P
                        for k in range(kt):
                            last = pe.transpose(ps[:, (4 + k // 4) if wide else 4 + n % 2, (k % 4) * P:(k % 4 + 1) * P], pr[:, n % 2, k * P:(k + 1) * P], ident)
                        last.then_inc(*up("turned", (i, n)))

                    def attend(u):
                        n = u["n"]
                        kt = u["W"] // P
                        pe.wait_ge(*at("turned_copied", (i, n)))
                        a, b = u["rows"]
                        if u["pair"] >= 2:
                            pe.wait_ge(*at("operand_low", (i, u["pair"] - 2)))
                        o = ps[a:b, 6 + u["pair"] % 2, u["q"] * P:(u["q"] + 1) * P]
                        for k in range(kt):
                            last = mm(o, u["vals"][k], pt[:, n % 2, k * P:(k + 1) * P], k == 0, k == kt - 1)
                        last.then_inc(*up("attended", (i, n)))

                    N = len(units)
                    ahead = 2 if units[0]["mask"] is not None else 3
                    for n in range(ahead):
                        scores(units[n])
                    for n in range(N):
                        if n + ahead < N:
                            scores(units[n + ahead])
                        turn(units[n])
                        if n >= 1:
                            attend(units[n - 1])
                    attend(units[N - 1])
                elif kind == "ple":
                    pe.wait_ge(loaded["arena"], p["arena_value"])
                    for k in range(2):
                        for t in range(2):
                            last = pe.transpose(ps[:, 4, k * S + t * P:k * S + (t + 1) * P], pin[:, t, k * P:(k + 1) * P], ident)
                    last.then_inc(*up("turned", (i, 0)))
                elif kind == "qknorm":
                    for b in range(6):
                        pe.wait_ge(*at("stat_squares", (i, "q" if b < 4 else "k")))
                        last = mm(ps[:, b, :], ones, y[:, b, :], True, True)
                        if b in (3, 5):
                            last.then_inc(*up("stat_summed", (i, "q" if b < 4 else "k")))
                elif kind in ("final", "dump"):
                    for k in range(8):
                        if kind == "final":
                            pe.wait_ge(*at("normed", (i, k)))
                        src = y if kind == "final" else h
                        if k >= 3:
                            pe.wait_ge(*at("turned_copied", (i, k - 3)))
                        for t in range(2):
                            last = pe.transpose(ps[:, 1 + k % 3, t * P:(t + 1) * P], src[:, k, t * P:(t + 1) * P], ident)
                        last.then_inc(*up("turned", (i, k)))
                C.end("tensor", i)

        @block.scalar
        def _(act):
            def up(family, key=None):
                return C.sems[family], C.raised("scalar", family, key)

            def own():
                return C.sems[C.last["scalar"][0]], C.last["scalar"][1]


            def split_high(s):
                if s >= len(splits):
                    return
                c = splits[s]
                n = c["kn"] * c["C"]
                act.wait_ge(landed[c["r"] % RAW], 16 * (c["r"] // RAW + 1))
                if s >= SPLIT:
                    act.wait_ge(*at("weights_used", s - SPLIT))
                act.wait_ge(*own())
                nc.scalar.activation(whi[:, s % SPLIT, 0:n], raw[:, c["r"] % RAW, 0:n], ACT.Copy).then_inc(
                    *up("weights_high", s))

            def hidden_high(p, g):
                b = g % 2
                act.wait_ge(*at("normed", (p["i"], g)))
                act.wait_ge(*own())
                nc.scalar.activation(hh[:, 2 * g * S:2 * (g + 1) * S].rearrange("p (t c) -> p t c", t=2), y[:, 2 * b:2 * b + 2, 0:S], ACT.Copy).then_inc(
                    *up("operand_high", (p["i"], g)))

            def hidden_high_conv(p, g):
                for j in range(2):
                    act.wait_ge(*at("group_read_v", (p["i"], g, j)))
                    act.wait_ge(*own())
                    nc.scalar.activation(hid(hh, g - 1 + j, p["T"]), csil[:, j, 0:p["T"]], ACT.Copy).then_inc(
                        *up("operand_high", (p["i"], g, j)))

            def squares_of(p, g):
                T, i = p["T"], p["i"]
                src = y if p["stat"] == "y" else h
                if p["kind"] == "linear" and p["evac"] != "addgated":
                    act.wait_ge(*at("group_read_v", ("group", p["groups"][g][0]["gi"])))
                else:
                    act.wait_ge(*at("tiles_ready", (i, g)))
                if T == S:
                    if g >= 2:
                        act.wait_ge(*at("stat_summed", (i, g - 2)))
                    act.wait_ge(*own())
                    nc.scalar.activation(sq[:, g % 2, :].rearrange("p (t c) -> p t c", t=2), src[:, 2 * g:2 * g + 2, 0:S], ACT.Square).then_inc(
                        *up("stat_squares", (i, g)))
                else:
                    if g >= 1:
                        act.wait_ge(*at("stat_summed", (i, g - 1)))
                    act.wait_ge(*own())
                    nc.scalar.activation(sq[:, :, :], src[:, 2 * g:2 * g + 2, :], ACT.Square).then_inc(
                        *up("stat_squares", (i, g)))

            def rstd_of(p):
                act.wait_ge(*at("stat_summed", (p["i"], 3)))
                act.wait_ge(*own())
                nc.scalar.activation(lnv[:, 0:p["T"]], ps[:, 4, 0:p["T"]], ACT.Ln, scale=1.0 / D, bias=small[:, 40:41]).then_inc(
                    *up("scalar_step"))
                act.wait_ge(*own())
                nc.scalar.activation(rstd[:, 0:p["T"]], lnv[:, 0:p["T"]], ACT.Exp, scale=-0.5).then_inc(
                    *up("rstd_ready", p["i"]))

            def evac(p, grp):
                c = grp[0]
                T, kind, i, g = p["T"], p["evac"], p["i"], c["g"]
                key = ("group", c["gi"])
                A_ = acc(c, T)
                act.wait_ge(*at("weights_used", grp[-1]["s"]))
                if kind == "qk1":
                    dst = (q1 if g < 4 else k1)[:, (g % 4) * 2:(g % 4) * 2 + 2, :]
                    act.wait_ge(*own())
                    nc.scalar.activation(dst, A_, ACT.Copy, scale=HD ** -0.5 if g < 4 else 1.0).then_inc(
                        *up("group_read_s", key))
                elif kind == "qk2":
                    grp_no = int(p["name"][-1])
                    act.wait_ge(*own())
                    nc.scalar.activation(qk2[:, grp_no * 8 + g * 2:grp_no * 8 + g * 2 + 2, :], A_, ACT.Copy).then_inc(
                        *up("group_read_s", key))
                elif kind == "v":
                    nt = T // P
                    src = ps[:, (c["gi"] % 2) * 2:(c["gi"] % 2) * 2 + 2, 0:256 if nt == 2 else 512]
                    if nt == 4:
                        src = src.rearrange("p b (t c) -> p b t c", t=2)
                    name = p["name"]
                    if name == "stick_v":
                        dst = v1[:, :, g * 256:(g + 1) * 256]
                    elif name.startswith("dil_v"):
                        c0 = int(name[-1]) * 512 + g * 256
                        dst = v2[:, :, c0:c0 + 256]
                    elif name == "uv":
                        dst = vm[:, :, g * 256:(g + 1) * 256].rearrange("p (b t) c -> p b t c", b=2)
                    else:
                        dst = vg[:, :, :].rearrange("p (b t) c -> p b t c", b=2)
                    act.wait_ge(*own())
                    nc.scalar.activation(dst, src, ACT.Copy).then_inc(*up("group_read_s", key))
                elif kind == "relu2":
                    act.wait_ge(*own())
                    nc.scalar.activation(work[:, c["gi"] % 2, :, 0:S], A_, ACT.Relu).then_inc(*up("group_read_s", key))
                    if g >= 1:
                        hidden_high(p, g - 1)
                    if g == len(p["groups"]) - 1:
                        hidden_high(p, g)
                elif kind == "gate":
                    if g >= 2:
                        act.wait_ge(*at("normed", ("gate", i, g - 2)))
                    act.wait_ge(*own())
                    nc.scalar.activation(ge[:, g % 2, :, :], A_, ACT.Exp, scale=-1.0).then_inc(*up("group_read_s", key))
                elif kind == "mixc":
                    if g < 2:
                        act.wait_ge(*own())
                        nc.scalar.activation(y[:, 2 * g:2 * g + 2, :], A_, ACT.Copy).then_inc(*up("group_read_s", key))
                    else:
                        act.wait_ge(*own())
                        nc.scalar.activation(y[:, 4, :], A_[:, 0, :], ACT.Copy).then_inc(*up("scalar_step"))
                        act.wait_ge(*own())
                        nc.scalar.activation(kr[0:96, :], A_[0:96, 1, :], ACT.Copy).then_inc(*up("group_read_s", key))
                elif kind == "mixp":
                    for j in range(2):
                        act.wait_ge(*own())
                        nc.scalar.activation(pbuf[:, 2 * g + j, :, PAD:PAD + S], A_[:, j, :].rearrange("p (s c) -> p s c", s=2), ACT.Copy).then_inc(
                            *up("group_read_s", key if j else None))
                elif kind == "uq":
                    act.wait_ge(*own())
                    nc.scalar.activation(qm[0:96, 2 * g:2 * g + 2, :], A_[0:96], ACT.Copy).then_inc(*up("group_read_s", key))
                elif kind == "uk":
                    for par in range(2):
                        act.wait_ge(*own())
                        nc.scalar.activation(km[0:64, 4 * g + par:4 * g + 4:2, :], A_[64 * par:64 * par + 64], ACT.Copy).then_inc(
                            *up("group_read_s", key if par else None))
                elif kind == "qg":
                    act.wait_ge(*own())
                    nc.scalar.activation(qg[:, 2 * g:2 * g + 2, :], A_, ACT.Copy).then_inc(*up("group_read_s", key))
                elif kind == "kg":
                    act.wait_ge(*own())
                    nc.scalar.activation(kg[:, :, :], A_, ACT.Copy).then_inc(*up("group_read_s", key))
                elif kind == "poolw":
                    for t in range(4):
                        act.wait_ge(*own())
                        nc.scalar.activation(uh[:, 4 + t, :], ps[:, t, :], ACT.Copy, scale=vec[:, ROW["pool_scale_2"] + t:ROW["pool_scale_2"] + t + 1]).then_inc(
                            *up("operand_high", (i, t)))
                elif kind == "conv" and g % 2 == 0:
                    l, f0 = p["l"], p["f0"]
                    for j in range(2):
                        f = f0 + g + j
                        act.wait_ge(*own())
                        nc.scalar.activation(cacc[:, j, 0:T], A_[:, j, :], ACT.Identity, bias=convv[:, l, 66 + f:67 + f], scale=convv[:, l, 22 + f:23 + f]).then_inc(
                            *up("moved", (i, g, j)))
                    if g >= 2:
                        hidden_high_conv(p, g - 1)
                elif kind == "conv":
                    for j in range(2):
                        act.wait_ge(*at("group_read_v", (i, g - 1, j)))
                        if g >= 2:
                            act.wait_ge(*at("operand_low", (i, g - 2, j)))
                        act.wait_ge(*own())
                        nc.scalar.activation(csil[:, j, 0:T], cacc[:, j, 0:T], ACT.Silu).then_inc(
                            *up("gated_silu", (i, g - 1, j)))
                    if g == len(p["groups"]) - 1:
                        hidden_high_conv(p, g)

            def mod_rows(n, pair):
                act.wait_ge(*at("weights_used", ("mod", pair[1]["r"])))
                act.wait_ge(*own())
                nc.scalar.activation(modrow, ps[:, 6 + n % 2, :], ACT.Copy).then_inc(*up("mod_rows", n))

            nc.scalar.preload_act_table_set("natural_log_exp_and_others")
            for p in phases:
                kind, i = p["kind"], p["i"]
                for sem, value in ended(i):
                    act.wait_ge(sem, value)
                for dst, src in p.get("loads", ()):
                    act.dma_start(dst, src).then_inc(loaded["arena"], 16)
                if kind == "init":
                    act.wait_ge(*at("turned", "rows"))
                    for n, dst in enumerate((vec[:, 0:at_row], convv[:, 0, 0:88], convv[:, 1, 0:88], bmod[:, 0:96])):
                        nc.scalar.activation(dst, ps[:, 0, n * P:n * P + (at_row, 88, 88, 96)[n]], ACT.Copy).then_inc(
                            *up("scalar_step"))
                    for k in range(8):
                        act.wait_ge(*at("turned", ("x", k)))
                        act.wait_ge(*own())
                        nc.scalar.activation(h[:, k, :], ps[:, 1 + k % 3, :], ACT.Copy).then_inc(
                            *up("turned_copied", ("x", k)))
                    act.wait_ge(*at("normed", "angles"))
                    act.wait_ge(*own())
                    nc.scalar.activation(sin1[:, :], turns[:, 0, :], ACT.Sin).then_inc(*up("scalar_step"))
                    act.wait_ge(*own())
                    nc.scalar.activation(cos1[:, :], turns[:, 1, :], ACT.Sin).then_inc(*up("scalar_step"))
                    nc.scalar.preload_act_table_set("natural_log_exp_and_others")
                    act.wait_ge(*own())
                    nc.scalar.activation(silu[:, 0, :], vec[:, ROW["c_2"]:ROW["c_2"] + 8], ACT.Exp, scale=-1.0).then_inc(
                        *up("scalar_step"))
                    act.wait_ge(*own())
                    nc.scalar.activation(silu[:, 1, :], vec[:, ROW["c_ctx_2"]:ROW["c_ctx_2"] + 8], ACT.Exp, scale=-1.0).then_inc(
                        *up("weights_exp", "cond"))
                    for s in range(SPLIT):
                        split_high(s)
                elif kind == "stats":
                    src = h if p["src"] == "h" else y
                    s0 = p.get("s0", 0)
                    for k in range(p["n"]):
                        if k >= 2:
                            act.wait_ge(*at("stat_summed", (i, k - 2)))
                        act.wait_ge(*own())
                        nc.scalar.activation(sq[:, k % 2, 0:p["T"]], src[:, s0 + k, 0:p["T"]], ACT.Square).then_inc(
                            *up("stat_squares", (i, k)))
                    act.wait_ge(*at("stat_summed", (i, p["n"] - 1)))
                    act.wait_ge(*own())
                    nc.scalar.activation(lnv[:, 0:p["T"]], ps[:, 4, 0:p["T"]], ACT.Ln, scale=1.0 / p["D"], bias=small[:, 40:41]).then_inc(
                        *up("scalar_step"))
                    act.wait_ge(*own())
                    nc.scalar.activation(rstd[:, 0:p["T"]], lnv[:, 0:p["T"]], ACT.Exp, scale=-0.5).then_inc(
                        *up("rstd_ready", i))
                elif kind == "apply":
                    for k in range(p["n"]):
                        act.wait_ge(*at("normed", (i, k)))
                        dst = ch if p.get("dst") == "c" else uh
                        k_ = p.get("s0", 0) + k if p.get("dst") == "c" else k
                        if "mod" in p:
                            for s_, sl in segs(p["T"]):
                                act.wait_ge(*own())
                                nc.scalar.activation(uh[:, k, sl], y[:, k, sl], ACT.Identity, bias=mod_at(*p["mod"], k, s_)).then_inc(
                                    *up("operand_high", (i, k)))
                            continue
                        act.wait_ge(*own())
                        nc.scalar.activation(dst[:, k_, 0:p["T"]], y[:, p.get("s0", 0) + k, 0:p["T"]], ACT.Copy).then_inc(
                            *up("operand_high", (i, k)))
                elif kind == "linear":
                    for grp in p["groups"]:
                        for c in grp[:-1]:
                            split_high(c["s"] + SPLIT)
                        evac(p, grp)
                        if grp[0]["g"] in p["mods"]:
                            mod_rows(*p["mods"][grp[0]["g"]])
                        if p.get("stat") and grp[0]["g"] >= 1:
                            squares_of(p, grp[0]["g"] - 1)
                        split_high(grp[-1]["s"] + SPLIT)
                    if p.get("stat"):
                        squares_of(p, 3)
                        rstd_of(p)
                elif kind == "join":
                    for g in range(4):
                        squares_of(p, g)
                    rstd_of(p)
                elif kind == "stick":
                    def ex(hd):
                        b = hd % 2
                        act.wait_ge(*at("scores", (i, hd)))
                        act.wait_ge(*own())
                        nc.scalar.activation(sbt[:, b, :], ps[:, hd % 4, 0:384], ACT.Abs).then_inc(*up("scalar_step"))
                        act.wait_ge(*own())
                        nc.scalar.activation(sbe[:, b, :], sbt[:, b, :], ACT.Exp, scale=-1.0).then_inc(*up("scalar_step"))
                        if hd >= 2:
                            act.wait_ge(*at("fail_ready", (i, hd - 2)))
                        act.wait_ge(*own())
                        nc.scalar.activation(sbl[:, b, :], sbe[:, b, :], ACT.Ln, bias=1.0).then_inc(
                            *up("weights_exp", (i, hd)))

                    def high(pair):
                        act.wait_ge(*at("attended", (i, 2 * pair + 1)))
                        act.wait_ge(*own())
                        nc.scalar.activation(uh[:, pair, 0:S], ps[:, 4 + pair % 2, 0:S], ACT.Copy).then_inc(
                            *up("operand_high", (i, pair)))

                    ex(0)
                    for hd in range(HEADS):
                        if hd + 1 < HEADS:
                            ex(hd + 1)
                        b = hd % 2
                        act.wait_ge(*at("fail_summed", (i, hd)))
                        if hd >= 2:
                            act.wait_ge(*at("attended", (i, hd - 2)))
                        act.wait_ge(*own())
                        nc.scalar.activation(sba[:, b, :], ps[:, hd % 4, 0:384], ACT.Exp).then_inc(*up("stick_weights", (i, hd)))
                        if hd % 2 == 1 and hd // 2 < len(p["mods"]):
                            mod_rows(*p["mods"][hd // 2])
                        if hd % 2 == 0 and hd >= 2:
                            high(hd // 2 - 1)
                    high(HEADS // 2 - 1)
                elif kind == "softmax":
                    units = softmax_units(p["what"])
                    N = len(units)

                    def exp_(u):
                        n = u["n"]
                        act.wait_ge(*at("max_ready", (i, n)))
                        b = n % 2
                        W = u["W"]
                        if u["mask"] is not None:
                            src = sm[:, b, 0:W]
                        else:
                            src = ps[:, n % 4, 0:W]
                        if n >= 2:
                            act.wait_ge(*at("turned", (i, n - 2)))
                        act.wait_ge(*own())
                        nc.scalar.activation(pr[:, b, 0:W], src, ACT.Exp, scale=u["scale"], bias=small[:, b:b + 1], accum_out=small[:, 2 + b:3 + b]).then_inc(
                            *up("weights_exp", (i, n)))

                    def copy_(u):
                        n = u["n"]
                        W = u["W"]
                        act.wait_ge(*at("turned", (i, n)))
                        if n >= 2:
                            act.wait_ge(*at("attended", (i, n - 2)))
                        for c0 in range(0, W, 512):
                            w = min(512, W - c0)
                            act.wait_ge(*own())
                            nc.scalar.activation(pt[:, n % 2, c0:c0 + w], ps[:, (4 + c0 // 512) if u["mask"] is not None else 4 + n % 2, 0:w], ACT.Copy).then_inc(
                                *up("turned_copied", (i, n)))

                    def high_(u):
                        n = u["n"]
                        act.wait_ge(*at("attended", (i, n)))
                        t0 = u["col"] - u["q"] * P
                        act.wait_ge(*own())
                        nc.scalar.activation(uh[:, u["opair"], t0:t0 + S], ps[:, 6 + u["pair"] % 2, 0:S], ACT.Copy).then_inc(
                            *up("operand_high", (i, u["pair"])))

                    exp_(units[0])
                    for n in range(N):
                        if n + 1 < N:
                            exp_(units[n + 1])
                        copy_(units[n])
                        if n >= 1 and units[n - 1]["ends"]:
                            high_(units[n - 1])
                    high_(units[N - 1])
                elif kind == "ple":
                    act.wait_ge(*at("turned", (i, 0)))
                    act.wait_ge(*own())
                    nc.scalar.activation(ph_[:, :, :], ps[:, 4, :].rearrange("p (k c) -> p k c", k=2), ACT.Copy).then_inc(
                        *up("operand_high", (i, 0)))
                    act.wait_ge(*at("operand_low", (i, 0)))
                elif kind == "pool":
                    act.wait_ge(*at("normed", (i, 0)))
                    act.wait_ge(*own())
                    nc.scalar.activation(uh[:, 0:4, :], pdif[:, :, :], ACT.Copy).then_inc(*up("operand_high", (i, 0)))
                elif kind == "qknorm":
                    parts = (("q", qg[:, :, :].rearrange("p (b t) c -> p b t c", b=4), slice(0, 4)), ("k", kg[:, :, :], slice(4, 6)))
                    for name, src, b in parts:
                        dst = y[:, b, :].rearrange("p b (t c) -> p b t c", t=2) if name == "q" else y[:, b, :]
                        act.wait_ge(*own())
                        nc.scalar.activation(dst, src, ACT.Square).then_inc(*up("stat_squares", (i, name)))
                    for name, src, b in parts:
                        act.wait_ge(*at("stat_summed", (i, name)))
                        act.wait_ge(*own())
                        nc.scalar.activation(y[:, b, :], ps[:, b, :], ACT.Ln, scale=1.0 / P, bias=small[:, 40:41]).then_inc(
                            *up("scalar_step"))
                        act.wait_ge(*own())
                        nc.scalar.activation(y[:, b, :], y[:, b, :], ACT.Exp, scale=-0.5).then_inc(*up("rstd_ready", (i, name)))
                elif kind in ("final", "dump"):
                    for k in range(8):
                        act.wait_ge(*at("turned", (i, k)))
                        act.wait_ge(*own())
                        nc.scalar.activation(xin[:, 0:2, k * P:(k + 1) * P], ps[:, 1 + k % 3, 0:S].rearrange("p (t c) -> p t c", t=2), ACT.Copy).then_inc(
                            *up("turned_copied", (i, k)))
                C.end("scalar", i)

        @block.vector
        def _(dve):
            def up(family, key=None):
                return C.sems[family], C.raised("vector", family, key)

            def own():
                return C.sems[C.last["vector"][0]], C.last["vector"][1]

            def split_low(s):
                if s >= len(splits):
                    return
                c = splits[s]
                n = c["kn"] * c["C"]
                dve.wait_ge(*at("weights_high", s))
                dve.wait_ge(*own())
                nc.vector.tensor_tensor(wlo[:, s % SPLIT, 0:n], raw[:, c["r"] % RAW, 0:n], whi[:, s % SPLIT, 0:n].bitcast(F32), ALU.subtract).then_inc(
                    *up("weights_low", s))

            def hidden_low_conv(p, g):
                T = p["T"]
                for j in range(2):
                    dve.wait_ge(*at("operand_high", (p["i"], g, j)))
                    dve.wait_ge(*own())
                    nc.vector.tensor_tensor(hid(hl, g - 1 + j, T), csil[:, j, 0:T], hid(hh, g - 1 + j, T).bitcast(F32), ALU.subtract).then_inc(
                        *up("operand_low", (p["i"], g, j)))

            def hidden_low(p, g):
                b = g % 2
                dve.wait_ge(*at("operand_high", (p["i"], g)))
                v = lambda b: b[:, 2 * g * S:2 * (g + 1) * S].rearrange("p (t c) -> p t c", t=2)
                dve.wait_ge(*own())
                nc.vector.tensor_tensor(v(hl), y[:, 2 * b:2 * b + 2, 0:S], v(hh).bitcast(F32), ALU.subtract).then_inc(
                    *up("operand_low", (p["i"], g)))

            def evac(p, grp):
                c = grp[0]
                T, kind, i, g = p["T"], p["evac"], p["i"], c["g"]
                key = ("group", c["gi"])
                A_ = acc(c, T)
                if kind == "y":
                    dve.wait_ge(*at("weights_used", grp[-1]["s"]))
                    dve.wait_ge(*own())
                    nc.vector.tensor_copy(y[:, 2 * g:2 * g + 2, 0:T], A_).then_inc(*up("group_read_v", key))
                elif kind == "relu2":
                    dve.wait_ge(*at("group_read_s", key))
                    w = work[:, c["gi"] % 2, :, 0:S]
                    yy = y[:, 2 * (g % 2):2 * (g % 2) + 2, 0:S]
                    dve.wait_ge(*own())
                    nc.vector.tensor_tensor(yy, w, w, ALU.mult).then_inc(*up("normed", (i, g)))
                    if g >= 1:
                        hidden_low(p, g - 1)
                    if g == len(p["groups"]) - 1:
                        hidden_low(p, g)
                elif kind == "gate":
                    dve.wait_ge(*at("group_read_s", key))
                    gg = ge[:, g % 2, :, :]
                    dve.wait_ge(*own())
                    nc.vector.tensor_scalar(gg, gg, 1.0, None, ALU.add).then_inc(*up("vector_step"))
                    dve.wait_ge(*own())
                    nc.vector.reciprocal(y[:, 2 * g:2 * g + 2, 0:S], gg).then_inc(*up("normed", ("gate", i, g)))
                elif kind == "addgated":
                    dve.wait_ge(*at("weights_used", grp[-1]["s"]))
                    yy = y[:, 2 * g:2 * g + 2, 0:S]
                    dve.wait_ge(*own())
                    nc.vector.tensor_tensor(yy, A_, yy, ALU.mult).then_inc(*up("group_read_v", key))
                    hh_ = h[:, 2 * g:2 * g + 2, 0:S]
                    dve.wait_ge(*own())
                    nc.vector.tensor_tensor(hh_, hh_, yy, ALU.add).then_inc(*up("tiles_ready", (i, g)))
                elif kind in ("gated", "gated2"):
                    dve.wait_ge(*at("weights_used", grp[-1]["s"]))
                    src = A_
                    if kind == "gated2":
                        src = y[:, 2 * g:2 * g + 2, 0:T]
                        dve.wait_ge(*own())
                        nc.vector.tensor_tensor(src, A_, src, ALU.add).then_inc(*up("vector_step"))
                    l, which = p["mod"]
                    for j in range(2):
                        for s_, sl in segs(T):
                            k = 2 * g + j
                            dve.wait_ge(*own())
                            nc.vector.scalar_tensor_tensor(h[:, k, sl], src[:, j, sl], mod_at(l, which, k, s_), h[:, k, sl], ALU.mult, ALU.add).then_inc(
                                *up("group_read_v", key))
                elif kind == "poolw":
                    for t in range(4):
                        dve.wait_ge(*at("operand_high", (i, t)))
                        sc = vec[:, ROW["pool_scale_2"] + t:ROW["pool_scale_2"] + t + 1]
                        dve.wait_ge(*own())
                        nc.vector.scalar_tensor_tensor(ul[:, 4 + t, :], ps[:, t, :], sc, uh[:, 4 + t, :].bitcast(F32), ALU.mult, ALU.subtract).then_inc(
                            *up("group_read_v", key))
                elif kind == "conv" and g % 2 == 0:
                    l, f0 = p["l"], p["f0"]
                    ns = T // S
                    for j in range(2):
                        f = f0 + g + j
                        dve.wait_ge(*at("moved", (i, g, j)))
                        a = cacc[:, j, 0:T].rearrange("p (s c) -> p s c", s=ns)
                        x = A_[:, j, :].rearrange("p (s c) -> p s c", s=ns)
                        dve.wait_ge(*own())
                        nc.vector.scalar_tensor_tensor(a[:, :, 1:S], x[:, :, 0:S - 1], convv[:, l, f:f + 1], a[:, :, 1:S], ALU.mult, ALU.add).then_inc(
                            *up("vector_step"))
                        dve.wait_ge(*own())
                        nc.vector.scalar_tensor_tensor(a[:, :, 0:S - 1], x[:, :, 1:S], convv[:, l, 44 + f:45 + f], a[:, :, 0:S - 1], ALU.mult, ALU.add).then_inc(
                            *up("group_read_v", (i, g, j)))
                    C.note("group_read_v", key)
                    if g >= 2:
                        hidden_low_conv(p, g - 1)
                elif kind == "conv":
                    dve.wait_ge(*at("weights_used", grp[-1]["s"]))
                    for j in range(2):
                        dve.wait_ge(*at("gated_silu", (i, g - 1, j)))
                        dve.wait_ge(*own())
                        nc.vector.tensor_tensor(csil[:, j, 0:T], A_[:, j, :], csil[:, j, 0:T], ALU.mult).then_inc(
                            *up("group_read_v", (i, g, j)))
                    C.note("group_read_v", key)
                    if g == len(p["groups"]) - 1:
                        hidden_low_conv(p, g)

            pending = []
            swaps = [0]

            def rotate_pending():
                while pending:
                    q, g = pending.pop()
                    tile, _, cos, sin, r = rotation(q, g)
                    nt = tile.shape[1]
                    wide = lambda a: a[0:r, :].rearrange("p (o c) -> p o c", o=1).to_broadcast([r, nt, S])
                    tmp = work[0:r, 0, 0:nt, :]
                    dve.wait_ge(*at("swapped", swaps[0]))
                    dve.wait_ge(*own())
                    nc.vector.tensor_tensor(tmp, ps[0:r, 5, :].rearrange("p (t c) -> p t c", t=2)[:, 0:nt, :], wide(sin), ALU.mult).then_inc(
                        *up("vector_step"))
                    dve.wait_ge(*own())
                    nc.vector.tensor_tensor(tile, tile, wide(cos), ALU.mult).then_inc(*up("vector_step"))
                    dve.wait_ge(*own())
                    nc.vector.tensor_tensor(tile, tile, tmp, ALU.add).then_inc(*up("rotated", swaps[0]))
                    swaps[0] += 1

            def mod_keep(n):
                l, c = divmod(n, 12)
                dst = modc[:, l, 4 * c:4 * c + 4, :]
                dve.wait_ge(*at("mod_turned", n))
                for s_ in range(2):
                    dve.wait_ge(*own())
                    nc.vector.tensor_tensor(dst[:, :, s_], ps[:, 6 + n % 2, s_:8:2], bmod[:, l * 48 + 4 * c:l * 48 + 4 * c + 4], ALU.add).then_inc(
                        *up("vector_step"))
                dve.wait_ge(*own())
                nc.vector.tensor_scalar(dst, dst, 1.0 if c // 2 in (1, 4) else 0.0, None, ALU.add).then_inc(*up("mod_kept", n))

            for p in phases:
                kind, i = p["kind"], p["i"]
                if kind != "linear":
                    rotate_pending()
                    C.end("vector", i - 1)
                for sem, value in ended(i):
                    dve.wait_ge(sem, value)
                if kind == "init":
                    nc.vector.memset(small[:, :], EPS).then_inc(*up("vector_step"))
                    dve.wait_ge(loaded["pos"], 16)
                    dve.wait_ge(loaded["freq"], 16)
                    dve.wait_ge(*own())
                    nc.vector.tensor_copy(ang[:, :], posi[:, :]).then_inc(*up("vector_step"))
                    dve.wait_ge(*own())
                    nc.vector.tensor_scalar(ang[:, :], ang[:, :], freq[:, 0:1], None, ALU.mult).then_inc(*up("vector_step"))
                    magic = 12582912.0
                    c1 = 6.28125
                    c2 = float(np.float32(2 * np.pi - c1))
                    c3 = 2 * np.pi - c1 - c2
                    for n, off in enumerate((0.0, 0.25)):
                        t = turns[:, n, :]
                        dve.wait_ge(*own())
                        nc.vector.tensor_scalar(lnv[:, 0:S], ang[:, :], 1 / (2 * np.pi), off, ALU.mult, ALU.add).then_inc(
                            *up("vector_step"))
                        dve.wait_ge(*own())
                        nc.vector.tensor_scalar(lnv[:, 0:S], lnv[:, 0:S], magic, magic, ALU.add, ALU.subtract).then_inc(
                            *up("vector_step"))
                        dve.wait_ge(*own())
                        nc.vector.scalar_tensor_tensor(t, lnv[:, 0:S], -c1, ang[:, :], ALU.mult, ALU.add).then_inc(
                            *up("vector_step"))
                        dve.wait_ge(*own())
                        nc.vector.scalar_tensor_tensor(t, lnv[:, 0:S], -c2, t, ALU.mult, ALU.add).then_inc(
                            *up("vector_step"))
                        dve.wait_ge(*own())
                        nc.vector.scalar_tensor_tensor(t, lnv[:, 0:S], -c3, t, ALU.mult, ALU.add).then_inc(
                            *up("vector_step"))
                        dve.wait_ge(*own())
                        nc.vector.tensor_scalar(t, t, off * 2 * np.pi, 3.1415925, ALU.add, ALU.min).then_inc(
                            *up("vector_step"))
                        dve.wait_ge(*own())
                        nc.vector.tensor_scalar(t, t, -3.1415925, None, ALU.max).then_inc(*up("normed", "angles"))
                    dve.wait_ge(*at("weights_exp", "cond"))
                    dve.wait_ge(*own())
                    nc.vector.tensor_scalar(silu[:, :, :], silu[:, :, :], 1.0, None, ALU.add).then_inc(*up("vector_step"))
                    dve.wait_ge(*own())
                    nc.vector.reciprocal(silu[:, :, :], silu[:, :, :]).then_inc(*up("vector_step"))
                    for n, name in enumerate(("c_2", "c_ctx_2")):
                        dve.wait_ge(*own())
                        nc.vector.tensor_tensor(cc[:, :, n], vec[:, ROW[name]:ROW[name] + 8], silu[:, n, :], ALU.mult).then_inc(
                            *up("vector_step"))
                    dve.wait_ge(*at("turned_copied", ("x", 7)))
                    for s in range(SPLIT):
                        split_low(s)
                elif kind == "apply":
                    T = p["T"]
                    src = h if p["src"] == "h" else y
                    s0 = p.get("s0", 0)
                    if "mod" in p:
                        l, which = p["mod"]

                    def low(k):
                        c = p.get("dst") == "c"
                        k_ = s0 + k if c else k
                        dve.wait_ge(*at("operand_high", (i, k)))
                        if "mod" in p:
                            for s_, sl in segs(T):
                                dve.wait_ge(*own())
                                nc.vector.scalar_tensor_tensor(ul[:, k, sl], y[:, k, sl], mod_at(l, which, k, s_), uh[:, k, sl].bitcast(F32), ALU.add, ALU.subtract).then_inc(
                                    *up("operand_low", (i, k)))
                            return
                        dve.wait_ge(*own())
                        nc.vector.tensor_tensor((cl if c else ul)[:, k_, 0:T], y[:, s0 + k, 0:T], (ch if c else uh)[:, k_, 0:T].bitcast(F32), ALU.subtract).then_inc(
                            *up("operand_low", (i, k)))

                    for k in range(p["n"]):
                        d = y[:, s0 + k, 0:T]
                        if "gain" in p:
                            dve.wait_ge(*own())
                            nc.vector.scalar_tensor_tensor(d, src[:, s0 + k, 0:T], gain(p, k), rstd[:, 0:T], ALU.mult, ALU.mult).then_inc(
                                *up("normed", (i, k)))
                        else:
                            l, which = p["mod"]
                            for s_, sl in segs(T):
                                dve.wait_ge(*own())
                                nc.vector.scalar_tensor_tensor(y[:, k, sl], h[:, k, sl], mod_at(l, which + 1, k, s_), rstd[:, sl], ALU.mult, ALU.mult).then_inc(
                                    *up("normed", (i, k)))
                        if k >= 1:
                            low(k - 1)
                    low(p["n"] - 1)
                elif kind == "join":
                    for g in range(4):
                        for k in (2 * g, 2 * g + 1):
                            dve.wait_ge(*own())
                            nc.vector.scalar_tensor_tensor(y[:, k, 0:S], y[:, k, 0:S], gain(p, k), rstd[:, 0:S], ALU.mult, ALU.mult).then_inc(
                                *up("vector_step"))
                        hh_ = h[:, 2 * g:2 * g + 2, 0:S]
                        dve.wait_ge(*own())
                        nc.vector.tensor_tensor(hh_, hh_, y[:, 2 * g:2 * g + 2, 0:S], ALU.add).then_inc(
                            *up("tiles_ready", (i, g)))
                elif kind == "linear":
                    for grp in p["groups"]:
                        for c in grp[:-1]:
                            split_low(c["s"] + SPLIT)
                        evac(p, grp)
                        g = grp[0]["g"]
                        if g - 1 in p["mods"]:
                            mod_keep(p["mods"][g - 1][0])
                        split_low(grp[-1]["s"] + SPLIT)
                        rotate_pending()
                        if rotation(p, g):
                            pending.append((p, g))
                elif kind == "stick":
                    def fail(hd):
                        b = hd % 2
                        dve.wait_ge(*at("weights_exp", (i, hd)))
                        if hd >= 2:
                            dve.wait_ge(*at("fail_summed", (i, hd - 2)))
                        dve.wait_ge(*own())
                        nc.vector.scalar_tensor_tensor(sbf[:, b, :], ps[:, hd % 4, 0:384], 0.0, sbl[:, b, :], ALU.max, ALU.add).then_inc(
                            *up("vector_step"))
                        dve.wait_ge(*own())
                        f = sbf[:, b, :].rearrange("p (t c) -> p t c", t=3)[:, 0:3:2, :]
                        nc.vector.tensor_tensor(f, f, past2, ALU.mult).then_inc(*up("fail_ready", (i, hd)))

                    def mask(hd):
                        b = hd % 2
                        dve.wait_ge(*at("stick_weights", (i, hd)))
                        dve.wait_ge(*own())
                        a = sba[:, b, :].rearrange("p (t c) -> p t c", t=3)[:, 0:3:2, :]
                        nc.vector.scalar_tensor_tensor(a, a, 1.0, past2, ALU.min, ALU.mult).then_inc(*up("masked", (i, hd)))

                    def low(pair):
                        dve.wait_ge(*at("operand_high", (i, pair)))
                        dve.wait_ge(*own())
                        nc.vector.tensor_tensor(ul[:, pair, 0:S], ps[:, 4 + pair % 2, 0:S], uh[:, pair, 0:S].bitcast(F32), ALU.subtract).then_inc(
                            *up("operand_low", (i, pair)))

                    past2 = squares[:, 7:8, :].to_broadcast([P, 2, P])
                    fail(0)
                    for hd in range(HEADS):
                        if hd + 1 < HEADS:
                            fail(hd + 1)
                        mask(hd)
                        if hd % 2 == 1 and hd // 2 < len(p["mods"]):
                            mod_keep(p["mods"][hd // 2][0])
                        if hd % 2 == 0 and hd >= 2:
                            low(hd // 2 - 1)
                    low(HEADS // 2 - 1)
                elif kind == "rope":
                    dve.wait_ge(loaded["arena"], p["arena_value"])
                    for t, (tile, perm, c_, s_, r) in enumerate(rope_tiles(p["what"])):
                        dve.wait_ge(*at("swapped", (i, t)))
                        tmp = work[0:r, 0, 0, 0:S]
                        dve.wait_ge(*own())
                        nc.vector.tensor_tensor(tmp, ps[0:r, t % 2, 0:S], s_, ALU.mult).then_inc(*up("vector_step"))
                        dve.wait_ge(*own())
                        nc.vector.tensor_tensor(tile, tile, c_, ALU.mult).then_inc(*up("vector_step"))
                        dve.wait_ge(*own())
                        nc.vector.tensor_tensor(tile, tile, tmp, ALU.add).then_inc(*up("rotated", (i, t)))
                    if p["what"] == "mla":
                        src = kr[64:96, :]
                        for hd in range(8):
                            dve.wait_ge(*own())
                            nc.vector.tensor_copy(km[64:96, hd, :], src).then_inc(*up("vector_step"))
                elif kind == "softmax":
                    units = softmax_units(p["what"])
                    N = len(units)

                    def max_(u):
                        n, W, b = u["n"], u["W"], u["n"] % 2
                        dve.wait_ge(*at("scores", (i, n)))
                        if n >= 2:
                            dve.wait_ge(*at("weights_exp", (i, n - 2)))
                        if u["mask"] is not None:
                            for c0 in range(0, W, 512):
                                w = min(512, W - c0)
                                dve.wait_ge(*own())
                                nc.vector.tensor_tensor(sm[:, b, c0:c0 + w], ps[:, b * 2 + c0 // 512, 0:w], masks[:, u["mask"] + c0:u["mask"] + c0 + w], ALU.add).then_inc(
                                    *up("vector_step"))
                            src = sm[:, b, 0:W]
                        else:
                            src = ps[:, n % 4, 0:W]
                        dve.wait_ge(*own())
                        nc.vector.tensor_reduce(small[:, 4 + b:5 + b], src, AX.X, ALU.max).then_inc(*up("vector_step"))
                        dve.wait_ge(*own())
                        nc.vector.tensor_scalar(small[:, b:b + 1], small[:, 4 + b:5 + b], -u["scale"], None, ALU.mult).then_inc(
                            *up("max_ready", (i, n)))

                    def norm_(u):
                        n, W, b = u["n"], u["W"], u["n"] % 2
                        dve.wait_ge(*at("weights_exp", (i, n)))
                        dve.wait_ge(*own())
                        nc.vector.reciprocal(small[:, 6 + b:7 + b], small[:, 2 + b:3 + b]).then_inc(*up("vector_step"))
                        dve.wait_ge(*own())
                        nc.vector.tensor_scalar(pr[:, b, 0:W], pr[:, b, 0:W], small[:, 6 + b:7 + b], None, ALU.mult).then_inc(
                            *up("weights_normed", (i, n)))

                    def low_(u):
                        t0 = u["col"] - u["q"] * P
                        dve.wait_ge(*at("operand_high", (i, u["pair"])))
                        dve.wait_ge(*own())
                        nc.vector.tensor_tensor(ul[:, u["opair"], t0:t0 + S], ps[:, 6 + u["pair"] % 2, 0:S], uh[:, u["opair"], t0:t0 + S].bitcast(F32), ALU.subtract).then_inc(
                            *up("operand_low", (i, u["pair"])))

                    if units[0]["mask"] is not None:
                        dve.wait_ge(loaded["arena"], p["arena_value"])
                    max_(units[0])
                    for n in range(N):
                        if n + 1 < N:
                            max_(units[n + 1])
                        norm_(units[n])
                        if n >= 1 and units[n - 1]["ends"]:
                            low_(units[n - 1])
                    low_(units[N - 1])
                elif kind == "ple":
                    dve.wait_ge(*at("operand_high", (i, 0)))
                    dve.wait_ge(*own())
                    nc.vector.tensor_tensor(pl_[:, :, :], ps[:, 4, :].rearrange("p (k c) -> p k c", k=2), ph_[:, :, :].bitcast(F32), ALU.subtract).then_inc(
                        *up("operand_low", (i, 0)))
                elif kind == "pool":
                    dve.wait_ge(loaded["arena"], p["arena_value"])
                    L = S + 2 * PAD
                    dve.wait_ge(*own())
                    nc.vector.memset(pbuf[:, :, :, 0:PAD], 0.0).then_inc(*up("vector_step"))
                    dve.wait_ge(*own())
                    nc.vector.memset(pbuf[:, :, :, PAD + S:L], 0.0).then_inc(*up("vector_step"))
                    dve.wait_ge(*own())
                    nc.vector.tensor_tensor(abuf[:, :, :, 0:L - 1], pbuf[:, :, :, 0:L - 1], pbuf[:, :, :, 1:L], ALU.add).then_inc(
                        *up("vector_step"))
                    for n, w in enumerate((2, 4, 8)):
                        end = L - 2 * w + 1
                        dve.wait_ge(*own())
                        nc.vector.tensor_tensor(abuf[:, n + 1:4, :, 0:end], abuf[:, n + 1:4, :, 0:end], abuf[:, n + 1:4, :, w:w + end], ALU.add).then_inc(
                            *up("vector_step"))
                    for g, w in enumerate(POOL_W):
                        for s_, sl in segs(T2):
                            a = abuf[:, g, s_, PAD - w // 2:PAD - w // 2 + S]
                            dve.wait_ge(*own())
                            nc.vector.tensor_tensor(a, a, rcount[:, g, :], ALU.mult).then_inc(*up("vector_step"))
                            dve.wait_ge(*own())
                            nc.vector.tensor_tensor(pdif[:, g, sl], a, pbuf[:, g, s_, PAD:PAD + S], ALU.subtract).then_inc(
                                *up("normed", (i, 0)))
                    dve.wait_ge(*at("operand_high", (i, 0)))
                    dve.wait_ge(*own())
                    nc.vector.tensor_tensor(ul[:, 0:4, :], pdif[:, :, :], uh[:, 0:4, :].bitcast(F32), ALU.subtract).then_inc(
                        *up("operand_low", (i, 0)))
                elif kind == "qknorm":
                    for name, row in (("q", "gqa_g_q"), ("k", "gqa_g_k")):
                        t, r = (qg[:, :, :], y[:, 0:4, :].rearrange("p b (t c) -> p (b t) c", t=2)) if name == "q" else (kg[:, :, :], y[:, 4:6, :])
                        dve.wait_ge(*at("rstd_ready", (i, name)))
                        dve.wait_ge(*own())
                        nc.vector.scalar_tensor_tensor(t, t, vec[:, ROW[row]:ROW[row] + 1], r, ALU.mult, ALU.mult).then_inc(
                            *up("normed", (i, name)))
                elif kind == "final":
                    for k in range(8):
                        c = ROW["g_final_2"] + k
                        dve.wait_ge(*own())
                        nc.vector.scalar_tensor_tensor(y[:, k, 0:S], h[:, k, 0:S], vec[:, c:c + 1], rstd[:, 0:S], ALU.mult, ALU.mult).then_inc(
                            *up("normed", (i, k)))
                C.end("vector", i)
    return C


def kernel(**inputs):
    import concourse.bacc as bacc
    from concourse.bass_utils import run_bass_kernel_spmd as run

    skip = {"w_in_dsa", "w_out_dsa", "w_in_moba", "w_out_moba"}
    arrays = {n: np.ascontiguousarray(a) for n, a in inputs.items() if n not in skip}
    arrays.update(constants())

    def program(noted):
        nc = bacc.Bacc("TRN2", target_bir_lowering=False, num_devices=1, dynamic_dma_scratch_size=1024)
        A = {n: nc.dram_tensor("in_" + n, a.shape, mybir.dt.from_np(a.dtype), kind="ExternalInput").ap()
             for n, a in arrays.items()}
        out = nc.dram_tensor("out", (1, S, D), F32, kind="ExternalOutput").ap()
        return nc, build(nc, A, out, noted, STOP)

    noted = program(None)[1].seen
    nc, _ = program(noted)
    r = run(nc, [{"in_" + n: a for n, a in arrays.items()}], core_ids=[0])
    return r.results[0]["out"]
```

```python
from contextlib import ExitStack

import concourse.bass as bass
import numpy as np
from concourse import mybir

F32 = mybir.dt.float32
F32R = mybir.dt.float32r
I32 = mybir.dt.int32
ALU = mybir.AluOpType
ACT = mybir.ActivationFunctionType
AX = mybir.AxisListType

P = 128
D = 1024
S = 256
T2 = 2 * S
KD = D // P
EPS = 1e-6
DFF = 4096
DFF2 = 2816
KF2 = DFF2 // P
HEADS, HD = 16, 64
DIL = (1, 4, 16)
DIL_BACK = 128
MLA_HEADS, MLA_NOPE, MLA_ROPE = 8, 64, 32
MLA_HD = MLA_NOPE + MLA_ROPE
GQA_HEADS, GQA_KV = 8, 2
POOL_W = (2, 4, 8, 16)
PAD = 16
SLOT = 2048
RAW = 3
SPLIT = 3
NEG = -1.0e30
STOP = None


def constants():
    i = np.arange(P)
    ident = np.eye(P)
    ones = np.ones((P, P))
    negtri = -(i[:, None] >= i[None, :]).astype(float)
    perm1 = np.zeros((P, P))
    for base in (0, 64):
        for j in range(8):
            perm1[base + j + 8, base + j] = -1.0
            perm1[base + j, base + j + 8] = 1.0
    perm_g = np.zeros((P, P))
    for j in range(0, P, 2):
        perm_g[j + 1, j] = -1.0
        perm_g[j, j + 1] = 1.0
    perm_m = np.zeros((P, P))
    perm_m[MLA_NOPE:MLA_HD, MLA_NOPE:MLA_HD] = perm_g[:MLA_ROPE, :MLA_ROPE]
    past = (i[:, None] < i[None, :]).astype(float)
    select = np.zeros((P, P))
    for q in range(4):
        select[32 * q, 0] = select[32 * q + 1, 1] = 1.0
    squares = np.concatenate([ident, ones, negtri, -ones, perm1, perm_m, perm_g, past, select], axis=1)

    freq = np.zeros((P, 1))
    for base in (0, 64):
        freq[base:base + 16, 0] = 500000.0 ** (-np.tile(np.arange(8), 2) / 8.0)

    def axial(dim):
        t = np.arange(S)
        f = 10000.0 ** (-np.arange(dim // 4) / (dim // 4))
        ang = np.concatenate([(t // 64)[:, None] * f, (t % 64)[:, None] * f], axis=-1)
        return np.repeat(np.cos(ang).T, 2, axis=0), np.repeat(np.sin(ang).T, 2, axis=0)

    cm, sm = np.ones((P, S)), np.zeros((P, S))
    cm[MLA_NOPE:MLA_HD], sm[MLA_NOPE:MLA_HD] = axial(MLA_ROPE)
    cg, sg = axial(P)
    t = np.arange(S)
    count = [np.clip(t - w // 2 + w, 0, S) - np.clip(t - w // 2, 0, S) for w in POOL_W]
    rcount = np.broadcast_to((1.0 / np.stack(count)).reshape(1, -1), (P, 4 * S))
    def band(q0, nk):
        q = q0 + i[:, None]
        k = np.arange(nk)[None, :]
        return [np.where((k <= q) & ((q - k) % d == 0) & (q - k <= DIL_BACK * d), 0.0, NEG) for d in DIL]
    masks = np.concatenate(band(0, P) + band(P, 2 * P), axis=1)
    rope2 = np.concatenate([cm, sm, cg, sg], axis=1)
    return {k: np.ascontiguousarray(v, dtype=np.float32) for k, v in dict(
        const_squares=squares, const_freq=freq, const_rope2=rope2, const_rcount=rcount, const_masks=masks).items()}


class Counting:

    def __init__(self, noted):
        self.noted, self.seen, self.count, self.engine, self.sems = noted, {}, {}, {}, {}
        self.last = {}

    def raised(self, engine, family, key=None, by=1):
        assert self.engine.setdefault(family, engine) == engine, family
        self.count[family] = self.count.get(family, 0) + by
        self.seen[family, key] = self.count[family]
        self.last[engine] = (family, self.count[family])
        return by

    def note(self, family, key):
        self.seen[family, key] = self.count[family]

    def end(self, engine, i):
        self.seen["end", (engine, i)] = self.last.get(engine)

    def after(self, family, key=None):
        return self.noted[family, key] if self.noted else 1

    def after_phase(self, engine, i):
        last = self.noted["end", (engine, i)] if self.noted else None
        return (self.sems[last[0]], last[1]) if last else None


FAMILIES = """weights_high weights_low weights_used scalar_step vector_step
 group_read_s group_read_v operand_high operand_low stat_squares stat_summed rstd_ready
 normed moved rotated swapped scores weights_exp weights_normed turned turned_copied attended
 max_ready fail_ready fail_summed stick_weights masked mod_rows mod_turned mod_kept gated_silu tiles_ready squares_folded""".split()


def build(nc, A, out, noted, dry_stop=None):
    C = Counting(noted)
    with ExitStack() as ctx:
        for f in FAMILIES:
            C.sems[f] = ctx.enter_context(nc.semaphore(f))
        landed = [ctx.enter_context(nc.semaphore(f"landed{i}")) for i in range(RAW)]
        loaded = {n: ctx.enter_context(nc.semaphore(f"loaded_{n}")) for n in ("squares", "rows", "freq", "pos", "x", "arena", "p")}
        stored = ctx.enter_context(nc.semaphore("stored"))

        def sb(name, shape, dt=F32):
            return ctx.enter_context(nc.sbuf_tensor(name, shape, dt))

        HH0 = -(-nc.sbuf_base // 32) * 32
        hh = sb("hh", [P, 8192], F32R)
        hl = sb("hl", [P, 8192], F32R)
        raw = sb("raw", [P, RAW, SLOT])
        whi = sb("whi", [P, SPLIT, SLOT], F32R)
        wlo = sb("wlo", [P, SPLIT, SLOT], F32R)
        h = sb("h", [P, KD, T2])
        uh = sb("uh", [P, KD, T2], F32R)
        ul = sb("ul", [P, KD, T2], F32R)
        y = sb("y", [P, KD, T2])
        squares = sb("squares", [P, 9, P])
        sq = sb("sq", [P, 2, T2])
        lnv = sb("lnv", [P, T2])
        rstd = sb("rstd", [P, T2])
        cos1 = sb("cos1", [P, S])
        sin1 = sb("sin1", [P, S])
        freq = sb("freq", [P, 1])
        vec = sb("vec", [P, P])
        convv = sb("convv", [P, 2, 96])
        bmod = sb("bmod", [P, 96])
        modc = sb("modc", [P, 2, 48, 2])
        silu = sb("silu", [P, 2, KD])
        cc = sb("cc", [P, KD, 2])
        small = sb("small", [P, 64])
        ident, ones, negtri, negones, perm1, perm_m, perm_g, past, select = (squares[:, j, :] for j in range(9))
        select = select[:, 0:2]
        ps = ctx.enter_context(nc.psum_tensor("ps", [P, 8, 512], F32))


        def arena(name, shape, off, dt=F32):
            n = int(np.prod(shape[1:])) * 4
            assert off + n <= 65536, (name, off + n)
            return nc.alloc_sbuf_tensor_at(name, shape, dt, offset=HH0 + off)

        K = 1024
        rows = arena("rows", [P, 4, P], 0)
        xin = arena("xin", [P, 4, D], 4 * K)
        posi = arena("posi", [P, S], 20 * K, I32)
        ang = arena("ang", [P, S], 21 * K)
        turns = arena("turns", [P, 2, S], 22 * K)
        q1 = arena("q1", [P, 8, S], 0)
        k1 = arena("k1", [P, 8, S], 8 * K)
        v1 = arena("v1", [P, 2, D], 16 * K)
        sbt = arena("sbt", [P, 2, 384], 24 * K)
        sbe = arena("sbe", [P, 2, 384], 27 * K)
        sbl = arena("sbl", [P, 2, 384], 30 * K)
        sbf = arena("sbf", [P, 2, 384], 33 * K)
        sba = arena("sba", [P, 2, 384], 36 * K)
        qk2 = arena("qk2", [P, 24, S], 0)
        v2 = arena("v2", [P, 2, 3 * 512], 24 * K)
        masks = arena("masks", [P, 1152], 36 * K)
        sm = arena("sm", [P, 2, 768], 41 * K)
        pr = arena("pr", [P, 2, 768], 47 * K)
        pt = arena("pt", [P, 2, 768], 53 * K)
        pbuf = arena("pbuf", [P, 4, 2, S + 2 * PAD], 0)
        abuf = arena("abuf", [P, 4, 2, S + 2 * PAD], 10 * K)
        csq = arena("csq", [P, 5, T2], 0)
        rcount = arena("rcount", [P, 4, S], 20 * K)
        pdif = arena("pdif", [P, 4, T2], 24 * K)
        qm = arena("qm", [P, 8, T2], 0)
        km = arena("km", [P, 8, T2], 16 * K)
        vm = arena("vm", [P, 4, 512], 32 * K)
        kr = arena("kr", [P, T2], 62 * K)
        ropem = arena("ropem", [P, 2, S], 40 * K)
        ch = arena("ch", [P, 5, T2], 42 * K, F32R)
        cl = arena("cl", [P, 5, T2], 52 * K, F32R)
        qg = arena("qg", [P, 8, S], 0)
        kg = arena("kg", [P, 2, T2], 8 * K)
        vg = arena("vg", [P, 4, S], 12 * K)
        ropeg = arena("ropeg", [P, 2, S], 16 * K)
        pin = arena("pin", [P, 2, S], 0)
        ph_ = arena("ph", [P, 2, S], 2 * K, F32R)
        pl_ = arena("pl", [P, 2, S], 4 * K, F32R)
        ge = arena("ge", [P, 2, 2, S], 8 * K)
        work = sb("work", [P, 2, 2, S])
        modrow = lnv[:, :]
        cacc = arena("cacc", [P, 2, 512], 24 * K)
        csil = arena("csil", [P, 2, 512], 28 * K)

        def hid(buf, t, T):
            return buf[:, t * T:(t + 1) * T]

        chunks = []
        phases = []

        def linear(name, W, nk, cols, T, kind, mode="T", m=P, xin=("u", 0), kmax=8, tok0=0, k0=0, split=True, last=None):
            job = dict(kind="linear", name=name, evac=kind, T=T, mode=mode, m=m, x=xin, tok0=tok0, groups=[])
            for g, (c0, nc_) in enumerate(cols):
                grp = []
                nparts = -(-nk // kmax)
                sizes = [nk // nparts + (1 if i < nk % nparts else 0) for i in range(nparts)]
                a = 0
                for kn in sizes:
                    ck = dict(job=job, g=g, k=a, kn=kn, C=nc_, src=W[(k0 + a) * P:(k0 + a + kn) * P, c0:c0 + nc_],
                              r=len(chunks), first=a == 0, last=a + kn == nk)
                    assert kn * nc_ <= SLOT
                    chunks.append(ck)
                    grp.append(ck)
                    a += kn
                job["groups"].append(grp)
            phases.append(job)
            return job

        def phase(kind, **kw):
            phases.append(dict(kind=kind, **kw))

        def pairs(c0, n, w=256):
            return [(c0 + j, w) for j in range(0, n, w)]

        phase("init")
        for l in range(2):
            if l == 0:
                phase("stats", src="h", n=8, T=S, D=D)
            phase("apply", src="h", n=8, T=S, gain=("g_mix_pre", l))
            if l == 0:
                Wi = A["w_in_sb"][0]
                linear("stick_qk", Wi, 8, pairs(0, 2 * D), S, "qk1")
                linear("stick_v", Wi, 8, pairs(2 * D, D), S, "v", mode="V")
                phase("stick", n_mods=7)
                linear("stick_out", A["w_out_sb"][0], 8, pairs(0, D), S, "y")
            else:
                Wi = A["w_in_dil"][0]
                for g in range(3):
                    linear(f"dil_qk{g}", Wi, 8, pairs(g * 1536, 1024), S, "qk2")
                    linear(f"dil_v{g}", Wi, 8, pairs(g * 1536 + 1024, 512), S, "v", mode="V")
                phase("softmax", what="dil")
                linear("dil_out", A["w_out_dil"][0], 4, pairs(0, D), S, "y")
            phases[-1].update(stat="y")
            phase("join", T=S, stat="h", gain=("g_mix_post", l))
            phase("apply", src="h", n=8, T=S, gain=("g_ffn_pre", l))
            linear(f"ff_in{l}", A["w_ff_in"][l], 8, pairs(0, DFF), S, "relu2")
            linear(f"ff_out{l}", A["w_ff_out"][l], 32, pairs(0, D), S, "y", xin=("h", 0))
            phases[-1].update(stat="y")
            phase("join", T=S, stat="h", gain=("g_ffn_post", l))
            phase("apply", src="h", n=8, T=S, gain=("g_ple", l))
            linear(f"gate{l}", A["w_ple_gate"][l], 8, pairs(0, D), S, "gate")
            linear(f"ple{l}", A["w_ple"][l], 2, pairs(0, D), S, "addgated", xin=("p", 0))
            phases[-1].update(stat="h")
        for l in range(2):
            Tt = T2 if l == 0 else S
            if l == 0:
                phase("stats", src="h", n=8, T=T2, D=D)
            phase("apply", src="h", n=8, T=T2, mod=(l, 0))
            if l == 0:
                Wi = A["mix0_w_in_2"][0]
                linear("mix_p", Wi, 8, pairs(672, 512), T2, "mixp")
                linear("mix_c", Wi, 8, [(0, 256), (256, 256), (512, 160)], T2, "mixc")
                phase("cnorm")
                linear("uq", A["mla_w_uq_2"][0], 3, pairs(0, 768, 192), T2, "uq", m=96, xin=("c", 0))
                linear("uk", A["mla_w_uk_2"][0], 2, pairs(0, 512), T2, "uk", xin=("c", 3))
                linear("uv", A["mla_w_uv_2"][0], 2, pairs(0, 512), T2, "v", mode="V", xin=("c", 3))
                linear("pool_w", A["pool_w_2"][0].rearrange("g i o -> (g i) o"), 4, [(0, P)], T2, "poolw", xin=("u", 0))
                phase("softmax", what="mla")
                linear("mix_out", A["mix0_w_out_2"][0], 8, pairs(0, D), T2, "gated", last=(0, 2))
                phases[-1].update(mod=(0, 2), stat="h")
            else:
                Wi = A["gqa_w_in_2"][0]
                linear("gqa_q", Wi, 8, pairs(0, D), S, "qg")
                linear("gqa_k", Wi, 8, pairs(D, 256), T2, "kg")
                linear("gqa_v", Wi, 8, pairs(D + 256, 256), T2, "v", mode="V")
                phase("softmax", what="gqa")
                linear("gqa_out", A["gqa_w_out_2"][0], 8, pairs(0, D), S, "gated")
                phases[-1].update(mod=(1, 2), stat="h")
            phase("apply", src="h", n=8, T=Tt, mod=(l, 3))
            Wu, Wd = A["ffn_w_up_2"][l], A["ffn_w_down_2"][l]
            halves = [(0, 12), (12, 10)] if l == 0 else [(0, 22)]
            for n, (f0, nf) in enumerate(halves):
                cols = [c for j in range(nf // 2) for c in ((f0 * P + j * 256, 256), (DFF2 + f0 * P + j * 256, 256))]
                linear(f"up{l}{n}", Wu, 8, cols, Tt, "conv")
                phases[-1].update(l=l, f0=f0)
                only = "gated" if len(halves) == 1 else ("y" if n == 0 else "gated2")
                linear(f"down{l}{n}", Wd, nf, pairs(0, D), Tt, only, xin=("h", 0), k0=f0)
                phases[-1]["mod"] = (l, 5)
            phases[-1]["stat"] = "h"
        phase("final")
        if dry_stop is not None:
            phases[:] = phases[:dry_stop]
            live = {id(p) for p in phases}
            chunks[:] = [c for c in chunks if id(c["job"]) in live]
            phase("dump")
        for i, p in enumerate(phases):
            p["i"] = i
        mod_after = dict(stick_qk=(4,), ff_in0=(2, 7, 12), ff_out0=(0, 1, 2), gate0=(1,), dil_qk0=(1,), dil_qk1=(1,),
                         dil_qk2=(1,), ff_in1=(2, 7, 12), ff_out1=(0, 1, 2))
        own_chunks, behind, mod_n = [], {}, 0
        for p in phases:
            p["mods"] = {}
            places = range(p["n_mods"]) if "n_mods" in p else mod_after.get(p.get("name"), ())
            for g, grp in enumerate(p.get("groups", [()])):
                own_chunks += grp
                for place in places:
                    if "groups" in p and place != g:
                        continue
                    l, c = divmod(mod_n, 12)
                    pair = [dict(job=p, mod=(l, c, half), kn=4, C=512,
                                 src=A["w_mod_2"][l][half * 512:(half + 1) * 512, c * 512:(c + 1) * 512]) for half in range(2)]
                    behind.setdefault(len(own_chunks) + SPLIT - (2 if "groups" in p else 1), []).extend(pair)
                    p["mods"][place] = (mod_n, pair)
                    mod_n += 1
        assert mod_n == 24 or dry_stop is not None
        order = []
        for n, c in enumerate(own_chunks):
            order += [c] + behind.get(n, [])
        chunks = order
        n_split = 0
        for r, c in enumerate(chunks):
            c["r"] = r
            if "mod" not in c:
                c["s"] = n_split
                n_split += 1
        splits = [c for c in chunks if "s" in c]

        for p in phases:
            before = phases[p["i"] - 1] if p["i"] else None
            p["barrier"] = True
            if p["kind"] != "linear":
                continue
            p["fed"] = None
            if before["kind"] == "apply" and before.get("dst") != "c":
                p["fed"] = lambda k, b=before["i"]: (b, k)
                p["barrier"] = False
            elif p["name"] == "pool_w":
                p["barrier"] = False
            elif p["evac"] == "addgated":
                p["fed"] = lambda k, b=before["i"]: (b, "p")
                p["barrier"] = False
            elif p["name"] == "uq":
                p["fed"] = lambda k, b=before["i"]: (b, k)
                p["barrier"] = False
            elif p["name"] == "uk":
                p["fed"] = lambda k, b=before["i"] - 1: (b, 3 + k)
                p["barrier"] = False
            elif p["name"] == "uv":
                p["barrier"] = False
            elif before["kind"] == "linear" and before["evac"] == "relu2":
                p["fed"] = lambda k, b=before["i"]: (b, k // 2)
                p["barrier"] = False
            elif before["kind"] == "linear" and before["evac"] == "conv":
                p["fed"] = lambda k, b=before["i"]: (b, k // 2 * 2 + 1, k % 2)
                p["barrier"] = False
            elif before["kind"] == "linear" and p["x"][0] == "u" and not before.get("stat"):
                p["barrier"] = False
        gi = 0
        for p in phases:
            if p["kind"] == "linear":
                for g in p["groups"]:
                    for c in g:
                        c["gi"] = gi
                    gi += 1
        VREADS = {"y", "gated", "gated2", "addgated", "conv", "poolw"}
        group_sem = {}
        for p in phases:
            if p["kind"] == "linear":
                for g in p["groups"]:
                    group_sem[g[0]["gi"]] = "group_read_v" if p["evac"] in VREADS else "group_read_s"

        def late_splits(p):
            if p["kind"] != "linear" or phases[p["i"] + 1]["kind"] in ("linear", "final", "dump") or phases[p["i"] + 1]["mods"]:
                return [], []
            s = p["groups"][-1][-1]["s"]
            return ([s + 1], [s + 2, s + SPLIT]) if p["name"] == "dil_out" or p["evac"] == "addgated" else ([], [s + SPLIT])

        def waiting_splits(i):
            if phases[i]["kind"] == "linear" or i + 1 >= len(phases) or phases[i + 1]["kind"] != "linear":
                return []
            while i >= 0 and phases[i]["kind"] != "linear":
                i -= 1
            return late_splits(phases[i])[1] if i >= 0 else []

        def tokens(p):
            return slice(p.get("tok0", 0), p.get("tok0", 0) + p["T"])

        def gain(p, k):
            name, l = p["gain"]
            c = ROW[name] + (l * 8 if name.startswith("g_") else 0) + k
            return vec[:, c:c + 1]

        ROW = {}
        at_row = 0
        for name, n in (("g_mix_pre", 16), ("g_mix_post", 16), ("g_ffn_pre", 16), ("g_ffn_post", 16), ("g_ple", 16),
                        ("g_final_2", 8), ("mla_g_q", 3), ("mla_g_kv", 2), ("pool_scale_2", 4), ("gqa_g_q", 1),
                        ("gqa_g_k", 1), ("c_2", 8), ("c_ctx_2", 8)):
            ROW[name] = at_row
            at_row += n

        def mod_at(l, which, k, seg):
            return modc[:, l, which * 8 + k, seg:seg + 1]

        def operand(p, k, T, hi):
            name, off = p["x"]
            t = tokens(p)
            if name == "u":
                return (uh if hi else ul)[:, off + k, t]
            if name == "h":
                return hid(hh if hi else hl, off + k, T)
            if name == "c":
                return (ch if hi else cl)[:, off + k, t]
            return (ph_ if hi else pl_)[:, k, :]

        def acc(g, T, cols=None):
            b = (g["gi"] % 2) * 2
            return ps[:, b:b + 2, 0:T]

        def segs(T):
            return [(s, slice(s * S, (s + 1) * S)) for s in range(T // S)]

        def softmax_units(what):
            units = []
            if what == "dil":
                for pair in range(4):
                    for q in range(2):
                        for hd in (2 * pair, 2 * pair + 1):
                            nk = q + 1
                            o = (hd % 2) * 64
                            prod = []
                            for g in range(3):
                                prod.append((qk2[o:o + 64, g * 8 + hd // 2, q * P:(q + 1) * P],
                                             qk2[o:o + 64, g * 8 + 4 + hd // 2, 0:nk * P], g * nk * P))
                            vals = [v2[:, kt, g * 512 + hd * 64:g * 512 + hd * 64 + 64] for g in range(3) for kt in range(nk)]
                            units.append(dict(prod=prod, W=3 * nk * P, mask=(0 if q == 0 else 384), vals=vals,
                                              scale=HD ** -0.5, rows=(o, o + 64), pair=pair, q=q, opair=pair, col=q * P))
            if what == "mla":
                n = 0
                for seg in (1, 0):
                    for pair in range(4):
                        for q in range(2):
                            for hd in (2 * pair, 2 * pair + 1):
                                o = (hd % 2) * 64
                                keys = [(S, T2)] if seg == 1 else [(0, T2)]
                                a, b = keys[0]
                                t0 = seg * S + q * P
                                prod = [(qm[0:96, hd, t0:t0 + P], km[0:96, hd, a:b], 0)]
                                vals = [vm[:, kt, hd * 64:(hd + 1) * 64] for kt in range(a // P, b // P)]
                                units.append(dict(prod=prod, W=b - a, mask=None, vals=vals, scale=MLA_HD ** -0.5,
                                                  rows=(o, o + 64), pair=n, opair=pair, q=q, col=t0))
                        n += 1
            if what == "gqa":
                for hd in range(8):
                    for q in range(2):
                        kv = hd // 4
                        prod = [(qg[:, hd, q * P:(q + 1) * P], kg[:, kv, :], 0)]
                        vals = [vg[:, kt, kv * P:(kv + 1) * P] for kt in range(4)]
                        units.append(dict(prod=prod, W=T2, mask=None, vals=vals, scale=P ** -0.5, rows=(0, P),
                                          pair=hd, opair=hd, q=q, col=q * P))
            for n, u in enumerate(units):
                u["n"] = n
                u["ends"] = n + 1 == len(units) or units[n + 1]["pair"] != u["pair"]
            return units

        def rotation(p, g):
            if p["evac"] == "qk2":
                t = int(p["name"][-1]) * 8 + 2 * g
                return qk2[:, t:t + 2, :], perm1, cos1, sin1, P
            r = MLA_HD
            if p["evac"] == "mixc" and g == 2:
                return kr[0:r, :].rearrange("p (t c) -> p t c", t=2)[:, 0:1, :], perm_m[0:r, 0:r], ropem[:, 0, :], ropem[:, 1, :], r
            if p["evac"] == "uq":
                return qm[0:r, 2 * g:2 * g + 2, 0:S], perm_m[0:r, 0:r], ropem[:, 0, :], ropem[:, 1, :], r
            if p["evac"] == "qg":
                return qg[:, 2 * g:2 * g + 2, :], perm_g, ropeg[:, 0, :], ropeg[:, 1, :], P
            if p["evac"] == "kg":
                return kg[:, :, 0:S], perm_g, ropeg[:, 0, :], ropeg[:, 1, :], P
            return None

        def at(family, key=None):
            return C.sems[family], C.after(family, key)

        def ended(i):
            return [v for v in (C.after_phase(e, i - 1) for e in ENGINES) if v] if i and phases[i]["barrier"] else []

        ENGINES = ("tensor", "scalar", "vector")

        block = ctx.enter_context(nc.Block())

        @block.sync
        def _(sp):
            with nc.allow_non_contiguous_dma(reason="small"):
                sp.dma_start(squares[:, :, :], A["const_squares"].rearrange("p (j c) -> p j c", j=9)).then_inc(loaded["squares"], 16)
                sp.dma_start(freq[:, :], A["const_freq"]).then_inc(loaded["freq"], 16)
                sp.dma_start(posi[:, :], A["positions"].to_broadcast([P, S])).then_inc(loaded["pos"], 16)
                row = lambda ap: ap.rearrange("a (k p) -> (a k) p", p=P)
                r0 = 0
                for name in ("g_mix_pre", "g_mix_post", "g_ffn_pre", "g_ffn_post", "g_ple", "g_final_2", "mla_g_q_2",
                             "mla_g_kv_2", "pool_scale_2", "gqa_g_q_2", "gqa_g_k_2", "c_2", "c_ctx_2"):
                    ap = A[name]
                    ap = row(ap) if len(ap.shape) == 2 else ap.rearrange("(k p) -> k p", p=P)
                    sp.dma_start(rows[r0:r0 + ap.shape[0], 0, :], ap).then_inc(loaded["rows"], 16)
                    r0 += ap.shape[0]
                for l in range(2):
                    sp.dma_start(rows[0:66, 1 + l, :], A["ffn_conv_w_2"][l].rearrange("j (k p) -> (j k) p", p=P)).then_inc(loaded["rows"], 16)
                    sp.dma_start(rows[66:88, 1 + l, :], A["ffn_conv_b_2"][l:l + 1].rearrange("a (k p) -> (a k) p", p=P)).then_inc(loaded["rows"], 16)
                sp.dma_start(rows[0:96, 3, :], row(A["b_mod_2"])).then_inc(loaded["rows"], 16)
                for c in chunks:
                    r = c["r"]
                    if r >= RAW:
                        o = chunks[r - RAW]
                        if "s" in o:
                            sp.wait_ge(*at("weights_low", o["s"]))
                        else:
                            sp.wait_ge(*at("weights_used", ("mod", o["r"])))
                    dst = raw[:, r % RAW, 0:c["kn"] * c["C"]].rearrange("p (k c) -> p k c", k=c["kn"])
                    sp.dma_start(dst, c["src"].rearrange("(k p) c -> p k c", p=P)).then_inc(landed[r % RAW], 16)
                sp.wait_ge(*at("turned_copied", (phases[-1]["i"], 7)))
                for t in range(2):
                    sp.dma_start(out[0].rearrange("(t p) d -> p t d", p=P)[:, t, :], xin[:, t, :]).then_inc(stored, 16)
                sp.wait_ge(stored, 32)

        n_arena = [0]
        for p in phases:
            if p.get("name") == "dil_qk0":
                p["loads"] = [(masks[:, :], A["const_masks"])]
            if p.get("name") == "gqa_q":
                p["loads"] = [(ropeg[:, :, :], A["const_rope2"][:, 2 * S:].rearrange("p (j c) -> p j c", j=2))]
            if p.get("name") == "mix_p":
                p["loads"] = [(rcount[:, :, :], A["const_rcount"].rearrange("p (g c) -> p g c", g=4))] + [(ropem[:, :, :], A["const_rope2"][:, 0:2 * S].rearrange("p (j c) -> p j c", j=2))]
            if p.get("name", "").startswith("gate"):
                p["loads"] = [(pin[:, :, :], A["p"][int(p["name"][4:]), 0].rearrange("(t p) d -> p t d", p=P))]
            for _ in p.get("loads", ()):
                n_arena[0] += 1
            p["arena_value"] = 16 * n_arena[0]

        @block.tensor
        def _(pe):
            def up(family, key=None):
                return C.sems[family], C.raised("tensor", family, key)


            def mm(out_, lhsT, rhs, start, stop):
                return pe.matmul(out_, lhsT, rhs, start=start, stop=stop, skip_group_check=True)

            def square_sums(p, g):
                T, last_g = p["T"], 3
                pe.wait_ge(*at("stat_squares", (p["i"], g)))
                for j in range(2):
                    sq_ = sq[:, g % 2, j * S:(j + 1) * S] if T == S else sq[:, j, :]
                    last = mm(ps[:, 4, 0:T], ones, sq_, g == 0 and j == 0, g == last_g and j == 1)
                last.then_inc(*up("stat_summed", (p["i"], g)))

            pending = []

            def swap_pending():
                while pending:
                    q, g = pending.pop()
                    tile, perm, _, _, r = rotation(q, g)
                    pe.wait_ge(*at("group_read_s", ("group", q["groups"][g][0]["gi"])))
                    if swaps[0] >= 2:
                        pe.wait_ge(*at("rotated", swaps[0] - 2))
                    if q["evac"] in ("qg", "kg"):
                        pe.wait_ge(*at("stat_squares", ("head", swaps[0])))
                        if q["evac"] == "qg":
                            last = mm(ps[:, 6 + swaps[0] % 2, :], ones, sq[:, g % 2, :], True, True)
                        else:
                            pe.wait_ge(*at("rotated", swaps[0] - 1))
                            mm(ps[:, 6, :], ones, sq[:, 0, :], True, True)
                            last = mm(ps[:, 7, :], ones, sq[:, 1, :], True, True)
                        last.then_inc(*up("stat_summed", ("head", swaps[0])))
                    mm(ps[0:r, 4 + swaps[0] % 2, :].rearrange("p (t c) -> p t c", t=2)[:, 0:tile.shape[1], :], perm, tile, True, True).then_inc(
                        *up("swapped", swaps[0]))
                    swaps[0] += 1

            swaps = [0]

            def linear_pe(p):
                T = p["T"]
                for g, grp in enumerate(p["groups"]):
                    for c in grp:
                        if c["first"] and c["gi"] >= 2:
                            pe.wait_ge(*at(group_sem[c["gi"] - 2], ("group", c["gi"] - 2)))
                        pe.wait_ge(*at("weights_low", c["s"]))
                        s = c["s"] % SPLIT
                        A_ = acc(c, T)
                        if p["mode"] == "T":
                            tiles = [(j, j * p["m"], p["m"]) for j in range(c["C"] // p["m"])]
                            if c["C"] == 160:
                                tiles = [(0, 0, P), (1, 64, 96)]
                            if p["evac"] == "poolw":
                                tiles = [(0, 0, P)]
                            steps = [(t, k) for t in tiles for k in range(c["kn"])]
                            if g == 0 and p["fed"]:
                                steps = [(t, k) for k in range(c["kn"]) for t in tiles]
                            for (j, c0, m), k in steps:
                                kk = c["k"] + k
                                if g == 0 and j == 0 and p["fed"]:
                                    pe.wait_ge(*at("operand_low", p["fed"](kk)))
                                w = [b[:, s, k * c["C"] + c0:k * c["C"] + c0 + m] for b in (whi, wlo)]
                                x = [operand(p, kk, T, hi) for hi in (True, False)]
                                st, en = c["first"] and k == 0, c["last"] and k == c["kn"] - 1
                                o = A_[0:m, j, :]
                                mm(o, w[0], x[0], st, False)
                                mm(o, w[0], x[1], False, False)
                                last = mm(o, w[1], x[0], False, en)
                        else:
                            nt = T // P
                            for t in range(nt):
                                b, col = (t, 0) if nt == 2 else (t // 2, (t % 2) * 256)
                                o = ps[:, (c["gi"] % 2) * 2 + b, col:col + 256]
                                for k in range(c["kn"]):
                                    kk = c["k"] + k
                                    if g == 0 and t == 0 and p["fed"]:
                                        pe.wait_ge(*at("operand_low", p["fed"](kk)))
                                    w = [b_[:, s, k * 256:(k + 1) * 256] for b_ in (whi, wlo)]
                                    x = [operand(p, kk, T, hi)[:, t * P:(t + 1) * P] for hi in (True, False)]
                                    mm(o, x[0], w[0], k == 0, False)
                                    mm(o, x[0], w[1], False, False)
                                    last = mm(o, x[1], w[0], False, k == c["kn"] - 1)
                                if t == 0:
                                    swap_pending()
                        last.then_inc(*up("weights_used", c["s"]))
                    if g - 1 in p["mods"]:
                        mod_turn(p["mods"][g - 1][0])
                    if g in p["mods"]:
                        mod_products(*p["mods"][g])
                    if p["name"].startswith("gate") and g == 1:
                        pe.wait_ge(loaded["arena"], p["arena_value"])
                        for k in range(2):
                            for t in range(2):
                                last = pe.transpose(ps[:, 5, k * S + t * P:k * S + (t + 1) * P], pin[:, t, k * P:(k + 1) * P], ident)
                        last.then_inc(*up("turned", (p["i"], "p")))
                    swap_pending()
                    if rotation(p, g):
                        pending.append((p, g))
                if p.get("stat"):
                    pe.wait_ge(*at("squares_folded", (p["i"], 3)))
                    mm(ps[:, 4, 0:T], ones, rstd[:, 0:T], True, True).then_inc(*up("stat_summed", (p["i"], 3)))

            def pool_pe(p):
                c = p["groups"][0][0]
                pe.wait_ge(*at("weights_low", c["s"]))
                if c["gi"] >= 2:
                    pe.wait_ge(*at(group_sem[c["gi"] - 2], ("group", c["gi"] - 2)))
                pe.wait_ge(*at(group_sem[c["gi"] - 1], ("group", c["gi"] - 1)))
                s = c["s"] % SPLIT
                pe.wait_ge(*at("operand_low", (p["i"] - 4, "pool")))
                for g in range(4):
                    w = [b[:, s, g * P:(g + 1) * P] for b in (whi, wlo)]
                    o = ps[:, g, :]
                    mm(o, w[0], uh[:, g, :], True, False)
                    mm(o, w[0], ul[:, g, :], False, False)
                    last = mm(o, w[1], uh[:, g, :], False, True)
                last.then_inc(*up("weights_used", c["s"]))

            def mod_products(n, pair):
                if n >= 2:
                    pe.wait_ge(*at("mod_kept", n - 2))
                for half, c in enumerate(pair):
                    pe.wait_ge(landed[c["r"] % RAW], 16 * (c["r"] // RAW + 1))
                    for k in range(4):
                        last = mm(ps[32 * k:32 * k + 2, 6 + n % 2, :], cc[:, half * 4 + k, :], raw[:, c["r"] % RAW, k * 512:(k + 1) * 512],
                                  half == 0, half == 1)
                    last.then_inc(*up("weights_used", ("mod", c["r"])))

            def mod_turn(n):
                pe.wait_ge(*at("mod_rows", n))
                for j in range(4):
                    last = mm(ps[:, 6 + n % 2, 2 * j:2 * j + 2], modrow[:, j * P:(j + 1) * P], select, True, True)
                last.then_inc(*up("mod_turned", n))

            for p in phases:
                kind, i = p["kind"], p["i"]
                if kind != "linear":
                    swap_pending()
                for sem, value in ended(i):
                    pe.wait_ge(sem, value)
                if kind == "init":
                    pe.wait_ge(loaded["squares"], 16)
                    pe.wait_ge(loaded["x"], 32)
                    for k in range(8):
                        if k >= 3:
                            pe.wait_ge(*at("turned_copied", ("x", k - 3)))
                        for t in range(4):
                            last = pe.transpose(ps[:, 1 + k % 3, t * P:(t + 1) * P], xin[:, t, k * P:(k + 1) * P], ident)
                        last.then_inc(*up("turned", ("x", k)))
                    pe.wait_ge(loaded["rows"], 16 * 18)
                    for b in (6, 7):
                        mm(ps[:, b, :], ones, squares[:, 0:4, :].rearrange("p j c -> p (j c)"), True, True)
                    for j in range(4):
                        n = (at_row, 88, 88, 96)[j]
                        last = pe.transpose(ps[:, 0, j * P:j * P + n], rows[0:n, j, :], ident[0:n, 0:n])
                    last.then_inc(*up("turned", "rows"))
                elif kind == "stats":
                    for k in range(p["n"]):
                        pe.wait_ge(*at("stat_squares", (i, k)))
                        mm(ps[:, 4, 0:p["T"]], ones, sq[:, k % 2, 0:p["T"]], k == 0, k == p["n"] - 1).then_inc(
                            *up("stat_summed", (i, k)))
                elif kind == "join":
                    for g in range(4):
                        square_sums(p, g)
                elif kind == "linear":
                    if p["evac"] == "poolw":
                        pool_pe(p)
                    else:
                        linear_pe(p)
                elif kind == "stick":
                    def z(hd):
                        o = (hd % 2) * 64
                        if hd >= 4:
                            pe.wait_ge(*at("stick_weights", (i, hd - 4)))
                        b = hd % 4
                        qh = q1[o:o + 64, hd // 2, :]
                        mm(ps[:, b, 0:256], k1[o:o + 64, hd // 2, 0:P], qh, True, False)
                        mm(ps[:, b, 256:384], k1[o:o + 64, hd // 2, P:S], qh[:, P:S], False, True).then_inc(
                            *up("scores", (i, hd)))

                    def attend(hd):
                        b = hd % 2
                        pe.wait_ge(*at("masked", (i, hd)))
                        pair, o = hd // 2, (hd % 2) * 64
                        if pair >= 2 and hd % 2 == 0:
                            pe.wait_ge(*at("operand_low", (i, pair - 2)))
                        dst = ps[o:o + 64, 4 + pair % 2, 0:S]
                        vv = [v1[:, t, hd * 64:(hd + 1) * 64] for t in range(2)]
                        mm(dst[:, 0:256], vv[0], sba[:, b, 0:256], True, False)
                        mm(dst[:, 128:256], vv[1], sba[:, b, 256:384], False, True).then_inc(
                            *up("attended", (i, hd)))

                    z(0)
                    z(1)
                    for hd in range(HEADS):
                        if hd + 2 < HEADS:
                            z(hd + 2)
                        b = hd % 2
                        pe.wait_ge(*at("fail_ready", (i, hd)))
                        zb = hd % 4
                        mm(ps[:, zb, 0:256], negtri, sbf[:, b, 0:256], False, False)
                        mm(ps[:, zb, 128:256], negones, sbf[:, b, 256:384], False, False)
                        mm(ps[:, zb, 256:384], negtri, sbf[:, b, 256:384], False, True).then_inc(
                            *up("fail_summed", (i, hd)))
                        if hd >= 1:
                            attend(hd - 1)
                        if hd % 2 == 1 and hd // 2 - 1 in p["mods"]:
                            mod_turn(p["mods"][hd // 2 - 1][0])
                        if hd % 2 == 1 and hd // 2 in p["mods"]:
                            mod_products(*p["mods"][hd // 2])
                    attend(HEADS - 1)
                elif kind == "softmax":
                    units = softmax_units(p["what"])

                    def scores(u):
                        n = u["n"]
                        if u["mask"] is not None and n >= 2:
                            pe.wait_ge(*at("max_ready", (i, n - 2)))
                        if u["mask"] is None and n >= 4:
                            pe.wait_ge(*at("weights_exp", (i, n - 4)))
                        for lhsT, rhs, col in u["prod"]:
                            width = rhs.shape[-1]
                            c0 = 0
                            while c0 < width:
                                w = min(width - c0, 512 - (col + c0) % 512)
                                bank = (n % 2) * 2 + (col + c0) // 512 if u["mask"] is not None else n % 4
                                last = mm(ps[:, bank, (col + c0) % 512:(col + c0) % 512 + w], lhsT, rhs[:, c0:c0 + w], True, True)
                                c0 += w
                        last.then_inc(*up("scores", (i, n)))

                    def turn(u):
                        n = u["n"]
                        pe.wait_ge(*at("weights_normed", (i, n)))
                        wide = u["mask"] is not None
                        if n >= (1 if wide else 2):
                            pe.wait_ge(*at("turned_copied", (i, n - (1 if wide else 2))))
                        kt = u["W"] // P
                        for k in range(kt):
                            last = pe.transpose(ps[:, (4 + k // 4) if wide else 4 + n % 2, (k % 4) * P:(k % 4 + 1) * P], pr[:, n % 2, k * P:(k + 1) * P], ident)
                        last.then_inc(*up("turned", (i, n)))

                    def attend(u):
                        n = u["n"]
                        kt = u["W"] // P
                        pe.wait_ge(*at("turned_copied", (i, n)))
                        a, b = u["rows"]
                        if u["pair"] >= 2:
                            pe.wait_ge(*at("operand_low", (i, u["pair"] - 2)))
                        o = ps[a:b, 6 + u["pair"] % 2, u["q"] * P:(u["q"] + 1) * P]
                        for k in range(kt):
                            last = mm(o, u["vals"][k], pt[:, n % 2, k * P:(k + 1) * P], k == 0, k == kt - 1)
                        last.then_inc(*up("attended", (i, n)))

                    N = len(units)
                    ahead = 2 if units[0]["mask"] is not None else 3
                    for n in range(ahead):
                        scores(units[n])
                    for n in range(N):
                        if n + ahead < N:
                            scores(units[n + ahead])
                        turn(units[n])
                        if n >= 1:
                            attend(units[n - 1])
                    attend(units[N - 1])
                elif kind == "cnorm":
                    for name, n0, n1, bank in (("q", 0, 3, 4), ("kv", 3, 5, 5)):
                        pe.wait_ge(*at("stat_squares", (i, name)))
                        for k in range(n0, n1):
                            last = mm(ps[:, bank, :], ones, csq[:, k, :], k == n0, k == n1 - 1)
                        last.then_inc(*up("stat_summed", (i, name)))
                elif kind in ("final", "dump"):
                    for k in range(8):
                        if kind == "final":
                            pe.wait_ge(*at("normed", (i, k)))
                        src = y if kind == "final" else h
                        if k >= 3:
                            pe.wait_ge(*at("turned_copied", (i, k - 3)))
                        for t in range(2):
                            last = pe.transpose(ps[:, 1 + k % 3, t * P:(t + 1) * P], src[:, k, t * P:(t + 1) * P], ident)
                        last.then_inc(*up("turned", (i, k)))
                C.end("tensor", i)

        @block.scalar
        def _(act):
            def up(family, key=None):
                return C.sems[family], C.raised("scalar", family, key)

            def own():
                return C.sems[C.last["scalar"][0]], C.last["scalar"][1]


            def split_high(s):
                if s >= len(splits):
                    return
                c = splits[s]
                n = c["kn"] * c["C"]
                act.wait_ge(landed[c["r"] % RAW], 16 * (c["r"] // RAW + 1))
                if s >= SPLIT:
                    act.wait_ge(*at("weights_used", s - SPLIT))
                act.wait_ge(*own())
                nc.scalar.activation(whi[:, s % SPLIT, 0:n], raw[:, c["r"] % RAW, 0:n], ACT.Copy).then_inc(
                    *up("weights_high", s))

            def hidden_high(p, g):
                b = g % 2
                act.wait_ge(*at("normed", (p["i"], g)))
                act.wait_ge(*own())
                nc.scalar.activation(hh[:, 2 * g * S:2 * (g + 1) * S].rearrange("p (t c) -> p t c", t=2), y[:, 2 * b:2 * b + 2, 0:S], ACT.Copy).then_inc(
                    *up("operand_high", (p["i"], g)))

            def angles_and_conditioning():
                act.wait_ge(*at("normed", "angles"))
                act.wait_ge(*own())
                nc.scalar.activation(sin1[:, :], turns[:, 0, :], ACT.Sin).then_inc(*up("scalar_step"))
                act.wait_ge(*own())
                nc.scalar.activation(cos1[:, :], turns[:, 1, :], ACT.Sin).then_inc(*up("scalar_step"))
                nc.scalar.preload_act_table_set("natural_log_exp_and_others")
                act.wait_ge(*own())
                nc.scalar.activation(silu[:, 0, :], vec[:, ROW["c_2"]:ROW["c_2"] + 8], ACT.Exp, scale=-1.0).then_inc(
                    *up("scalar_step"))
                act.wait_ge(*own())
                nc.scalar.activation(silu[:, 1, :], vec[:, ROW["c_ctx_2"]:ROW["c_ctx_2"] + 8], ACT.Exp, scale=-1.0).then_inc(
                    *up("weights_exp", "cond"))

            pending = []
            heads = [0]

            def head_rstd_pending():
                while pending:
                    q, g = pending.pop()
                    n = heads[0]
                    src, dst = ((ps[:, 6 + n % 2, :], y[:, n % 2, :]) if q["evac"] == "qg" else (ps[:, 6:8, :], y[:, 2:4, :]))
                    act.wait_ge(*at("stat_summed", ("head", n)))
                    act.wait_ge(*own())
                    nc.scalar.activation(dst, src, ACT.Ln, scale=1.0 / P, bias=small[:, 40:41]).then_inc(*up("scalar_step"))
                    act.wait_ge(*own())
                    nc.scalar.activation(dst, dst, ACT.Exp, scale=-0.5).then_inc(*up("rstd_ready", ("head", n)))
                    heads[0] += 1

            def hidden_high_conv(p, g):
                for j in range(2):
                    act.wait_ge(*at("group_read_v", (p["i"], g, j)))
                    act.wait_ge(*own())
                    nc.scalar.activation(hid(hh, g - 1 + j, p["T"]), csil[:, j, 0:p["T"]], ACT.Copy).then_inc(
                        *up("operand_high", (p["i"], g, j)))

            def squares_of(p, g):
                T, i = p["T"], p["i"]
                src = y if p["stat"] == "y" else h
                if p["kind"] == "linear" and p["evac"] != "addgated":
                    act.wait_ge(*at("group_read_v", ("group", p["groups"][g][0]["gi"])))
                else:
                    act.wait_ge(*at("tiles_ready", (i, g)))
                if T == S:
                    if g >= 2:
                        act.wait_ge(*at("squares_folded" if p["kind"] == "linear" else "stat_summed", (i, g - 2)))
                    act.wait_ge(*own())
                    nc.scalar.activation(sq[:, g % 2, :].rearrange("p (t c) -> p t c", t=2), src[:, 2 * g:2 * g + 2, 0:S], ACT.Square).then_inc(
                        *up("stat_squares", (i, g)))
                else:
                    if g >= 1:
                        act.wait_ge(*at("squares_folded", (i, g - 1)))
                    act.wait_ge(*own())
                    nc.scalar.activation(sq[:, :, :], src[:, 2 * g:2 * g + 2, :], ACT.Square).then_inc(
                        *up("stat_squares", (i, g)))

            def rstd_of(p):
                act.wait_ge(*at("stat_summed", (p["i"], 3)))
                act.wait_ge(*own())
                nc.scalar.activation(lnv[:, 0:p["T"]], ps[:, 4, 0:p["T"]], ACT.Ln, scale=1.0 / D, bias=small[:, 40:41]).then_inc(
                    *up("scalar_step"))
                act.wait_ge(*own())
                nc.scalar.activation(rstd[:, 0:p["T"]], lnv[:, 0:p["T"]], ACT.Exp, scale=-0.5).then_inc(
                    *up("rstd_ready", p["i"]))

            def evac(p, grp):
                c = grp[0]
                T, kind, i, g = p["T"], p["evac"], p["i"], c["g"]
                key = ("group", c["gi"])
                A_ = acc(c, T)
                act.wait_ge(*at("weights_used", grp[-1]["s"]))
                if kind == "qk1":
                    dst = (q1 if g < 4 else k1)[:, (g % 4) * 2:(g % 4) * 2 + 2, :]
                    act.wait_ge(*own())
                    nc.scalar.activation(dst, A_, ACT.Copy, scale=HD ** -0.5 if g < 4 else 1.0).then_inc(
                        *up("group_read_s", key))
                elif kind == "qk2":
                    grp_no = int(p["name"][-1])
                    act.wait_ge(*own())
                    nc.scalar.activation(qk2[:, grp_no * 8 + g * 2:grp_no * 8 + g * 2 + 2, :], A_, ACT.Copy).then_inc(
                        *up("group_read_s", key))
                elif kind == "v":
                    nt = T // P
                    src = ps[:, (c["gi"] % 2) * 2:(c["gi"] % 2) * 2 + 2, 0:256 if nt == 2 else 512]
                    if nt == 4:
                        src = src.rearrange("p b (t c) -> p b t c", t=2)
                    name = p["name"]
                    if name == "stick_v":
                        dst = v1[:, :, g * 256:(g + 1) * 256]
                    elif name.startswith("dil_v"):
                        c0 = int(name[-1]) * 512 + g * 256
                        dst = v2[:, :, c0:c0 + 256]
                    elif name == "uv":
                        dst = vm[:, :, g * 256:(g + 1) * 256].rearrange("p (b t) c -> p b t c", b=2)
                    else:
                        dst = vg[:, :, :].rearrange("p (b t) c -> p b t c", b=2)
                    act.wait_ge(*own())
                    nc.scalar.activation(dst, src, ACT.Copy).then_inc(*up("group_read_s", key))
                elif kind == "relu2":
                    act.wait_ge(*own())
                    nc.scalar.activation(work[:, c["gi"] % 2, :, 0:S], A_, ACT.Relu).then_inc(*up("group_read_s", key))
                    if g >= 1:
                        hidden_high(p, g - 1)
                    if g == len(p["groups"]) - 1:
                        hidden_high(p, g)
                elif kind == "gate":
                    if g >= 2:
                        act.wait_ge(*at("normed", ("gate", i, g - 2)))
                    act.wait_ge(*own())
                    nc.scalar.activation(ge[:, g % 2, :, :], A_, ACT.Exp, scale=-1.0).then_inc(*up("group_read_s", key))
                elif kind == "mixc":
                    if g < 2:
                        act.wait_ge(*own())
                        nc.scalar.activation(y[:, 2 * g:2 * g + 2, :], A_, ACT.Copy).then_inc(*up("group_read_s", key))
                    else:
                        act.wait_ge(*own())
                        nc.scalar.activation(y[:, 4, :], A_[:, 0, :], ACT.Copy).then_inc(*up("scalar_step"))
                        act.wait_ge(*own())
                        nc.scalar.activation(kr[0:96, :], A_[0:96, 1, :], ACT.Copy).then_inc(*up("group_read_s", key))
                elif kind == "mixp":
                    for j in range(2):
                        act.wait_ge(*own())
                        nc.scalar.activation(pbuf[:, 2 * g + j, :, PAD:PAD + S], A_[:, j, :].rearrange("p (s c) -> p s c", s=2), ACT.Copy).then_inc(
                            *up("group_read_s", key if j else None))
                elif kind == "uq":
                    act.wait_ge(*own())
                    nc.scalar.activation(qm[0:96, 2 * g:2 * g + 2, :], A_[0:96], ACT.Copy).then_inc(*up("group_read_s", key))
                elif kind == "uk":
                    for par in range(2):
                        act.wait_ge(*own())
                        nc.scalar.activation(km[0:64, 4 * g + par:4 * g + 4:2, :], A_[64 * par:64 * par + 64], ACT.Copy).then_inc(
                            *up("group_read_s", key if par else None))
                elif kind in ("qg", "kg"):
                    n = heads[0] + len(pending)
                    dst, gain_, sq_ = ((qg[:, 2 * g:2 * g + 2, :], "gqa_g_q", sq[:, g % 2, :].rearrange("p (t c) -> p t c", t=2)) if kind == "qg"
                                       else (kg[:, :, :], "gqa_g_k", sq[:, :, :]))
                    if g >= 2 or kind == "kg":
                        act.wait_ge(*at("stat_summed", ("head", n - (2 if kind == "qg" else 1))))
                    act.wait_ge(*own())
                    nc.scalar.activation(sq_, A_, ACT.Square).then_inc(*up("stat_squares", ("head", n)))
                    act.wait_ge(*own())
                    nc.scalar.activation(dst, A_, ACT.Copy, scale=vec[:, ROW[gain_]:ROW[gain_] + 1]).then_inc(*up("group_read_s", key))
                elif kind == "poolw":
                    for t in range(4):
                        act.wait_ge(*own())
                        nc.scalar.activation(uh[:, 4 + t, :], ps[:, t, :], ACT.Copy, scale=vec[:, ROW["pool_scale_2"] + t:ROW["pool_scale_2"] + t + 1]).then_inc(
                            *up("operand_high", (i, t)))
                elif kind == "conv" and g % 2 == 0:
                    l, f0 = p["l"], p["f0"]
                    for j in range(2):
                        f = f0 + g + j
                        act.wait_ge(*own())
                        nc.scalar.activation(cacc[:, j, 0:T], A_[:, j, :], ACT.Identity, bias=convv[:, l, 66 + f:67 + f], scale=convv[:, l, 22 + f:23 + f]).then_inc(
                            *up("moved", (i, g, j)))
                    if g >= 2:
                        hidden_high_conv(p, g - 1)
                elif kind == "conv":
                    for j in range(2):
                        act.wait_ge(*at("group_read_v", (i, g - 1, j)))
                        if g >= 2:
                            act.wait_ge(*at("operand_low", (i, g - 2, j)))
                        act.wait_ge(*own())
                        nc.scalar.activation(csil[:, j, 0:T], cacc[:, j, 0:T], ACT.Silu).then_inc(
                            *up("gated_silu", (i, g - 1, j)))
                    if g == len(p["groups"]) - 1:
                        hidden_high_conv(p, g)

            def mod_rows(n, pair):
                act.wait_ge(*at("weights_used", ("mod", pair[1]["r"])))
                act.wait_ge(*own())
                nc.scalar.activation(modrow, ps[:, 6 + n % 2, :], ACT.Copy).then_inc(*up("mod_rows", n))

            nc.scalar.preload_act_table_set("natural_log_exp_and_others")
            for p in phases:
                kind, i = p["kind"], p["i"]
                early, late = late_splits(p)
                if kind != "linear":
                    head_rstd_pending()
                for sem, value in ended(i):
                    act.wait_ge(sem, value)
                for dst, src in p.get("loads", ()):
                    act.dma_start(dst, src).then_inc(loaded["arena"], 16)
                if p.get("name") in ("down01", "down10"):
                    nc.scalar.preload_act_table_set("natural_log_exp_and_others")
                if kind == "init":
                    for n in range(2):
                        act.dma_start(xin[:, 2 * n:2 * n + 2, :], (A["x"], A["ctx_2"])[n][0].rearrange("(t p) d -> p t d", p=P)).then_inc(loaded["x"], 16)
                    for k in range(8):
                        act.wait_ge(*at("turned", ("x", k)))
                        if k:
                            act.wait_ge(*own())
                        nc.scalar.activation(h[:, k, :], ps[:, 1 + k % 3, :], ACT.Copy).then_inc(
                            *up("turned_copied", ("x", k)))
                    act.wait_ge(*at("turned", "rows"))
                    for n, dst in enumerate((vec[:, 0:at_row], convv[:, 0, 0:88], convv[:, 1, 0:88], bmod[:, 0:96])):
                        nc.scalar.activation(dst, ps[:, 0, n * P:n * P + (at_row, 88, 88, 96)[n]], ACT.Copy).then_inc(
                            *up("scalar_step"))
                elif kind == "stats":
                    src = h if p["src"] == "h" else y
                    s0 = p.get("s0", 0)
                    for k in range(p["n"]):
                        if k >= 2:
                            act.wait_ge(*at("stat_summed", (i, k - 2)))
                        act.wait_ge(*own())
                        nc.scalar.activation(sq[:, k % 2, 0:p["T"]], src[:, s0 + k, 0:p["T"]], ACT.Square).then_inc(
                            *up("stat_squares", (i, k)))
                    if i == 1:
                        split_high(0)
                    act.wait_ge(*at("stat_summed", (i, p["n"] - 1)))
                    act.wait_ge(*own())
                    nc.scalar.activation(lnv[:, 0:p["T"]], ps[:, 4, 0:p["T"]], ACT.Ln, scale=1.0 / p["D"], bias=small[:, 40:41]).then_inc(
                        *up("scalar_step"))
                    act.wait_ge(*own())
                    nc.scalar.activation(rstd[:, 0:p["T"]], lnv[:, 0:p["T"]], ACT.Exp, scale=-0.5).then_inc(
                        *up("rstd_ready", i))
                elif kind == "apply":
                    for k in range(p["n"]):
                        act.wait_ge(*at("normed", (i, k)))
                        dst = ch if p.get("dst") == "c" else uh
                        k_ = p.get("s0", 0) + k if p.get("dst") == "c" else k
                        if "mod" in p:
                            for s_, sl in segs(p["T"]):
                                l, which = p["mod"]
                                act.wait_ge(*own())
                                nc.scalar.activation(y[:, k, sl], y[:, k, sl], ACT.Identity, bias=mod_at(l, which, k, s_), scale=mod_at(l, which + 1, k, s_)).then_inc(
                                    *up("scalar_step"))
                        act.wait_ge(*own())
                        nc.scalar.activation(dst[:, k_, 0:p["T"]], y[:, p.get("s0", 0) + k, 0:p["T"]], ACT.Copy).then_inc(
                            *up("operand_high", (i, k)))
                    if i == 2:
                        for s in range(1, SPLIT):
                            split_high(s)
                elif kind == "linear":
                    for grp in p["groups"]:
                        if p.get("stat") and grp[0]["g"] >= 1:
                            squares_of(p, grp[0]["g"] - 1)
                        if p["mode"] == "V":
                            head_rstd_pending()
                        for c in grp[:-1]:
                            split_high(c["s"] + SPLIT)
                        evac(p, grp)
                        already = bool(pending)
                        if already:
                            split_high(grp[-1]["s"] + SPLIT)
                        head_rstd_pending()
                        if p["evac"] in ("qg", "kg"):
                            pending.append((p, grp[0]["g"]))
                        elif rotation(p, grp[0]["g"]):
                            heads[0] += 1
                        if grp[0]["g"] in p["mods"]:
                            mod_rows(*p["mods"][grp[0]["g"]])
                        if not already and grp[-1]["s"] + SPLIT not in early + late:
                            split_high(grp[-1]["s"] + SPLIT)
                        if p["name"] == "stick_qk" and grp[0]["g"] == 0:
                            angles_and_conditioning()
                        if p["name"].startswith("gate") and grp[0]["g"] == 2:
                            act.wait_ge(*at("turned", (i, "p")))
                            act.wait_ge(*own())
                            nc.scalar.activation(ph_[:, :, :], ps[:, 5, :].rearrange("p (k c) -> p k c", k=2), ACT.Copy).then_inc(
                                *up("operand_high", (i, "p")))
                    if p.get("stat"):
                        squares_of(p, 3)
                        for s in early:
                            split_high(s)
                        rstd_of(p)
                elif kind == "join":
                    for g in range(4):
                        squares_of(p, g)
                    rstd_of(p)
                elif kind == "stick":
                    def ex(hd):
                        b = hd % 2
                        act.wait_ge(*at("scores", (i, hd)))
                        act.wait_ge(*own())
                        nc.scalar.activation(sbt[:, b, :], ps[:, hd % 4, 0:384], ACT.Abs).then_inc(*up("scalar_step"))
                        act.wait_ge(*own())
                        nc.scalar.activation(sbe[:, b, :], sbt[:, b, :], ACT.Exp, scale=-1.0).then_inc(*up("scalar_step"))
                        if hd >= 2:
                            act.wait_ge(*at("fail_ready", (i, hd - 2)))
                        act.wait_ge(*own())
                        nc.scalar.activation(sbl[:, b, :], sbe[:, b, :], ACT.Ln, bias=1.0).then_inc(
                            *up("weights_exp", (i, hd)))

                    def high(pair):
                        act.wait_ge(*at("attended", (i, 2 * pair + 1)))
                        act.wait_ge(*own())
                        nc.scalar.activation(uh[:, pair, 0:S], ps[:, 4 + pair % 2, 0:S], ACT.Copy).then_inc(
                            *up("operand_high", (i, pair)))

                    ex(0)
                    for hd in range(HEADS):
                        if hd + 1 < HEADS:
                            ex(hd + 1)
                        b = hd % 2
                        act.wait_ge(*at("fail_summed", (i, hd)))
                        if hd >= 2:
                            act.wait_ge(*at("attended", (i, hd - 2)))
                        act.wait_ge(*own())
                        nc.scalar.activation(sba[:, b, :], ps[:, hd % 4, 0:384], ACT.Exp).then_inc(*up("stick_weights", (i, hd)))
                        if hd % 2 == 0 and hd // 2 - 1 in p["mods"]:
                            mod_rows(*p["mods"][hd // 2 - 1])
                        if hd % 2 == 1 and hd >= 3:
                            high(hd // 2 - 1)
                    high(HEADS // 2 - 1)
                elif kind == "softmax":
                    units = softmax_units(p["what"])
                    N = len(units)

                    def exp_(u):
                        n = u["n"]
                        act.wait_ge(*at("max_ready", (i, n)))
                        b = n % 2
                        W = u["W"]
                        if u["mask"] is not None:
                            src = sm[:, b, 0:W]
                        else:
                            src = ps[:, n % 4, 0:W]
                        if n >= 2:
                            act.wait_ge(*at("turned", (i, n - 2)))
                        act.wait_ge(*own())
                        nc.scalar.activation(pr[:, b, 0:W], src, ACT.Exp, scale=u["scale"], bias=small[:, b:b + 1], accum_out=small[:, 2 + b:3 + b]).then_inc(
                            *up("weights_exp", (i, n)))

                    def copy_(u):
                        n = u["n"]
                        W = u["W"]
                        act.wait_ge(*at("turned", (i, n)))
                        if n >= 2:
                            act.wait_ge(*at("attended", (i, n - 2)))
                        for c0 in range(0, W, 512):
                            w = min(512, W - c0)
                            act.wait_ge(*own())
                            nc.scalar.activation(pt[:, n % 2, c0:c0 + w], ps[:, (4 + c0 // 512) if u["mask"] is not None else 4 + n % 2, 0:w], ACT.Copy).then_inc(
                                *up("turned_copied", (i, n)))

                    def high_(u):
                        n = u["n"]
                        act.wait_ge(*at("attended", (i, n)))
                        t0 = u["col"] - u["q"] * P
                        act.wait_ge(*own())
                        nc.scalar.activation(uh[:, u["opair"], t0:t0 + S], ps[:, 6 + u["pair"] % 2, 0:S], ACT.Copy).then_inc(
                            *up("operand_high", (i, u["pair"])))

                    exp_(units[0])
                    for n in range(N):
                        if n + 1 < N:
                            exp_(units[n + 1])
                        copy_(units[n])
                        if n >= 2 and units[n - 2]["ends"]:
                            high_(units[n - 2])
                    for n in (N - 2, N - 1):
                        if units[n]["ends"]:
                            high_(units[n])
                elif kind == "cnorm":
                    parts = (("q", 0, 3, rstd), ("kv", 3, 5, sq[:, 0, :]))
                    for name, n0, n1, _ in parts:
                        act.wait_ge(*own())
                        nc.scalar.activation(csq[:, n0:n1, :], y[:, n0:n1, :], ACT.Square).then_inc(*up("stat_squares", (i, name)))
                    for name, n0, n1, r in parts:
                        act.wait_ge(*at("stat_summed", (i, name)))
                        act.wait_ge(*own())
                        nc.scalar.activation(lnv[:, :], ps[:, 4 if name == "q" else 5, :], ACT.Ln, scale=1.0 / (P * (n1 - n0)), bias=small[:, 40:41]).then_inc(
                            *up("scalar_step"))
                        act.wait_ge(*own())
                        nc.scalar.activation(r[:, :], lnv[:, :], ACT.Exp, scale=-0.5).then_inc(*up("rstd_ready", (i, name)))
                    for k in range(5):
                        act.wait_ge(*at("normed", (i, k)))
                        act.wait_ge(*own())
                        nc.scalar.activation(ch[:, k, :], y[:, k, :], ACT.Copy).then_inc(*up("operand_high", (i, k)))
                    act.wait_ge(*own())
                    nc.scalar.activation(uh[:, 0:4, :], pdif[:, :, :], ACT.Copy).then_inc(*up("operand_high", (i, "pool")))
                elif kind in ("final", "dump"):
                    for k in range(8):
                        act.wait_ge(*at("turned", (i, k)))
                        act.wait_ge(*own())
                        nc.scalar.activation(xin[:, 0:2, k * P:(k + 1) * P], ps[:, 1 + k % 3, 0:S].rearrange("p (t c) -> p t c", t=2), ACT.Copy).then_inc(
                            *up("turned_copied", (i, k)))
                C.end("scalar", i)
                for s in waiting_splits(i):
                    split_high(s)

        @block.vector
        def _(dve):
            def up(family, key=None):
                return C.sems[family], C.raised("vector", family, key)

            def own():
                return C.sems[C.last["vector"][0]], C.last["vector"][1]

            def split_low(s):
                if s >= len(splits):
                    return
                c = splits[s]
                n = c["kn"] * c["C"]
                dve.wait_ge(*at("weights_high", s))
                dve.wait_ge(*own())
                nc.vector.tensor_tensor(wlo[:, s % SPLIT, 0:n], raw[:, c["r"] % RAW, 0:n], whi[:, s % SPLIT, 0:n].bitcast(F32), ALU.subtract).then_inc(
                    *up("weights_low", s))

            def hidden_low_conv(p, g):
                T = p["T"]
                for j in range(2):
                    dve.wait_ge(*at("operand_high", (p["i"], g, j)))
                    dve.wait_ge(*own())
                    nc.vector.tensor_tensor(hid(hl, g - 1 + j, T), csil[:, j, 0:T], hid(hh, g - 1 + j, T).bitcast(F32), ALU.subtract).then_inc(
                        *up("operand_low", (p["i"], g, j)))

            def hidden_low(p, g):
                b = g % 2
                dve.wait_ge(*at("operand_high", (p["i"], g)))
                v = lambda b: b[:, 2 * g * S:2 * (g + 1) * S].rearrange("p (t c) -> p t c", t=2)
                dve.wait_ge(*own())
                nc.vector.tensor_tensor(v(hl), y[:, 2 * b:2 * b + 2, 0:S], v(hh).bitcast(F32), ALU.subtract).then_inc(
                    *up("operand_low", (p["i"], g)))

            def evac(p, grp):
                c = grp[0]
                T, kind, i, g = p["T"], p["evac"], p["i"], c["g"]
                key = ("group", c["gi"])
                A_ = acc(c, T)
                if kind == "y":
                    dve.wait_ge(*at("weights_used", grp[-1]["s"]))
                    dve.wait_ge(*own())
                    nc.vector.tensor_copy(y[:, 2 * g:2 * g + 2, 0:T], A_).then_inc(*up("group_read_v", key))
                elif kind == "relu2":
                    dve.wait_ge(*at("group_read_s", key))
                    w = work[:, c["gi"] % 2, :, 0:S]
                    yy = y[:, 2 * (g % 2):2 * (g % 2) + 2, 0:S]
                    dve.wait_ge(*own())
                    nc.vector.tensor_tensor(yy, w, w, ALU.mult).then_inc(*up("normed", (i, g)))
                    if g >= 1:
                        hidden_low(p, g - 1)
                    if g == len(p["groups"]) - 1:
                        hidden_low(p, g)
                elif kind == "gate":
                    dve.wait_ge(*at("group_read_s", key))
                    gg = ge[:, g % 2, :, :]
                    dve.wait_ge(*own())
                    nc.vector.tensor_scalar(gg, gg, 1.0, None, ALU.add).then_inc(*up("vector_step"))
                    dve.wait_ge(*own())
                    nc.vector.reciprocal(y[:, 2 * g:2 * g + 2, 0:S], gg).then_inc(*up("normed", ("gate", i, g)))
                elif kind == "addgated":
                    dve.wait_ge(*at("weights_used", grp[-1]["s"]))
                    yy = y[:, 2 * g:2 * g + 2, 0:S]
                    dve.wait_ge(*own())
                    nc.vector.tensor_tensor(yy, A_, yy, ALU.mult).then_inc(*up("group_read_v", key))
                    hh_ = h[:, 2 * g:2 * g + 2, 0:S]
                    dve.wait_ge(*own())
                    nc.vector.tensor_tensor(hh_, hh_, yy, ALU.add).then_inc(*up("tiles_ready", (i, g)))
                elif kind in ("gated", "gated2"):
                    dve.wait_ge(*at("weights_used", grp[-1]["s"]))
                    src = A_
                    if kind == "gated2":
                        src = y[:, 2 * g:2 * g + 2, 0:T]
                        dve.wait_ge(*own())
                        nc.vector.tensor_tensor(src, A_, src, ALU.add).then_inc(*up("vector_step"))
                    l, which = p["mod"]
                    for j in range(2):
                        for s_, sl in segs(T):
                            k = 2 * g + j
                            dve.wait_ge(*own())
                            nc.vector.scalar_tensor_tensor(h[:, k, sl], src[:, j, sl], mod_at(l, which, k, s_), h[:, k, sl], ALU.mult, ALU.add).then_inc(
                                *up("group_read_v", key))
                elif kind == "poolw":
                    for t in range(4):
                        dve.wait_ge(*at("operand_high", (i, t)))
                        sc = vec[:, ROW["pool_scale_2"] + t:ROW["pool_scale_2"] + t + 1]
                        dve.wait_ge(*own())
                        nc.vector.scalar_tensor_tensor(ul[:, 4 + t, :], ps[:, t, :], sc, uh[:, 4 + t, :].bitcast(F32), ALU.mult, ALU.subtract).then_inc(
                            *up("group_read_v", key))
                elif kind == "conv" and g % 2 == 0:
                    l, f0 = p["l"], p["f0"]
                    ns = T // S
                    for j in range(2):
                        f = f0 + g + j
                        dve.wait_ge(*at("moved", (i, g, j)))
                        a = cacc[:, j, 0:T].rearrange("p (s c) -> p s c", s=ns)
                        x = A_[:, j, :].rearrange("p (s c) -> p s c", s=ns)
                        dve.wait_ge(*own())
                        nc.vector.scalar_tensor_tensor(a[:, :, 1:S], x[:, :, 0:S - 1], convv[:, l, f:f + 1], a[:, :, 1:S], ALU.mult, ALU.add).then_inc(
                            *up("vector_step"))
                        dve.wait_ge(*own())
                        nc.vector.scalar_tensor_tensor(a[:, :, 0:S - 1], x[:, :, 1:S], convv[:, l, 44 + f:45 + f], a[:, :, 0:S - 1], ALU.mult, ALU.add).then_inc(
                            *up("group_read_v", (i, g, j)))
                    C.note("group_read_v", key)
                    if g >= 2:
                        hidden_low_conv(p, g - 1)
                elif kind == "conv":
                    dve.wait_ge(*at("weights_used", grp[-1]["s"]))
                    for j in range(2):
                        dve.wait_ge(*at("gated_silu", (i, g - 1, j)))
                        dve.wait_ge(*own())
                        nc.vector.tensor_tensor(csil[:, j, 0:T], A_[:, j, :], csil[:, j, 0:T], ALU.mult).then_inc(
                            *up("group_read_v", (i, g, j)))
                    C.note("group_read_v", key)
                    if g == len(p["groups"]) - 1:
                        hidden_low_conv(p, g)

            def conditioning():
                dve.wait_ge(*at("weights_exp", "cond"))
                dve.wait_ge(*own())
                nc.vector.tensor_scalar(silu[:, :, :], silu[:, :, :], 1.0, None, ALU.add).then_inc(*up("vector_step"))
                dve.wait_ge(*own())
                nc.vector.reciprocal(silu[:, :, :], silu[:, :, :]).then_inc(*up("vector_step"))
                for n, name in enumerate(("c_2", "c_ctx_2")):
                    dve.wait_ge(*own())
                    nc.vector.tensor_tensor(cc[:, :, n], vec[:, ROW[name]:ROW[name] + 8], silu[:, n, :], ALU.mult).then_inc(
                        *up("vector_step"))

            pending = []
            swaps = [0]

            def rotate_pending():
                while pending:
                    q, g = pending.pop()
                    tile, _, cos, sin, r = rotation(q, g)
                    nt = tile.shape[1]
                    wide = lambda a: a[0:r, :].rearrange("p (o c) -> p o c", o=1).to_broadcast([r, nt, S])
                    tmp = work[0:r, 0, 0:nt, :]
                    dve.wait_ge(*at("swapped", swaps[0]))
                    if q["evac"] == "qg" and g == 0:
                        dve.wait_ge(loaded["arena"], q["arena_value"])
                    dve.wait_ge(*own())
                    nc.vector.tensor_tensor(tmp, ps[0:r, 4 + swaps[0] % 2, :].rearrange("p (t c) -> p t c", t=2)[:, 0:nt, :], wide(sin), ALU.mult).then_inc(
                        *up("vector_step"))
                    dve.wait_ge(*own())
                    nc.vector.tensor_tensor(tile, tile, wide(cos), ALU.mult).then_inc(*up("vector_step"))
                    dve.wait_ge(*own())
                    nc.vector.tensor_tensor(tile, tile, tmp, ALU.add).then_inc(*up("rotated", swaps[0]))
                    if q["evac"] in ("qg", "kg"):
                        t, rs = ((tile, y[:, swaps[0] % 2, :].rearrange("p (t c) -> p t c", t=2)) if q["evac"] == "qg"
                                 else (kg[:, :, :], y[:, 2:4, :]))
                        dve.wait_ge(*at("rstd_ready", ("head", swaps[0])))
                        dve.wait_ge(*own())
                        nc.vector.tensor_tensor(t, t, rs, ALU.mult).then_inc(*up("rotated", swaps[0]))
                    swaps[0] += 1

            def pool_windows(p):
                dve.wait_ge(loaded["arena"], p["arena_value"])
                dve.wait_ge(*at("group_read_s", ("group", p["groups"][0][0]["gi"] - 1)))
                L = S + 2 * PAD
                dve.wait_ge(*own())
                nc.vector.memset(pbuf[:, :, :, 0:PAD], 0.0).then_inc(*up("vector_step"))
                dve.wait_ge(*own())
                nc.vector.memset(pbuf[:, :, :, PAD + S:L], 0.0).then_inc(*up("vector_step"))
                dve.wait_ge(*own())
                nc.vector.tensor_tensor(abuf[:, :, :, 0:L - 1], pbuf[:, :, :, 0:L - 1], pbuf[:, :, :, 1:L], ALU.add).then_inc(
                    *up("vector_step"))
                for n, w in enumerate((2, 4, 8)):
                    end = L - 2 * w + 1
                    dve.wait_ge(*own())
                    nc.vector.tensor_tensor(abuf[:, n + 1:4, :, 0:end], abuf[:, n + 1:4, :, 0:end], abuf[:, n + 1:4, :, w:w + end], ALU.add).then_inc(
                        *up("vector_step"))
                for g, w in enumerate(POOL_W):
                    for s_, sl in segs(T2):
                        a = abuf[:, g, s_, PAD - w // 2:PAD - w // 2 + S]
                        dve.wait_ge(*own())
                        nc.vector.tensor_tensor(a, a, rcount[:, g, :], ALU.mult).then_inc(*up("vector_step"))
                        dve.wait_ge(*own())
                        nc.vector.tensor_tensor(pdif[:, g, sl], a, pbuf[:, g, s_, PAD:PAD + S], ALU.subtract).then_inc(
                            *up("normed", "pooled"))

            def fold_squares(p, g):
                T = p["T"]
                pair = [sq[:, g % 2, j * S:(j + 1) * S] if T == S else sq[:, j, :] for j in range(2)]
                total = rstd[:, 0:T]
                dve.wait_ge(*at("stat_squares", (p["i"], g)))
                if g >= 1:
                    dve.wait_ge(*own())
                    nc.vector.tensor_tensor(total, total, pair[0], ALU.add).then_inc(*up("vector_step"))
                dve.wait_ge(*own())
                nc.vector.tensor_tensor(total, pair[0] if g == 0 else total, pair[1], ALU.add).then_inc(
                    *up("squares_folded", (p["i"], g)))

            def mod_keep(n):
                l, c = divmod(n, 12)
                dst = modc[:, l, 4 * c:4 * c + 4, :]
                dve.wait_ge(*at("mod_turned", n))
                for s_ in range(2):
                    dve.wait_ge(*own())
                    nc.vector.tensor_tensor(dst[:, :, s_], ps[:, 6 + n % 2, s_:8:2], bmod[:, l * 48 + 4 * c:l * 48 + 4 * c + 4], ALU.add).then_inc(
                        *up("vector_step"))
                dve.wait_ge(*own())
                nc.vector.tensor_scalar(dst, dst, 1.0 if c // 2 in (1, 4) else 0.0, None, ALU.add).then_inc(*up("mod_kept", n))

            for p in phases:
                kind, i = p["kind"], p["i"]
                early, late = late_splits(p)
                if pending and kind != "linear":
                    rotate_pending()
                    C.end("vector", i - 1)
                for sem, value in ended(i):
                    dve.wait_ge(sem, value)
                if kind == "init":
                    nc.vector.memset(small[:, :], EPS).then_inc(*up("vector_step"))
                    dve.wait_ge(loaded["pos"], 16)
                    dve.wait_ge(loaded["freq"], 16)
                    dve.wait_ge(*own())
                    nc.vector.tensor_copy(ang[:, :], posi[:, :]).then_inc(*up("vector_step"))
                    dve.wait_ge(*own())
                    nc.vector.tensor_scalar(ang[:, :], ang[:, :], freq[:, 0:1], None, ALU.mult).then_inc(*up("vector_step"))
                    magic = 12582912.0
                    c1 = 6.28125
                    c2 = float(np.float32(2 * np.pi - c1))
                    c3 = 2 * np.pi - c1 - c2
                    for n, off in enumerate((0.0, 0.25)):
                        t = turns[:, n, :]
                        dve.wait_ge(*own())
                        nc.vector.tensor_scalar(lnv[:, 0:S], ang[:, :], 1 / (2 * np.pi), off, ALU.mult, ALU.add).then_inc(
                            *up("vector_step"))
                        dve.wait_ge(*own())
                        nc.vector.tensor_scalar(lnv[:, 0:S], lnv[:, 0:S], magic, magic, ALU.add, ALU.subtract).then_inc(
                            *up("vector_step"))
                        dve.wait_ge(*own())
                        nc.vector.scalar_tensor_tensor(t, lnv[:, 0:S], -c1, ang[:, :], ALU.mult, ALU.add).then_inc(
                            *up("vector_step"))
                        dve.wait_ge(*own())
                        nc.vector.scalar_tensor_tensor(t, lnv[:, 0:S], -c2, t, ALU.mult, ALU.add).then_inc(
                            *up("vector_step"))
                        dve.wait_ge(*own())
                        nc.vector.scalar_tensor_tensor(t, lnv[:, 0:S], -c3, t, ALU.mult, ALU.add).then_inc(
                            *up("vector_step"))
                        dve.wait_ge(*own())
                        nc.vector.tensor_scalar(t, t, off * 2 * np.pi, 3.1415925, ALU.add, ALU.min).then_inc(
                            *up("vector_step"))
                        dve.wait_ge(*own())
                        nc.vector.tensor_scalar(t, t, -3.1415925, None, ALU.max).then_inc(*up("normed", "angles"))
                elif kind == "stats" and i == 1:
                    split_low(0)
                elif kind == "apply":
                    T = p["T"]
                    src = h if p["src"] == "h" else y
                    s0 = p.get("s0", 0)
                    def low(k):
                        c = p.get("dst") == "c"
                        k_ = s0 + k if c else k
                        dve.wait_ge(*at("operand_high", (i, k)))
                        dve.wait_ge(*own())
                        nc.vector.tensor_tensor((cl if c else ul)[:, k_, 0:T], y[:, s0 + k, 0:T], (ch if c else uh)[:, k_, 0:T].bitcast(F32), ALU.subtract).then_inc(
                            *up("operand_low", (i, k)))

                    for k in range(p["n"]):
                        d = y[:, s0 + k, 0:T]
                        if "gain" in p:
                            dve.wait_ge(*own())
                            nc.vector.scalar_tensor_tensor(d, src[:, s0 + k, 0:T], gain(p, k), rstd[:, 0:T], ALU.mult, ALU.mult).then_inc(
                                *up("normed", (i, k)))
                        else:
                            dve.wait_ge(*own())
                            nc.vector.tensor_tensor(d, src[:, k, 0:T], rstd[:, 0:T], ALU.mult).then_inc(*up("normed", (i, k)))
                        if k >= 2:
                            low(k - 2)
                    low(p["n"] - 2)
                    low(p["n"] - 1)
                    if i == 2:
                        for s in range(1, SPLIT):
                            split_low(s)
                elif kind == "join":
                    for g in range(4):
                        for k in (2 * g, 2 * g + 1):
                            dve.wait_ge(*own())
                            nc.vector.scalar_tensor_tensor(y[:, k, 0:S], y[:, k, 0:S], gain(p, k), rstd[:, 0:S], ALU.mult, ALU.mult).then_inc(
                                *up("vector_step"))
                        hh_ = h[:, 2 * g:2 * g + 2, 0:S]
                        dve.wait_ge(*own())
                        nc.vector.tensor_tensor(hh_, hh_, y[:, 2 * g:2 * g + 2, 0:S], ALU.add).then_inc(
                            *up("tiles_ready", (i, g)))
                elif kind == "linear":
                    for grp in p["groups"]:
                        if p["mode"] == "V":
                            rotate_pending()
                        for c in grp[:-1]:
                            split_low(c["s"] + SPLIT)
                        evac(p, grp)
                        g = grp[0]["g"]
                        if p.get("stat") and g >= 1:
                            fold_squares(p, g - 1)
                        if g - 1 in p["mods"]:
                            mod_keep(p["mods"][g - 1][0])
                        if grp[-1]["s"] + SPLIT not in early + late:
                            split_low(grp[-1]["s"] + SPLIT)
                        if p["evac"] == "mixc" and g == 0:
                            pool_windows(p)
                        if p["name"] == "stick_qk" and g == 0:
                            conditioning()
                        if p["name"].startswith("gate") and g == 2:
                            dve.wait_ge(*at("operand_high", (i, "p")))
                            dve.wait_ge(*own())
                            nc.vector.tensor_tensor(pl_[:, :, :], ps[:, 5, :].rearrange("p (k c) -> p k c", k=2), ph_[:, :, :].bitcast(F32), ALU.subtract).then_inc(
                                *up("operand_low", (i, "p")))
                        if p["evac"] == "uq":
                            part = kr[64:96, :].rearrange("p (o c) -> p o c", o=1).to_broadcast([32, 2, T2])
                            dve.wait_ge(*own())
                            nc.vector.tensor_copy(km[64:96, 2 * g:2 * g + 2, :], part).then_inc(*up("vector_step"))
                        rotate_pending()
                        if rotation(p, g):
                            pending.append((p, g))
                    if p.get("stat"):
                        fold_squares(p, 3)
                        for s in early:
                            split_low(s)
                elif kind == "stick":
                    def fail(hd):
                        b = hd % 2
                        dve.wait_ge(*at("weights_exp", (i, hd)))
                        if hd >= 2:
                            dve.wait_ge(*at("fail_summed", (i, hd - 2)))
                        dve.wait_ge(*own())
                        nc.vector.scalar_tensor_tensor(sbf[:, b, :], ps[:, hd % 4, 0:384], 0.0, sbl[:, b, :], ALU.max, ALU.add).then_inc(
                            *up("vector_step"))
                        dve.wait_ge(*own())
                        f = sbf[:, b, :].rearrange("p (t c) -> p t c", t=3)[:, 0:3:2, :]
                        nc.vector.tensor_tensor(f, f, past2, ALU.mult).then_inc(*up("fail_ready", (i, hd)))

                    def mask(hd):
                        b = hd % 2
                        dve.wait_ge(*at("stick_weights", (i, hd)))
                        dve.wait_ge(*own())
                        a = sba[:, b, :].rearrange("p (t c) -> p t c", t=3)[:, 0:3:2, :]
                        nc.vector.scalar_tensor_tensor(a, a, 1.0, past2, ALU.min, ALU.mult).then_inc(*up("masked", (i, hd)))

                    def low(pair):
                        dve.wait_ge(*at("operand_high", (i, pair)))
                        dve.wait_ge(*own())
                        nc.vector.tensor_tensor(ul[:, pair, 0:S], ps[:, 4 + pair % 2, 0:S], uh[:, pair, 0:S].bitcast(F32), ALU.subtract).then_inc(
                            *up("operand_low", (i, pair)))

                    past2 = squares[:, 7:8, :].to_broadcast([P, 2, P])
                    fail(0)
                    for hd in range(HEADS):
                        if hd + 1 < HEADS:
                            fail(hd + 1)
                        mask(hd)
                        if hd % 2 == 0 and hd // 2 - 2 in p["mods"]:
                            mod_keep(p["mods"][hd // 2 - 2][0])
                        if hd % 2 == 0 and hd >= 4:
                            low(hd // 2 - 2)
                    if HEADS // 2 - 2 in p["mods"]:
                        mod_keep(p["mods"][HEADS // 2 - 2][0])
                    low(HEADS // 2 - 2)
                    low(HEADS // 2 - 1)
                elif kind == "softmax":
                    units = softmax_units(p["what"])
                    N = len(units)

                    def max_(u):
                        n, W, b = u["n"], u["W"], u["n"] % 2
                        dve.wait_ge(*at("scores", (i, n)))
                        if n >= 2:
                            dve.wait_ge(*at("weights_exp", (i, n - 2)))
                        if u["mask"] is not None:
                            for c0 in range(0, W, 512):
                                w = min(512, W - c0)
                                dve.wait_ge(*own())
                                nc.vector.tensor_tensor(sm[:, b, c0:c0 + w], ps[:, b * 2 + c0 // 512, 0:w], masks[:, u["mask"] + c0:u["mask"] + c0 + w], ALU.add).then_inc(
                                    *up("vector_step"))
                            src = sm[:, b, 0:W]
                        else:
                            src = ps[:, n % 4, 0:W]
                        dve.wait_ge(*own())
                        nc.vector.tensor_reduce(small[:, 4 + b:5 + b], src, AX.X, ALU.max).then_inc(*up("vector_step"))
                        dve.wait_ge(*own())
                        nc.vector.tensor_scalar(small[:, b:b + 1], small[:, 4 + b:5 + b], -u["scale"], None, ALU.mult).then_inc(
                            *up("max_ready", (i, n)))

                    def norm_(u):
                        n, W, b = u["n"], u["W"], u["n"] % 2
                        dve.wait_ge(*at("weights_exp", (i, n)))
                        dve.wait_ge(*own())
                        nc.vector.reciprocal(small[:, 6 + b:7 + b], small[:, 2 + b:3 + b]).then_inc(*up("vector_step"))
                        dve.wait_ge(*own())
                        nc.vector.tensor_scalar(pr[:, b, 0:W], pr[:, b, 0:W], small[:, 6 + b:7 + b], None, ALU.mult).then_inc(
                            *up("weights_normed", (i, n)))

                    def low_(u):
                        t0 = u["col"] - u["q"] * P
                        dve.wait_ge(*at("operand_high", (i, u["pair"])))
                        dve.wait_ge(*own())
                        nc.vector.tensor_tensor(ul[:, u["opair"], t0:t0 + S], ps[:, 6 + u["pair"] % 2, 0:S], uh[:, u["opair"], t0:t0 + S].bitcast(F32), ALU.subtract).then_inc(
                            *up("operand_low", (i, u["pair"])))

                    if units[0]["mask"] is not None:
                        dve.wait_ge(loaded["arena"], p["arena_value"])
                    max_(units[0])
                    for n in range(N):
                        if n + 1 < N:
                            max_(units[n + 1])
                        norm_(units[n])
                        if n >= 3 and units[n - 3]["ends"]:
                            low_(units[n - 3])
                    for n in (N - 3, N - 2, N - 1):
                        if units[n]["ends"]:
                            low_(units[n])
                elif kind == "cnorm":

                    def latent_low(k):
                        dve.wait_ge(*at("operand_high", (i, k)))
                        dve.wait_ge(*own())
                        nc.vector.tensor_tensor(cl[:, k, :], y[:, k, :], ch[:, k, :].bitcast(F32), ALU.subtract).then_inc(
                            *up("operand_low", (i, k)))

                    for k in range(5):
                        name, r, row = ("q", rstd, ROW["mla_g_q"] + k) if k < 3 else ("kv", sq[:, 0, :], ROW["mla_g_kv"] + k - 3)
                        dve.wait_ge(*at("rstd_ready", (i, name)))
                        dve.wait_ge(*own())
                        nc.vector.scalar_tensor_tensor(y[:, k, :], y[:, k, :], vec[:, row:row + 1], r[:, :], ALU.mult, ALU.mult).then_inc(
                            *up("normed", (i, k)))
                        if k >= 2:
                            latent_low(k - 2)
                    latent_low(3)
                    latent_low(4)
                    dve.wait_ge(*at("operand_high", (i, "pool")))
                    dve.wait_ge(*own())
                    nc.vector.tensor_tensor(ul[:, 0:4, :], pdif[:, :, :], uh[:, 0:4, :].bitcast(F32), ALU.subtract).then_inc(
                        *up("operand_low", (i, "pool")))
                elif kind == "final":
                    for k in range(8):
                        c = ROW["g_final_2"] + k
                        dve.wait_ge(*own())
                        nc.vector.scalar_tensor_tensor(y[:, k, 0:S], h[:, k, 0:S], vec[:, c:c + 1], rstd[:, 0:S], ALU.mult, ALU.mult).then_inc(
                            *up("normed", (i, k)))
                C.end("vector", i)
                for s in waiting_splits(i):
                    split_low(s)
    return C


def kernel(**inputs):
    import concourse.bacc as bacc
    from concourse.bass_utils import run_bass_kernel_spmd as run

    skip = {"w_in_dsa", "w_out_dsa", "w_in_moba", "w_out_moba"}
    arrays = {n: np.ascontiguousarray(a) for n, a in inputs.items() if n not in skip}
    arrays.update(constants())

    def program(noted):
        nc = bacc.Bacc("TRN2", target_bir_lowering=False, num_devices=1, dynamic_dma_scratch_size=1024)
        A = {n: nc.dram_tensor("in_" + n, a.shape, mybir.dt.from_np(a.dtype), kind="ExternalInput").ap()
             for n, a in arrays.items()}
        out = nc.dram_tensor("out", (1, S, D), F32, kind="ExternalOutput").ap()
        return nc, build(nc, A, out, noted, STOP)

    noted = program(None)[1].seen
    nc, _ = program(noted)
    r = run(nc, [{"in_" + n: a for n, a in arrays.items()}], core_ids=[0])
    return r.results[0]["out"]
```
